# Optimizing a Trainium2 kernel written in Bass

```python
import math
import jax, jax.numpy as jnp
from jax import lax
import numpy as np

D_MODEL = 1024
BATCH = 1
SEQ = 512
DEPTH = 1

A_HEADS = 8
A_HEAD_DIM = 64
A_WIDTH = A_HEADS * A_HEAD_DIM
IDX_HEADS = 8
IDX_DIM = 32
INDEX_TOPK = 256
SPARSE_Q_BLOCK = 64
N_BUCKETS = 32
MAX_DISTANCE = 128

B_HEADS = 4
B_KEY_DIM = 64
B_VAL_DIM = 128
B_KEY_WIDTH = B_HEADS * B_KEY_DIM
B_WIDTH = B_HEADS * B_VAL_DIM
GATE_RANK = 16
GATE_TEMP = 16.0
GLA_CHUNK = 64

MIX_WIDTH = A_WIDTH + B_WIDTH

PROJ_SPLITS = (A_WIDTH, A_WIDTH, A_WIDTH,
               IDX_HEADS * IDX_DIM, IDX_DIM, IDX_HEADS,
               B_KEY_WIDTH, B_KEY_WIDTH, B_WIDTH,
               GATE_RANK, B_WIDTH)
PROJ_WIDTH = 3 * A_WIDTH + IDX_HEADS * IDX_DIM + IDX_DIM + IDX_HEADS + 2 * B_KEY_WIDTH + B_WIDTH + GATE_RANK + B_WIDTH

N_GROUPS = 4
EXPERTS_PER_GROUP = 8
N_EXPERTS = N_GROUPS * EXPERTS_PER_GROUP
EXPERT_TOPK = 2
D_EXPERT = 256

EPS = 1e-6


def rmsnorm(x, g):
    xf = x.astype(jnp.float32)
    y = xf * lax.rsqrt(jnp.mean(xf * xf, axis=-1, keepdims=True) + EPS)
    return (y * g.astype(jnp.float32)).astype(x.dtype)

def t5_bucket(dist):
    max_exact = N_BUCKETS // 2
    d_f = jnp.maximum(dist, 1).astype(jnp.float32)
    large = max_exact + (jnp.log(d_f / max_exact) / math.log(MAX_DISTANCE / max_exact)
                         * (N_BUCKETS - max_exact)).astype(jnp.int32)
    large = jnp.minimum(large, N_BUCKETS - 1)
    return jnp.where(dist < max_exact, dist, large)

def dsa_attention(q, k, v, iq, ik, iw, rel_bias):
    bsz, s_len = q.shape[0], q.shape[1]
    topk = min(INDEX_TOPK, s_len // 4)
    nb = s_len // SPARSE_Q_BLOCK

    def blocks(a):
        return a.reshape(bsz, nb, SPARSE_Q_BLOCK, *a.shape[2:]).swapaxes(0, 1)

    q_pos = jnp.arange(s_len, dtype=jnp.int32).reshape(nb, SPARSE_Q_BLOCK)
    key_pos = jnp.arange(s_len, dtype=jnp.int32)
    ik_f = ik.astype(jnp.float32)
    gather = jax.vmap(lambda a, i: a[i])

    def one_block(args):
        qb, iqb, iwb, tb = args
        idx_logits = jnp.einsum('bqhd,bsd->bqhs', iqb.astype(jnp.float32), ik_f) * IDX_DIM ** -0.5
        score = jnp.einsum('bqhs,bqh->bqs', jax.nn.relu(idx_logits),
                           iwb.astype(jnp.float32) * IDX_HEADS ** -0.5)
        causal = key_pos[None, :] <= tb[:, None]
        score = jnp.where(causal[None], score, -jnp.inf)
        _, idx = lax.top_k(score, topk)
        valid = idx <= tb[None, :, None]
        k_sel = gather(k, idx)
        v_sel = gather(v, idx)
        logits = jnp.einsum('bqhd,bqkhd->bhqk', qb, k_sel).astype(jnp.float32) * A_HEAD_DIM ** -0.5
        dist = jnp.maximum(tb[None, :, None] - idx, 0)
        bias = rel_bias[t5_bucket(dist)]
        logits = logits + jnp.transpose(bias, (0, 3, 1, 2)).astype(jnp.float32)
        logits = jnp.where(valid[:, None], logits, -jnp.inf)
        p = jax.nn.softmax(logits, axis=-1).astype(v.dtype)
        return jnp.einsum('bhqk,bqkhd->bqhd', p, v_sel)

    out = lax.map(one_block, (blocks(q), blocks(iq), blocks(iw), q_pos))
    return out.swapaxes(0, 1).reshape(bsz, s_len, A_HEADS * A_HEAD_DIM)

def gla_chunked(q, k, v, log_a):
    bsz, s_len, h, dk = q.shape
    dv = v.shape[-1]
    nc = s_len // GLA_CHUNK

    def chunks(a):
        return a.reshape(bsz, nc, GLA_CHUNK, h, a.shape[-1]).transpose(1, 0, 3, 2, 4)

    tri = jnp.tril(jnp.ones((GLA_CHUNK, GLA_CHUNK), dtype=bool))

    def step(state, inp):
        qc, kc, vc, gc = inp
        b = jnp.cumsum(gc, axis=2)
        o_inter = jnp.einsum('bhcd,bhdv->bhcv', qc * jnp.exp(b), state)
        diff = b[:, :, :, None, :] - b[:, :, None, :, :]
        decay = jnp.exp(jnp.where(tri[None, None, :, :, None], diff, -jnp.inf))
        attn = jnp.einsum('bhtd,bhsd,bhtsd->bhts', qc, kc, decay)
        o_intra = jnp.einsum('bhts,bhsv->bhtv', attn, vc)
        b_last = b[:, :, -1:, :]
        state = (jnp.exp(b_last[:, :, 0, :])[..., None] * state
                 + jnp.einsum('bhsd,bhsv->bhdv', kc * jnp.exp(b_last - b), vc))
        return state, o_inter + o_intra

    init = jnp.zeros((bsz, h, dk, dv), jnp.float32)
    _, o = lax.scan(step, init, (chunks(q * dk ** -0.5), chunks(k), chunks(v), chunks(log_a)))
    return o.transpose(1, 0, 3, 2, 4).reshape(bsz, s_len, h, dv)

def hier_moe(h, w_rg, b_rg, w_re, b_re, w_g, w_u, w_d):
    bsz, s_len, d = h.shape
    hf = h.reshape(-1, d)
    g_logits = (hf @ w_rg).astype(jnp.float32) + b_rg.astype(jnp.float32)
    g_prob = jax.nn.softmax(g_logits, axis=-1)
    _, g_sel = lax.top_k(g_logits, 1)
    g_onehot = jax.nn.one_hot(g_sel[:, 0], N_GROUPS, dtype=jnp.float32)
    g_weight = jnp.sum(g_prob * g_onehot, axis=-1, keepdims=True)
    e_logits = ((hf @ w_re).astype(jnp.float32) + b_re.astype(jnp.float32)).reshape(-1, N_GROUPS, EXPERTS_PER_GROUP)
    e_logits_sel = jnp.einsum('nge,ng->ne', e_logits, g_onehot)
    top_val, top_idx = lax.top_k(e_logits_sel, EXPERT_TOPK)
    e_weight = jax.nn.softmax(top_val, axis=-1) * g_weight
    e_idx = g_sel * EXPERTS_PER_GROUP + top_idx
    gates = jnp.sum(jax.nn.one_hot(e_idx, N_EXPERTS, dtype=jnp.float32) * e_weight[..., None], axis=1)
    out = jnp.zeros(hf.shape, jnp.float32)
    for g in range(N_GROUPS):
        sl = slice(g * EXPERTS_PER_GROUP, (g + 1) * EXPERTS_PER_GROUP)
        a = jnp.einsum('nd,edf->nef', hf, w_g[sl])
        u = jnp.einsum('nd,edf->nef', hf, w_u[sl])
        hid = jax.nn.silu(a) * u * gates[:, sl, None].astype(hf.dtype)
        out = out + jnp.einsum('nef,efd->nd', hid, w_d[sl]).astype(jnp.float32)
    return out.astype(h.dtype).reshape(bsz, s_len, d)

def first_inputs(seed: int = 0) -> dict:
    key = jax.random.key(seed)
    ks = jax.random.split(key, 20)
    f32 = jnp.float32
    nrm = lambda k, shape, scale: jax.random.normal(k, shape, f32) * scale
    return {
        "x": nrm(ks[0], (BATCH, SEQ, D_MODEL), 1.0),
        "norm1_g": 1.0 + nrm(ks[1], (DEPTH, D_MODEL), 0.01),
        "w_in": nrm(ks[2], (DEPTH, D_MODEL, PROJ_WIDTH), D_MODEL ** -0.5),
        "q_norm_g": 1.0 + nrm(ks[3], (DEPTH, A_HEAD_DIM), 0.01),
        "k_norm_g": 1.0 + nrm(ks[4], (DEPTH, A_HEAD_DIM), 0.01),
        "rel_bias": nrm(ks[5], (N_BUCKETS, A_HEADS), 0.5),
        "gla_gate_w2": nrm(ks[6], (DEPTH, GATE_RANK, B_KEY_WIDTH), GATE_RANK ** -0.5),
        "gla_gate_b": nrm(ks[7], (DEPTH, B_KEY_WIDTH), 0.1),
        "gla_out_norm_g": 1.0 + nrm(ks[8], (DEPTH, B_VAL_DIM), 0.01),
        "w_out": nrm(ks[9], (DEPTH, MIX_WIDTH, D_MODEL), MIX_WIDTH ** -0.5),
        "norm2_g": 1.0 + nrm(ks[10], (DEPTH, D_MODEL), 0.01),
        "w_router_group": nrm(ks[11], (DEPTH, D_MODEL, N_GROUPS), D_MODEL ** -0.5),
        "b_router_group": nrm(ks[12], (DEPTH, N_GROUPS), 0.01),
        "w_router_expert": nrm(ks[13], (DEPTH, D_MODEL, N_EXPERTS), D_MODEL ** -0.5),
        "b_router_expert": nrm(ks[14], (DEPTH, N_EXPERTS), 0.01),
        "w_exp_gate": nrm(ks[15], (DEPTH, N_EXPERTS, D_MODEL, D_EXPERT), D_MODEL ** -0.5),
        "w_exp_up": nrm(ks[16], (DEPTH, N_EXPERTS, D_MODEL, D_EXPERT), D_MODEL ** -0.5),
        "w_exp_down": nrm(ks[17], (DEPTH, N_EXPERTS, D_EXPERT, D_MODEL), D_EXPERT ** -0.5),
    }

def first_block(x, norm1_g, w_in, q_norm_g, k_norm_g, rel_bias, gla_gate_w2, gla_gate_b,
              gla_out_norm_g, w_out, norm2_g, w_router_group, b_router_group,
              w_router_expert, b_router_expert, w_exp_gate, w_exp_up, w_exp_down):
    bsz, s_len, _ = x.shape
    split_points = np.cumsum(PROJ_SPLITS)[:-1].tolist()
    for l in range(DEPTH):
        h = rmsnorm(x, norm1_g[l])
        proj = h @ w_in[l]
        qa, ka, va, iq, ik, iw, qb, kb, vb, g_lr, r_gate = jnp.split(proj, split_points, axis=-1)

        qa = rmsnorm(qa.reshape(bsz, s_len, A_HEADS, A_HEAD_DIM), q_norm_g[l])
        ka = rmsnorm(ka.reshape(bsz, s_len, A_HEADS, A_HEAD_DIM), k_norm_g[l])
        va = va.reshape(bsz, s_len, A_HEADS, A_HEAD_DIM)
        o_a = dsa_attention(qa, ka, va, iq.reshape(bsz, s_len, IDX_HEADS, IDX_DIM), ik, iw, rel_bias)

        log_a = jax.nn.log_sigmoid((g_lr @ gla_gate_w2[l]).astype(jnp.float32)
                                   + gla_gate_b[l].astype(jnp.float32)) / GATE_TEMP
        o_b = gla_chunked(qb.reshape(bsz, s_len, B_HEADS, B_KEY_DIM).astype(jnp.float32),
                          kb.reshape(bsz, s_len, B_HEADS, B_KEY_DIM).astype(jnp.float32),
                          vb.reshape(bsz, s_len, B_HEADS, B_VAL_DIM).astype(jnp.float32),
                          log_a.reshape(bsz, s_len, B_HEADS, B_KEY_DIM))
        o_b = rmsnorm(o_b, gla_out_norm_g[l]).reshape(bsz, s_len, B_WIDTH).astype(x.dtype) * jax.nn.silu(r_gate)

        x = x + jnp.concatenate([o_a, o_b], axis=-1) @ w_out[l]

        x = x + hier_moe(rmsnorm(x, norm2_g[l]), w_router_group[l], b_router_group[l],
                         w_router_expert[l], b_router_expert[l],
                         w_exp_gate[l], w_exp_up[l], w_exp_down[l])
    return x


MLA_HEADS = 8
MLA_Q_LORA = 256
MLA_KV_LORA = 128
MLA_NOPE = 64
MLA_ROPE = 32
MLA_V = 64
MLA_QK = MLA_NOPE + MLA_ROPE
MLA_WIDTH = MLA_HEADS * MLA_V
ROPE_THETA = 10000.0
FOX_HEADS = 8
FOX_HEAD_DIM = 64
FOX_WIDTH = FOX_HEADS * FOX_HEAD_DIM
Q_BLOCK = 128
IN_SPLIT_SIZES = (MLA_Q_LORA, MLA_KV_LORA, MLA_ROPE, FOX_WIDTH, FOX_WIDTH, FOX_WIDTH, FOX_HEADS, D_MODEL, D_MODEL)
IN_COLS = MLA_Q_LORA + MLA_KV_LORA + MLA_ROPE + 3 * FOX_WIDTH + FOX_HEADS + 2 * D_MODEL
N_EXPERTS_2 = 64
N_GROUPS_2 = 8
TOPK_GROUPS = 4
TOP_K = 6
D_SHARED = 256
ROUTED_SCALE = 2.5
EXPERT_BLOCK = 128
N_MOD = 6
NORM_EPS = 1e-6
NEG_INF = -1e30


def rms_norm(x, gain):
    xf = x.astype(jnp.float32)
    y = xf * lax.rsqrt(jnp.mean(xf * xf, axis=-1, keepdims=True) + NORM_EPS)
    return (y * gain.astype(jnp.float32)).astype(x.dtype)

def split_cols(t, sizes):
    out, start = [], 0
    for n in sizes:
        out.append(t[..., start:start + n])
        start += n
    return out

def apply_rope(x, positions):
    half = x.shape[-1] // 2
    inv_freq = jnp.power(ROPE_THETA, -jnp.arange(half, dtype=jnp.float32) / half)
    ang = positions.astype(jnp.float32)[:, None, :, None] * inv_freq
    cos = jnp.cos(ang).astype(x.dtype)
    sin = jnp.sin(ang).astype(x.dtype)
    x1, x2 = x[..., :half], x[..., half:]
    return jnp.concatenate([x1 * cos - x2 * sin, x2 * cos + x1 * sin], axis=-1)

def causal_block_attention(q, k, v, scale, decay=None):
    B, H, S, _ = q.shape
    dv = v.shape[-1]
    nblk = S // Q_BLOCK

    def to_blocks(t):
        return jnp.moveaxis(t.reshape((B, H, nblk, Q_BLOCK) + t.shape[3:]), 2, 0)

    key_pos = jnp.arange(S)

    def one_block(xs):
        i, qb = xs[0], xs[1]
        logits = jnp.einsum('bhqd,bhkd->bhqk', qb, k).astype(jnp.float32) * scale
        if decay is not None:
            logits = logits + xs[2][..., :, None] - decay[:, :, None, :]
        q_pos = i * Q_BLOCK + jnp.arange(Q_BLOCK)
        logits = jnp.where(key_pos[None, :] <= q_pos[:, None], logits, NEG_INF)
        p = jax.nn.softmax(logits, axis=-1).astype(v.dtype)
        return jnp.einsum('bhqk,bhkd->bhqd', p, v)

    xs = (jnp.arange(nblk), to_blocks(q))
    if decay is not None:
        xs = xs + (to_blocks(decay),)
    out = lax.map(one_block, xs)
    return jnp.moveaxis(out, 0, 2).reshape(B, H, S, dv)

def hybrid_mixer(h, positions, w_in, b_forget, g_q_lat, w_q_up, g_kv_lat, w_kv_up, w_o_mla, w_o_fox, w_out):
    B, S, _ = h.shape
    proj = h @ w_in
    q_lat, kv_lat, k_rope, fq, fk, fv, f_logit, gate_a, gate_b = split_cols(proj, IN_SPLIT_SIZES)

    q = (rms_norm(q_lat, g_q_lat) @ w_q_up).reshape(B, S, MLA_HEADS, MLA_QK).transpose(0, 2, 1, 3)
    q_nope, q_pe = q[..., :MLA_NOPE], apply_rope(q[..., MLA_NOPE:], positions)
    kv = (rms_norm(kv_lat, g_kv_lat) @ w_kv_up).reshape(B, S, MLA_HEADS, MLA_NOPE + MLA_V).transpose(0, 2, 1, 3)
    k_nope, v_mla = kv[..., :MLA_NOPE], kv[..., MLA_NOPE:]
    k_pe = apply_rope(k_rope[:, None, :, :], positions)
    q_mla = jnp.concatenate([q_nope, q_pe], axis=-1)
    k_mla = jnp.concatenate([k_nope, jnp.broadcast_to(k_pe, (B, MLA_HEADS, S, MLA_ROPE))], axis=-1)
    o_mla = causal_block_attention(q_mla, k_mla, v_mla, 1.0 / math.sqrt(MLA_QK))
    o_mla = o_mla.transpose(0, 2, 1, 3).reshape(B, S, MLA_WIDTH)

    def heads(t):
        return t.reshape(B, S, FOX_HEADS, FOX_HEAD_DIM).transpose(0, 2, 1, 3)

    log_f = jax.nn.log_sigmoid((f_logit + b_forget).astype(jnp.float32))
    cum_log_f = jnp.cumsum(log_f, axis=1).transpose(0, 2, 1)
    o_fox = causal_block_attention(heads(fq), heads(fk), heads(fv), 1.0 / math.sqrt(FOX_HEAD_DIM), cum_log_f)
    o_fox = o_fox.transpose(0, 2, 1, 3).reshape(B, S, FOX_WIDTH)

    merged = jax.nn.sigmoid(gate_a) * (o_mla @ w_o_mla) + jax.nn.sigmoid(gate_b) * (o_fox @ w_o_fox)
    return merged @ w_out

def moe_ffn(h, w_router, b_router, w_exp_gate, w_exp_up, w_exp_down, w_sh_gate, w_sh_up, w_sh_down):
    B, S, D = h.shape
    T = B * S
    xf = h.reshape(T, D)

    scores = jax.nn.sigmoid((xf @ w_router).astype(jnp.float32))
    choice = scores + b_router.astype(jnp.float32)
    group_score = lax.top_k(choice.reshape(T, N_GROUPS_2, N_EXPERTS_2 // N_GROUPS_2), 2)[0].sum(-1)
    _, group_idx = lax.top_k(group_score, TOPK_GROUPS)
    group_keep = (group_idx[..., None] == jnp.arange(N_GROUPS_2)).any(axis=-2)
    expert_keep = jnp.repeat(group_keep, N_EXPERTS_2 // N_GROUPS_2, axis=-1)
    _, expert_idx = lax.top_k(jnp.where(expert_keep, choice, NEG_INF), TOP_K)
    gate = jnp.take_along_axis(scores, expert_idx, axis=-1)
    gate = (gate / gate.sum(-1, keepdims=True) * ROUTED_SCALE).astype(h.dtype)

    n_assign = T * TOP_K
    flat_e = expert_idx.reshape(-1).astype(jnp.int32)
    flat_tok = jnp.arange(n_assign, dtype=jnp.int32) // TOP_K
    order = jnp.argsort(flat_e)
    se, stok, sgate = flat_e[order], flat_tok[order], gate.reshape(-1)[order]
    counts = jnp.zeros((N_EXPERTS_2,), jnp.int32).at[flat_e].add(1)
    padded = (counts + EXPERT_BLOCK - 1) // EXPERT_BLOCK * EXPERT_BLOCK
    start = jnp.cumsum(counts) - counts
    pend = jnp.cumsum(padded)
    pstart = pend - padded
    dest = pstart[se] + jnp.arange(n_assign, dtype=jnp.int32) - start[se]
    n_blocks = (n_assign + EXPERT_BLOCK - 1) // EXPERT_BLOCK + N_EXPERTS_2
    n_rows = n_blocks * EXPERT_BLOCK
    row_tok = jnp.full((n_rows,), T, jnp.int32).at[dest].set(stok)
    row_gate = jnp.zeros((n_rows,), h.dtype).at[dest].set(sgate)
    block_e = jnp.minimum(
        jnp.searchsorted(pend, jnp.arange(n_blocks, dtype=jnp.int32) * EXPERT_BLOCK, side='right'),
        N_EXPERTS_2 - 1)
    x_pad = jnp.concatenate([xf, jnp.zeros((1, D), xf.dtype)], axis=0)

    def expert_block(xs):
        tok, g, e = xs
        xb = x_pad[tok]
        hb = jax.nn.silu(xb @ w_exp_gate[e]) * (xb @ w_exp_up[e])
        return (hb @ w_exp_down[e]) * g[:, None]

    yb = lax.map(expert_block, (row_tok.reshape(n_blocks, EXPERT_BLOCK),
                                row_gate.reshape(n_blocks, EXPERT_BLOCK), block_e))
    routed = jax.ops.segment_sum(yb.reshape(n_rows, D), row_tok, num_segments=T + 1)[:T]
    shared = (jax.nn.silu(xf @ w_sh_gate) * (xf @ w_sh_up)) @ w_sh_down
    return (shared + routed).reshape(B, S, D)

def dense_init(k, shape, fan_in, scale=1.0):
    return scale * fan_in ** -0.5 * jax.random.normal(k, shape, jnp.float32)

def second_inputs(seed: int = 0) -> dict:
    key = jax.random.key(seed)
    ks = jax.random.split(key, 25)
    L, D, E = DEPTH, D_MODEL, N_EXPERTS_2

    def gain(k, shape):
        return 1.0 + 0.02 * jax.random.normal(k, shape, jnp.float32)

    offset = jax.random.randint(ks[2], (BATCH, 1), 0, 1024, dtype=jnp.int32)
    return {
        'x': jax.random.normal(ks[0], (BATCH, SEQ, D), jnp.float32),
        'c': jax.random.normal(ks[1], (BATCH, D), jnp.float32),
        'positions': jnp.arange(SEQ, dtype=jnp.int32)[None, :] + offset,
        'w_mod': dense_init(ks[3], (L, D, N_MOD * D), D, 0.5),
        'b_mod': 0.02 * jax.random.normal(ks[4], (L, N_MOD * D), jnp.float32),
        'g_mix_norm': gain(ks[5], (L, D)),
        'w_in': dense_init(ks[6], (L, D, IN_COLS), D),
        'b_forget': 1.0 + 3.0 * jax.random.uniform(ks[7], (L, FOX_HEADS), jnp.float32),
        'g_q_lat': gain(ks[8], (L, MLA_Q_LORA)),
        'w_q_up': dense_init(ks[9], (L, MLA_Q_LORA, MLA_HEADS * MLA_QK), MLA_Q_LORA),
        'g_kv_lat': gain(ks[10], (L, MLA_KV_LORA)),
        'w_kv_up': dense_init(ks[11], (L, MLA_KV_LORA, MLA_HEADS * (MLA_NOPE + MLA_V)), MLA_KV_LORA),
        'w_o_mla': dense_init(ks[12], (L, MLA_WIDTH, D), MLA_WIDTH),
        'w_o_fox': dense_init(ks[13], (L, FOX_WIDTH, D), FOX_WIDTH),
        'w_out': dense_init(ks[14], (L, D, D), D),
        'g_ffn_norm': gain(ks[15], (L, D)),
        'w_router': dense_init(ks[16], (L, D, E), D),
        'b_router': 0.01 * jax.random.normal(ks[17], (L, E), jnp.float32),
        'w_exp_gate': dense_init(ks[18], (L, E, D, D_EXPERT), D),
        'w_exp_up': dense_init(ks[19], (L, E, D, D_EXPERT), D),
        'w_exp_down': dense_init(ks[20], (L, E, D_EXPERT, D), D_EXPERT),
        'w_sh_gate': dense_init(ks[21], (L, D, D_SHARED), D),
        'w_sh_up': dense_init(ks[22], (L, D, D_SHARED), D),
        'w_sh_down': dense_init(ks[23], (L, D_SHARED, D), D_SHARED),
        'g_final': gain(ks[24], (D,)),
    }

def second_block(x, c, positions, w_mod, b_mod, g_mix_norm, w_in, b_forget, g_q_lat, w_q_up, g_kv_lat,
              w_kv_up, w_o_mla, w_o_fox, w_out, g_ffn_norm, w_router, b_router, w_exp_gate, w_exp_up,
              w_exp_down, w_sh_gate, w_sh_up, w_sh_down, g_final):
    cond = jax.nn.silu(c)
    for l in range(DEPTH):
        mod = cond @ w_mod[l] + b_mod[l]
        shift_m, scale_m, gate_m, shift_f, scale_f, gate_f = [m[:, None, :] for m in jnp.split(mod, N_MOD, axis=-1)]
        h = rms_norm(x, g_mix_norm[l]) * (1.0 + scale_m) + shift_m
        x = x + gate_m * hybrid_mixer(h, positions, w_in[l], b_forget[l], g_q_lat[l], w_q_up[l], g_kv_lat[l],
                                      w_kv_up[l], w_o_mla[l], w_o_fox[l], w_out[l])
        h = rms_norm(x, g_ffn_norm[l]) * (1.0 + scale_f) + shift_f
        x = x + gate_f * moe_ffn(h, w_router[l], b_router[l], w_exp_gate[l], w_exp_up[l], w_exp_down[l],
                                 w_sh_gate[l], w_sh_up[l], w_sh_down[l])
    return rms_norm(x, g_final)


def setup_inputs(seed=0):
    out = dict(first_inputs(seed))
    for name, value in second_inputs(seed + 1).items():
        if name != "x":
            out[name + "_2"] = value
    return out


def reference(
    x, norm1_g, w_in, q_norm_g, k_norm_g, rel_bias, gla_gate_w2, gla_gate_b, gla_out_norm_g,
    w_out, norm2_g, w_router_group, b_router_group, w_router_expert, b_router_expert,
    w_exp_gate, w_exp_up, w_exp_down, c_2, positions_2, w_mod_2, b_mod_2, g_mix_norm_2, w_in_2,
    b_forget_2, g_q_lat_2, w_q_up_2, g_kv_lat_2, w_kv_up_2, w_o_mla_2, w_o_fox_2, w_out_2,
    g_ffn_norm_2, w_router_2, b_router_2, w_exp_gate_2, w_exp_up_2, w_exp_down_2, w_sh_gate_2,
    w_sh_up_2, w_sh_down_2, g_final_2,
):
    x = first_block(
        x, norm1_g, w_in, q_norm_g, k_norm_g, rel_bias, gla_gate_w2, gla_gate_b, gla_out_norm_g,
        w_out, norm2_g, w_router_group, b_router_group, w_router_expert, b_router_expert,
        w_exp_gate, w_exp_up, w_exp_down,
    )
    return second_block(
        x, c_2, positions_2, w_mod_2, b_mod_2, g_mix_norm_2, w_in_2, b_forget_2, g_q_lat_2,
        w_q_up_2, g_kv_lat_2, w_kv_up_2, w_o_mla_2, w_o_fox_2, w_out_2, g_ffn_norm_2,
        w_router_2, b_router_2, w_exp_gate_2, w_exp_up_2, w_exp_down_2, w_sh_gate_2, w_sh_up_2,
        w_sh_down_2, g_final_2,
    )


_drawn_inputs = setup_inputs


def setup_inputs(seed=0):
    import zlib

    import numpy as np

    out = dict(_drawn_inputs(seed))
    spreads = {}
    factors = {'q_norm_g': 5.814,
     'k_norm_g': 8.0,
     'gla_out_norm_g': 2.752,
     'b_router_group': 2.872,
     'b_router_expert': 6.195,
     'g_mix_norm_2': 6.075,
     'g_q_lat_2': 8.0,
     'g_kv_lat_2': 7.858,
     'g_final_2': 7.938,
     'g_ffn_norm_2': 4.161}
    for name, (base, spread) in spreads.items():
        noise = np.random.default_rng([zlib.crc32(name.encode()), seed]).standard_normal(out[name].shape)
        drawn = base * np.exp(spread * noise) if base else spread * noise
        out[name] = __import__('jax').numpy.asarray(drawn.astype(out[name].dtype))
    for name, factor in factors.items():
        out[name] = (out[name] * factor).astype(out[name].dtype)
    return out
```

```python
from contextlib import ExitStack

import numpy as np

import concourse.bass as bass
from concourse import mybir

F32 = mybir.dt.float32
I32 = mybir.dt.int32
ALU = mybir.AluOpType
ACT = mybir.ActivationFunctionType
AX = mybir.AxisListType

P = 128
S = 512
T = S // P
D = 1024
KC = D // P
EPS = 1e-6
MASKED = -float(2 ** 100)
TAKEN = -float(2 ** 120)
SENTINEL = float(2 ** 100)
NO_TOKEN = 4096
HEADS = 8
FE = 256
FH = 2
ROUTED_SCALE = 2.5
N_BUCKETS = 32
BIAS_COLS = 640
TWO_PI = 6.283185307179586
ROUNDER = 1.5 * 2.0 ** 23


def shape_constants():
    dist = np.maximum(511 - np.arange(BIAS_COLS), 0)
    big = 16 + (np.log(np.maximum(dist, 1).astype(np.float32) / np.float32(16)) / np.float32(np.log(8.0)) * np.float32(16)).astype(np.int32)
    bucket = np.where(dist < 16, dist, np.minimum(big, N_BUCKETS - 1))
    onehot = (bucket[None, :] == np.arange(N_BUCKETS)[:, None]).astype(np.float32)
    inv_freq = np.power(np.float32(10000.0), -np.arange(16, dtype=np.float32) / np.float32(16)).astype(np.float32)
    return {"bucket_onehot": onehot, "inv_freq": inv_freq}


class Chain:

    def __init__(self, sem):
        self.sem, self.n, self.eng = sem, 0, None

    def on(self, eng):
        self.eng = eng
        return self

    def __call__(self, ins):
        self.n += 1
        ins.then_inc(self.sem, 1)
        self.eng.wait_ge(self.sem, self.n)
        return ins


class State:
    pass


def bcast(ap, n):
    return ap.partition_broadcast(n)


def build_program(nc, *args, stop_after=None):
    names = _INS + list(_CONSTS)
    I = dict(zip(names, args[:len(names)]))
    out = args[len(names)]
    with ExitStack() as ctx:
        K = State()
        K.nc, K.I, K.out = nc, I, out

        def sb(name, cols, dt=F32, parts=P):
            return ctx.enter_context(nc.sbuf_tensor(name, [parts, cols], dt))

        def sem(name):
            return ctx.enter_context(nc.semaphore(name))

        def dram(name, shape):
            return nc.dram_tensor(name, shape, F32, kind="Internal").ap()

        K.sb, K.dram = sb, dram
        K.big = sb("big", 18432)
        K.x = sb("x_res", T * D)[:, :].rearrange("p (t d) -> p t d", t=T)
        K.hr = sb("h_rows", T * D)[:, :].rearrange("p (t d) -> p t d", t=T)
        K.ht = sb("h_cols", T * D)[:, :].rearrange("p (c s) -> p c s", c=KC)
        K.ht2 = K.ht.rearrange("p c s -> p (c s)")
        K.heads = sb("heads", 10240)
        K.qt = K.heads[:, 0:4096].rearrange("p (h s) -> p h s", h=HEADS)
        K.kt = K.heads[:, 4096:8192].rearrange("p (h s) -> p h s", h=HEADS)
        K.v = K.heads[:, 8192:10240].rearrange("p (t d) -> p t d", t=T)
        K.keep = sb("keep_mask", T * S)[:, :].rearrange("p (t s) -> p t s", t=T)
        K.small = sb("small", 2048)
        K.gain = sb("gain", D)
        K.shift = sb("shift", D)
        K.ident = sb("ident", P)
        K.tri = sb("tri_strict", P)
        K.tri_incl = sb("tri_incl", P)
        K.ones = sb("ones", P)
        K.iota = sb("iota", P)
        K.causal = sb("causal", S)
        K.token_id = sb("token_id", T)
        K.desc = sb("desc", 8)
        K.eps = sb("eps", 1)
        K.half_pi = sb("half_pi", 1)
        K.bank = [ctx.enter_context(nc.psum_tensor(f"bank{i}", [P, 512], F32)) for i in range(8)]
        K.dve, K.act, K.pool = (Chain(sem(f"{n}_step")) for n in ("vector", "scalar", "pool"))
        K.slot = [K.big[:, 0:4096], K.big[:, 4096:8192]]
        K.scr = K.big[:, 8192:18432]
        K.w_in_slot = [sem("weights_in_slot0"), sem("weights_in_slot1")]
        K.products = sem("products_ready")
        K.row_sems = {tag: [sem(f"{tag}_{n}") for n in ("gathered_even", "gathered_odd", "scattered")]
                      for tag in ("moe1", "moe2")}
        K.over_sems = {tag: [sem(f"{tag}_over_{n}") for n in ("gathered", "scattered")] for tag in ("moe1", "moe2")}
        K.n_products = 0
        K.job_end = []
        K.jobs = []
        K.next_load = 0
        K.next_job = 0
        K.slot_fill = [0, 0]
        K.h_dram = dram("h_scratch", [S, D])
        K.acc_dram = dram("acc_scratch", [S, D])
        K.mod_dram = dram("mod_scratch", [6 * D])
        K.bias_dram = dram("bias_scratch", [P, HEADS, BIAS_COLS])
        list_jobs(K)

        for stages in (FIRST_BLOCK, SECOND_BLOCK):
            with ExitStack() as stage_ctx:
                used = []

                def stage_sem(name, ctx=stage_ctx, used=used):
                    handle = ctx.enter_context(nc.semaphore(name))
                    used.append(handle.num)
                    return handle

                K.sem = stage_sem
                for name, stage in stages:
                    stage(K)
                    if name == stop_after:
                        return
                if stages is FIRST_BLOCK:
                    assert sorted(used) == list(range(min(used), max(used) + 1)), sorted(used)
                    nc.all_engine_barrier(sems_to_clear=range(min(used), max(used) + 1))



def list_jobs(K):
    I = K.I

    def cols(name, c0, n, at, width):
        src = I[name][0].rearrange("(p c) n -> p c n", p=P)[:, :, c0:c0 + n]
        chunks = src.shape[1]
        return (lambda slot: slot[:, 0:chunks * width].rearrange("p (c n) -> p c n", c=chunks)[:, :, at:at + n], src)

    def job(*parts):
        K.jobs.append(parts)

    for j in range(12):
        job(cols("w_mod_2", 512 * j, 512, 0, 512))
    job(cols("w_in", 1536, 256, 0, 408), *[cols("w_in", 1792, 32, 256 + 32 * r, 408) for r in range(4)],
        cols("w_in", 2856, 16, 384, 408), cols("w_in", 1824, 8, 400, 408))
    for c0 in (0, 512, 1024, 1832, 2344, 2872):
        job(cols("w_in", c0, 512, 0, 512))
    for j in range(2):
        job(cols("w_out", 512 * j, 512, 0, 512))
    job(cols("w_router_group", 0, 4, 0, 36), cols("w_router_expert", 0, 32, 4, 36))
    job(cols("w_in_2", 0, 416, 0, 424), cols("w_in_2", 1952, 8, 416, 424))
    job(cols("w_q_up_2", 0, 768, 0, 768))
    job(cols("w_kv_up_2", 0, 1024, 0, 1024))
    for c0 in (416, 928, 1440):
        job(cols("w_in_2", c0, 512, 0, 512))
    for half in range(2):
        job(cols("w_in_2", 1960 + 512 * half, 512, 0, 512))
        job(cols("w_o_mla_2", 512 * half, 512, 0, 1024), cols("w_o_fox_2", 512 * half, 512, 512, 1024))
        job(cols("w_in_2", 2984 + 512 * half, 512, 0, 512))
    for j in range(2):
        job(cols("w_out_2", 512 * j, 512, 0, 512))
    job(cols("w_router_2", 0, 64, 0, 64))
    job(cols("w_sh_gate_2", 0, 256, 0, 512), cols("w_sh_up_2", 0, 256, 256, 512))
    job(cols("w_sh_down_2", 0, 1024, 0, 1024))


def load_jobs(K, sp, n):
    for _ in range(n):
        g = K.next_load
        if g >= 2:
            sp.wait_ge(K.products, K.job_end[g - 2])
        for place, src in K.jobs[g]:
            sp.dma_start(place(K.slot[g % 2]), src).then_inc(K.w_in_slot[g % 2], 16)
        K.next_load += 1


def take_job(K, pe):
    g = K.next_job
    K.next_job += 1
    K.slot_fill[g % 2] += 16 * len(K.jobs[g])
    pe.wait_ge(K.w_in_slot[g % 2], K.slot_fill[g % 2])
    return K.slot[g % 2]


def product(K, mm):
    mm.then_inc(K.products, 1)
    K.n_products += 1
    return K.n_products


def end_job(K):
    K.job_end.append(K.n_products)


def chunked(slot, chunks, width):
    return slot[:, 0:chunks * width].rearrange("p (c n) -> p c n", c=chunks)



def setup_and_modulation(K):
    nc, I = K.nc, K.I
    s = K.sem
    consts, c_in, x_in = s("consts_ready"), s("c_arrived"), s("x_arrived")
    cond_ready, mod_row, mod_out = s("cond_ready"), s("mod_row_ready"), (s("mod_even_stored"), s("mod_odd_stored"))
    b_in = s("b_mod_arrived")
    cond = K.small[:, 0:KC]
    craw = K.small[:, 8:8 + KC]
    brow = K.scr[0:1, 0:6 * D]
    mrow = K.scr[0:1, 6144:6144 + 1024].rearrange("p (b n) -> p b n", b=2)
    K.rel = K.scr[0:N_BUCKETS, 7168:7168 + HEADS]
    K.hot = K.scr[0:N_BUCKETS, 7200:7200 + BIAS_COLS]
    bias_rows = K.scr[0:HEADS, 7840:7840 + BIAS_COLS]
    bias_in, bias_sb, bias_out = s("bias_arrived"), s("bias_rows_ready"), s("bias_stored")
    K.x_in = x_in
    with nc.Block(no_gpsimd_drain=True) as block:
        @block.tensor
        def _(pe):
            pe.wait_ge(cond_ready, 1)
            for j in range(12):
                w = chunked(take_job(K, pe), KC, 512)
                if j >= 2:
                    pe.wait_ge(mod_row, j - 1)
                for c in range(KC):
                    mm = pe.matmul(K.bank[j % 2][0:1, :], cond[:, c:c + 1], w[:, c, :], start=c == 0, stop=c == KC - 1)
                product(K, mm)
                end_job(K)
            pe.wait_ge(bias_in, 32)
            pe.matmul(K.bank[2][0:HEADS, :], K.rel, K.hot[:, 0:512], start=True, stop=True)
            mm = pe.matmul(K.bank[3][0:HEADS, 0:128], K.rel, K.hot[:, 512:640], start=True, stop=True)
            product(K, mm)

        @block.sync
        def _(sp):
            sp.dma_start(craw, I["c_2"][0].rearrange("(p c) -> p c", p=P)).then_inc(c_in, 16)
            load_jobs(K, sp, 2)
            sp.dma_start(brow, I["b_mod_2"]).then_inc(b_in, 16)
            sp.dma_start(K.rel, I["rel_bias"]).then_inc(bias_in, 16)
            sp.dma_start(K.hot, I["bucket_onehot"]).then_inc(bias_in, 16)
            load_jobs(K, sp, 10)
            sp.dma_start(K.gain[:, :], bcast(I["norm1_g"][0], P)).then_inc(x_in, 16)
            sp.dma_start(K.x, I["x"][0].rearrange("(t p) d -> p t d", p=P)).then_inc(x_in, 16)
            load_jobs(K, sp, 2)

        @block.gpsimd
        def _(pool):
            for buf, value in ((K.ident, 0.0), (K.tri, 1.0), (K.tri_incl, 1.0), (K.ones, 1.0), (K.eps, EPS)):
                pool.memset(buf[:, :], value).then_inc(consts, 1)
            pool.memset(K.causal[:, :], 0.0).then_inc(consts, 1)
            pool.wait_ge(consts, 6)
            for buf, compare, fill, base, pattern, mult in (
                    (K.ident, ALU.not_equal, 1.0, 0, [[-1, P]], 1), (K.tri, ALU.is_gt, 0.0, 0, [[1, P]], -1),
                    (K.tri_incl, ALU.is_ge, 0.0, 0, [[1, P]], -1), (K.causal, ALU.is_ge, MASKED, S - P, [[-1, S]], 1)):
                pool.affine_select(out=buf[:, :], in_=buf[:, :], compare_op=compare, fill=fill, base=base,
                                   pattern=pattern, channel_multiplier=mult).then_inc(consts, 1)
            for buf, pattern, base, mult in ((K.iota, [[1, P]], 0, 0), (K.token_id, [[P, T]], -NO_TOKEN, 1),
                                             (K.desc, [[-1, 8]], 8, 0)):
                pool.iota(buf[:, :], pattern=pattern, base=base, channel_multiplier=mult,
                          allow_small_or_imprecise_dtypes=True).then_inc(consts, 1)
            pool.wait_ge(consts, 13)

        @block.scalar
        def _(act):
            act.wait_ge(c_in, 16)
            act.activation(cond, craw, ACT.Silu).then_inc(cond_ready, 1)
            for j in range(12):
                act.wait_ge(mod_row, j + 1)
                act.dma_start(K.mod_dram[512 * j:512 * j + 512].unsqueeze(0), mrow[:, j % 2, :]).then_inc(mod_out[j % 2], 16)
            act.wait_ge(bias_sb, 2)
            act.dma_start(K.bias_dram.rearrange("p h k -> h p k"),
                          bias_rows.unsqueeze(1).broadcast_to([HEADS, P, BIAS_COLS])).then_inc(bias_out, 16)
            act.wait_ge(mod_out[0], 6 * 16)
            act.wait_ge(mod_out[1], 6 * 16)
            act.wait_ge(bias_out, 16)

        @block.vector
        def _(dve):
            dve.wait_ge(b_in, 16)
            for j in range(12):
                dve.wait_ge(K.products, j + 1)
                if j >= 2:
                    dve.wait_ge(mod_out[j % 2], 16 * (j // 2))
                dve.tensor_tensor(mrow[:, j % 2, :], K.bank[j % 2][0:1, :], brow[:, 512 * j:512 * j + 512],
                                  ALU.add).then_inc(mod_row, 1)
            dve.wait_ge(K.products, 13)
            dve.tensor_copy(bias_rows[:, 0:512], K.bank[2][0:HEADS, :]).then_inc(bias_sb, 1)
            dve.tensor_copy(bias_rows[:, 512:640], K.bank[3][0:HEADS, 0:128]).then_inc(bias_sb, 1)



def norm_columns(K, tag, shift=False, store=False, gain_ready=None):
    nc = K.nc
    squares, std, normed = K.sem(f"{tag}_squares"), K.sem(f"{tag}_std"), K.sem(f"{tag}_rows_ready")
    taken, stored = K.sem(f"{tag}_columns_copied"), K.sem(f"{tag}_stored")
    ss, sd, rs = K.small[:, 0:4], K.small[:, 4:8], K.small[:, 8:12]
    junk = K.scr[:, 0:2048].rearrange("p (b d) -> p b d", b=2)
    base = K.n_products
    with nc.Block(no_gpsimd_drain=True) as block:
        @block.tensor
        def _(pe):
            for t in range(T):
                pe.wait_ge(normed, t + 1)
                for half in range(2):
                    u = 2 * t + half
                    if u >= 4:
                        pe.wait_ge(taken, u - 3)
                    for k in range(4):
                        mm = pe.transpose(K.bank[u % 4][:, P * k:P * k + P], K.hr[:, t, 4 * half + k::KC], K.ident[:, :])
                    product(K, mm)

        @block.scalar
        def _(act):
            if gain_ready:
                act.wait_ge(*gain_ready)
            for t in range(T):
                if t >= 2:
                    act.wait_ge(squares, t - 1)
                act.activation(junk[:, t % 2, :], K.x[:, t, :], ACT.Square, accum_out=ss[:, t:t + 1]).then_inc(squares, 1)
            act.wait_ge(squares, T)
            act.activation(sd, ss, ACT.Sqrt, scale=1.0 / D, bias=K.eps[:, 0:1]).then_inc(std, 1)
            for u in range(2 * T):
                t, half = divmod(u, 2)
                act.wait_ge(K.products, base + u + 1)
                act.activation(K.ht[:, 4 * half:4 * half + 4, P * t:P * t + P],
                               K.bank[u % 4][:, :].rearrange("p (k s) -> p k s", k=4), ACT.Copy).then_inc(taken, 1)

        @block.vector
        def _(dve):
            step = K.dve.on(dve)
            dve.wait_ge(std, 1)
            step(dve.reciprocal(rs, sd))
            for t in range(T):
                ins = dve.scalar_tensor_tensor(out=K.hr[:, t, :], in0=K.x[:, t, :], scalar=rs[:, t:t + 1],
                                               in1=K.gain[:, :], op0=ALU.mult, op1=ALU.mult)
                if shift:
                    step(ins)
                    ins = dve.tensor_tensor(K.hr[:, t, :], K.hr[:, t, :], K.shift[:, :], ALU.add)
                ins.then_inc(normed, 1)

        @block.sync
        def _(sp):
            if store:
                for t in range(T):
                    sp.wait_ge(normed, t + 1)
                    sp.dma_start(K.h_dram[P * t:P * t + P, :], K.hr[:, t, :]).then_inc(stored, 16)
                sp.wait_ge(stored, 16 * T)


def first_norm(K):
    norm_columns(K, "norm1", gain_ready=(K.x_in, 32))



def first_projection(K):
    nc, I = K.nc, K.I
    taken, scored, picked = K.sem("p1_taken"), K.sem("p1_scored"), K.sem("p1_picked")
    iqT = K.heads[:, 0:1024].rearrange("p (j s) -> p j s", j=2)
    ikT = K.heads[:, 1024:1536]
    relu = K.heads[:, 1536:3072].rearrange("p (b s) -> p b s", b=3)
    iw = K.small[:, 32:64].rearrange("p (t h) -> p t h", t=T)
    top8 = K.small[:, 64:72]
    K.glr = K.small[0:16, 1024:1536]
    K.q_rows = K.scr[:, 0:2048].rearrange("p (t d) -> p t d", t=T)
    K.k_rows = K.scr[:, 2048:4096].rearrange("p (t d) -> p t d", t=T)
    K.vb = K.scr[:, 4096:6144].rearrange("p (t d) -> p t d", t=T)
    K.rg = K.scr[:, 6144:8192].rearrange("p (t d) -> p t d", t=T)
    K.qb = K.scr[:, 8192:9216].rearrange("p (j s) -> p j s", j=2)
    K.kb = K.scr[:, 9216:10240].rearrange("p (j s) -> p j s", j=2)
    copies = []
    score_units = [(t, h) for t in range(1, T) for h in range(HEADS)]
    base = K.n_products

    with nc.Block(no_gpsimd_drain=True) as block:
        @block.tensor
        def _(pe):
            def unit(lhs_rhs, out_of, dest, func=ACT.Copy, scale=1.0):
                u = len(copies)
                if u >= 8:
                    pe.wait_ge(taken, u - 7)
                bank = K.bank[u % 8]
                for c, (lhsT, rhs) in enumerate(lhs_rhs):
                    mm = pe.matmul(out_of(bank), lhsT, rhs, start=c == 0, stop=c == len(lhs_rhs) - 1)
                product(K, mm)
                copies.append((dest, out_of(bank), func, scale))

            def columns(w, c0, n, dest, func=ACT.Copy, scale=1.0):
                unit([(w[:, c, c0:c0 + n], K.ht[:, c, :]) for c in range(KC)], lambda b: b[0:n, :], dest, func, scale)

            def rows(w, dest):
                for t in range(T):
                    unit([(K.ht[:, c, P * t:P * t + P], w[:, c, :]) for c in range(KC)], lambda b: b[:, :], dest[:, t, :])

            w = chunked(take_job(K, pe), KC, 408)
            columns(w, 0, 128, iqT[:, 0, :], scale=32 ** -0.5)
            columns(w, 128, 128, iqT[:, 1, :], scale=32 ** -0.5)
            columns(w, 256, 128, ikT)
            columns(w, 384, 16, K.glr)
            for t in range(T):
                unit([(K.ht[:, c, P * t:P * t + P], w[:, c, 400:408]) for c in range(KC)], lambda b: b[:, 0:8],
                     iw[:, t, :], scale=8 ** -0.5)
            end_job(K)
            pe.wait_ge(taken, 3)
            for i, (t, h) in enumerate(score_units):
                g, n = 32 * (h % 4), P * (t + 1)
                unit([(iqT[g:g + 32, h // 4, P * t:P * t + P], ikT[g:g + 32, 0:n])], lambda b, n=n: b[:, 0:n],
                     relu[:, i % 3, 0:n], func=ACT.Relu)
            for dest in (K.q_rows, K.k_rows, K.v):
                rows(chunked(take_job(K, pe), KC, 512), dest)
                end_job(K)
            w = chunked(take_job(K, pe), KC, 512)
            for j in range(2):
                columns(w, 128 * j, 128, K.qb[:, j, :])
                columns(w, 256 + 128 * j, 128, K.kb[:, j, :])
            end_job(K)
            for dest in (K.vb, K.rg):
                rows(chunked(take_job(K, pe), KC, 512), dest)
                end_job(K)

        first_score = 8

        @block.scalar
        def _(act):
            for u, (dest, src, func, scale) in enumerate(copies):
                act.wait_ge(K.products, base + u + 1)
                i = u - first_score
                if 3 <= i < len(score_units):
                    act.wait_ge(scored, i - 2)
                act.activation(dest, src, func, scale=scale).then_inc(taken, 1)

        @block.vector
        def _(dve):
            step = K.dve.on(dve)
            step(dve.tensor_copy(K.keep[:, 0, 0:P], K.causal[:, S - P:S]))
            for i, (t, h) in enumerate(score_units):
                n = P * (t + 1)
                dve.wait_ge(taken, first_score + i + 1)
                if h == 0:
                    ins = dve.tensor_scalar(K.keep[:, t, 0:n], relu[:, i % 3, 0:n], iw[:, t, h:h + 1], None, ALU.mult)
                else:
                    dve.wait_ge(scored, i)
                    ins = dve.scalar_tensor_tensor(out=K.keep[:, t, 0:n], in0=relu[:, i % 3, 0:n],
                                                   scalar=iw[:, t, h:h + 1], in1=K.keep[:, t, 0:n], op0=ALU.mult,
                                                   op1=ALU.add)
                ins.then_inc(scored, 1)
            dve.wait_ge(scored, len(score_units))
            for t in range(1, T):
                n = P * (t + 1)
                score = K.keep[:, t, 0:n]
                step(dve.tensor_tensor(score[:, n - P:n], score[:, n - P:n], K.causal[:, S - P:S], ALU.add))
                for _ in range(TOPK // 8):
                    step(dve.max(top8, score))
                    step(dve.match_replace(score, top8, score, TAKEN))
                step(dve.tensor_scalar(score, score, TAKEN, MASKED, ALU.not_equal, ALU.mult))

        @block.sync
        def _(sp):
            load_jobs(K, sp, 6)


TOPK = 128



def gla(K):
    nc, I = K.nc, K.I
    C, NCH = 64, S // 64
    s = K.sem
    loaded = s("gla_weights_arrived")
    w2 = K.small[0:16, 1536:1792]
    gate_b = K.small[:, 72:74]
    gla_g = K.small[:, 80:208]
    el = K.small[:, 208:224].rearrange("p (j c) -> p j c", j=2)
    per_head = lambda a: a.rearrange("p (h s) -> p h s", h=4)
    qe, ke = per_head(K.ht2[0:C, 0:2048]), per_head(K.ht2[0:C, 2048:4096])
    qi, v_odd = per_head(K.slot[0][0:C, 0:2048]), per_head(K.slot[0][0:C, 2048:4096])
    el_head = K.small[0:C, 1792:1824].rearrange("p (c h) -> p c h", h=4)
    z, tmp, cum, e_up, e_down = (K.heads[:, 1024 * n:1024 * n + 1024].rearrange("p (j s) -> p j s", j=2)
                                 for n in range(5))
    kdr = K.heads[:, 5120:6144].rearrange("p (t d) -> p t d", t=T)
    kdr_odd = K.heads[0:C, 6144:7168].rearrange("p (t d) -> p t d", t=T)
    e_in, kd = z, tmp
    reset = K.gain[:, 0:512]
    masked = K.gain[0:C, 512:1024].rearrange("p (b h s) -> p b h s", b=2, h=4)
    state = K.shift[0:C, 0:1024].rearrange("p (b h v) -> p b h v", b=2, h=4)

    def of_chunk(even, odd, c):
        return (odd if c % 2 else even)[0:C, c // 2]

    both = lambda a: a.rearrange("p j (c s) -> p (j c) s", s=C)
    z_in, gate_in, decays, kd_ready = s("gla_z_ready"), s("gla_abs_ready"), s("gla_exponents"), s("gla_exps")
    ops_ready, kd_rows = s("gla_operands"), s("gla_kd_rows")
    masked_ready, outs_taken, state_ready = s("gla_masked"), s("gla_outs_taken"), s("gla_state")
    silu_ready, squares, std = s("gla_silu"), s("gla_squares"), s("gla_std")
    base = K.n_products

    with nc.Block(no_gpsimd_drain=True) as block:
        @block.tensor
        def _(pe):
            pe.wait_ge(loaded, 48)
            for j in range(2):
                product(K, pe.matmul(K.bank[j][:, :], w2[:, P * j:P * j + P], K.glr, start=True, stop=True))
            pe.wait_ge(ops_ready, 1)
            for j in range(2):
                for t in range(T):
                    mm = pe.transpose(K.bank[2 + j][:, P * t:P * t + P], kd[:, j, P * t:P * t + P], K.ident[:, :])
                product(K, mm)
            pe.wait_ge(kd_rows, 4)

            def scores(c):
                if c >= 2:
                    pe.wait_ge(masked_ready, c - 1)
                for h in range(4):
                    mm = pe.matmul(K.bank[c % 2][0:C, C * h:C * h + C], ke[:, h, C * c:C * c + C],
                                   qe[:, h, C * c:C * c + C], start=True, stop=True)
                product(K, mm)

            scores(0)
            for c in range(NCH):
                pb = C * (c % 2)
                keys, values = of_chunk(kdr, kdr_odd, c), of_chunk(K.vb, v_odd, c)
                if c + 1 < NCH:
                    scores(c + 1)
                if c >= 2:
                    pe.wait_ge(state_ready, c - 1)
                for h in range(4):
                    mm = pe.matmul(K.bank[4 + c % 2][0:C, P * h:P * h + P], keys[:, C * h:C * h + C],
                                   values[:, P * h:P * h + P], start=True, stop=True)
                product(K, mm)
                pe.wait_ge(masked_ready, c + 1)
                if c >= 1:
                    pe.wait_ge(state_ready, c)
                if c >= 2:
                    pe.wait_ge(outs_taken, c - 1)
                for h in range(4):
                    o = K.bank[6 + c % 2][pb:pb + C, P * h:P * h + P]
                    mm = pe.matmul(o, masked[:, c % 2, h, :], values[:, P * h:P * h + P], start=True, stop=c == 0)
                    if c > 0:
                        mm = pe.matmul(o, qi[:, h, C * c:C * c + C], state[:, (c - 1) % 2, h, :], start=False, stop=True)
                product(K, mm)

        def at_scores(c):
            return base + 5 + (3 * (c - 1) + 1 if c else 0)

        def at_state(c):
            return base + 5 + 3 * c + (2 if c + 1 < NCH else 1)

        @block.scalar
        def _(act):
            step = K.act.on(act)
            act.wait_ge(z_in, 2)
            step(act.activation(tmp, z, ACT.Abs))
            step(act.activation(tmp, tmp, ACT.Exp, scale=-1.0))
            act.activation(tmp, tmp, ACT.Ln, bias=K.ones[:, 0:1]).then_inc(gate_in, 1)
            act.wait_ge(decays, 1)
            act.activation(e_down, e_up, ACT.Exp, scale=-1.0).then_inc(kd_rows, 1)
            act.wait_ge(kd_rows, 1)
            act.activation(e_up, e_up, ACT.Exp)
            act.activation(e_in, cum, ACT.Exp)
            act.activation(kd, kd, ACT.Exp)
            act.activation(el, cum.rearrange("p j (c s) -> p j c s", s=C)[:, :, :, C - 1], ACT.Exp).then_inc(kd_ready, 1)
            act.activation(v_odd, K.vb[C:P, :, :], ACT.Copy).then_inc(kd_rows, 1)
            for j in range(2):
                act.wait_ge(K.products, base + 3 + j)
                both_chunks = K.bank[2 + j][:, :].rearrange("p (t d) -> p t d", t=T)
                act.activation(kdr[:, :, P * j:P * j + P], both_chunks, ACT.Copy)
                act.activation(kdr_odd[:, :, P * j:P * j + P], both_chunks[C:P], ACT.Copy).then_inc(kd_rows, 1)
            act.activation(K.rg, K.rg, ACT.Silu).then_inc(silu_ready, 1)
            for c in range(NCH):
                pb, t = C * (c % 2), c // 2
                act.wait_ge(K.products, at_state(c) + 1)
                act.activation(K.hr[pb:pb + C, t, 512:1024], K.bank[6 + c % 2][pb:pb + C, :], ACT.Copy).then_inc(outs_taken, 1)
            act.wait_ge(outs_taken, NCH)
            act.activation(K.heads[:, 0:2048].rearrange("p (t d) -> p t d", t=T), K.hr[:, :, 512:1024],
                           ACT.Square).then_inc(squares, 1)
            act.wait_ge(std, 1)
            act.activation(K.small[:, 240:256], K.small[:, 224:240], ACT.Sqrt, scale=1.0 / P,
                           bias=K.eps[:, 0:1]).then_inc(silu_ready, 1)

        @block.vector
        def _(dve):
            step = K.dve.on(dve)
            dve.wait_ge(loaded, 48)
            step(dve.memset(reset, 1.0))
            step(dve.memset(reset.rearrange("p (c s) -> p c s", s=C)[:, :, 0:1], 0.0))
            for j in range(2):
                dve.wait_ge(K.products, base + 1 + j)
                dve.tensor_scalar(z[:, j, :], K.bank[j][:, :], gate_b[:, j:j + 1], None, ALU.add).then_inc(z_in, 1)
            dve.wait_ge(gate_in, 1)
            step(dve.scalar_tensor_tensor(out=z, in0=z, scalar=0.0, in1=tmp, op0=ALU.min, op1=ALU.subtract))
            step(dve.tensor_scalar(z, z, 1.0 / 16.0, None, ALU.mult))
            for j in range(2):
                step(dve.tensor_tensor_scan(cum[:, j, :], reset, z[:, j, :], 0.0, ALU.mult, ALU.add))
            cb = both(cum)
            mid = cb[:, :, C // 2 - 1:C // 2].broadcast_to([P, 2 * NCH, C])
            end = cb[:, :, C - 1:C].broadcast_to([P, 2 * NCH, C])
            step(dve.tensor_tensor(both(e_up), cb, mid, ALU.subtract))
            step(dve.tensor_tensor(both(kd), end, cb, ALU.subtract))
            dve.tensor_scalar(e_up, e_up, -EXP_LIMIT, EXP_LIMIT, ALU.max, ALU.min).then_inc(decays, 1)
            dve.wait_ge(kd_ready, 1)
            for odd in range(2):
                half = slice(C * odd, C * odd + C)
                dve.scalar_tensor_tensor(out=qe[:, odd::2, :], in0=K.qb[half], scalar=C ** -0.5, in1=e_up[half],
                                         op0=ALU.mult, op1=ALU.mult)
                dve.scalar_tensor_tensor(out=qi[:, odd::2, :], in0=K.qb[half], scalar=C ** -0.5, in1=e_in[half],
                                         op0=ALU.mult, op1=ALU.mult)
                dve.tensor_tensor(ke[:, odd::2, :], K.kb[half], e_down[half], ALU.mult)
                dve.tensor_copy(el_head[:, :, odd::2], el[half].rearrange("p j c -> p c j"))
            dve.tensor_tensor(kd, K.kb, kd, ALU.mult).then_inc(ops_ready, 1)
            dve.wait_ge(ops_ready, 1)
            for c in range(NCH):
                dve.wait_ge(K.products, at_scores(c))
                if c >= 2:
                    dve.wait_ge(K.products, at_state(c - 2) + 1)
                dve.tensor_tensor(masked[:, c % 2, :, :],
                                  K.bank[c % 2][0:C, 0:256].rearrange("p (h s) -> p h s", h=4),
                                  K.tri_incl[0:C, 0:C].unsqueeze(1).broadcast_to([C, 4, C]),
                                  ALU.mult).then_inc(masked_ready, 1)
                dve.wait_ge(K.products, at_state(c))
                added = K.bank[4 + c % 2][0:C, :].rearrange("p (h v) -> p h v", h=4)
                if c == 0:
                    dve.tensor_copy(state[:, 0, :, :], added).then_inc(state_ready, 1)
                else:
                    if c >= 2:
                        dve.wait_ge(K.products, at_state(c - 1) + 1)
                    dve.wait_ge(state_ready, c)
                    step(dve.tensor_tensor(state[:, c % 2, :, :], state[:, (c - 1) % 2, :, :],
                                           el_head[:, c, :].unsqueeze(2).broadcast_to([C, 4, P]), ALU.mult))
                    dve.tensor_tensor(state[:, c % 2, :, :], state[:, c % 2, :, :], added,
                                      ALU.add).then_inc(state_ready, 1)
            dve.wait_ge(squares, 1)
            dve.tensor_reduce(K.small[:, 224:240], K.heads[:, 0:2048].rearrange("p (g v) -> p g v", v=P), AX.X,
                              ALU.add).then_inc(std, 1)
            dve.wait_ge(silu_ready, 2)
            step(dve.reciprocal(K.small[:, 224:240], K.small[:, 240:256]))
            for t in range(T):
                o = K.hr[:, t, 512:1024].rearrange("p (h v) -> p h v", h=4)
                r = K.small[:, 224 + 4 * t:228 + 4 * t].unsqueeze(2).broadcast_to([P, 4, P])
                step(dve.tensor_tensor(o, o, r, ALU.mult))
                step(dve.tensor_tensor(o, o, gla_g.unsqueeze(1).broadcast_to([P, 4, P]), ALU.mult))
                step(dve.tensor_tensor(o, o, K.rg[:, t, :].rearrange("p (h v) -> p h v", h=4), ALU.mult))

        @block.sync
        def _(sp):
            sp.dma_start(w2, I["gla_gate_w2"][0]).then_inc(loaded, 16)
            sp.dma_start(gate_b, I["gla_gate_b"][0].rearrange("(j p) -> p j", p=P),
                         allow_slow_non_contiguous=True).then_inc(loaded, 16)
            sp.dma_start(gla_g, bcast(I["gla_out_norm_g"][0], P)).then_inc(loaded, 16)


EXP_LIMIT = 80.0



def qk_norm(K):
    nc, I = K.nc, K.I
    s = K.sem
    loaded, squares, sums, std, normed = (s("qkn_gains"), s("qkn_squares"), s("qkn_sums"), s("qkn_std"), s("qkn_rows"))
    taken = (s("qkn_act_copied"), s("qkn_dve_copied"))
    K.bias_in = s("bias_matrix_arrived")
    gains = K.small[:, 256:384].rearrange("p (n d) -> p n d", n=2)
    ss, sd, rs = K.small[:, 384:448], K.small[:, 448:512], K.small[:, 512:576]
    sq = K.slot[0]
    rows = K.scr[:, 0:4096].rearrange("p (g d) -> p g d", d=64)
    at = []
    with nc.Block(no_gpsimd_drain=True) as block:
        @block.tensor
        def _(pe):
            for u in range(2 * HEADS):
                n, h = divmod(u, HEADS)
                pe.wait_ge(normed, n + 1)
                if u >= 8:
                    pe.wait_ge(taken[u % 2], (u - 8) // 2 + 1)
                src = (K.q_rows, K.k_rows)[n]
                for t in range(T):
                    mm = pe.transpose(K.bank[u % 8][0:64, P * t:P * t + P], src[:, t, 64 * h:64 * h + 64], K.ident[:, :])
                at.append(product(K, mm))

        def copy_heads(eng, copy, which):
            for u in range(which, 2 * HEADS, 2):
                n, h = divmod(u, HEADS)
                eng.wait_ge(K.products, at[u])
                copy((K.qt, K.kt)[n][0:64, h, :], K.bank[u % 8][0:64, :]).then_inc(taken[which], 1)

        @block.scalar
        def _(act):
            act.activation(sq, K.scr[:, 0:4096], ACT.Square).then_inc(squares, 1)
            act.wait_ge(sums, 1)
            act.activation(sd, ss, ACT.Sqrt, scale=1.0 / 64, bias=K.eps[:, 0:1]).then_inc(std, 1)
            copy_heads(act, lambda o, i: act.activation(o, i, ACT.Copy), 0)

        @block.vector
        def _(dve):
            step = K.dve.on(dve)
            dve.wait_ge(squares, 1)
            dve.tensor_reduce(ss, sq.rearrange("p (g d) -> p g d", d=64), AX.X, ALU.add).then_inc(sums, 1)
            dve.wait_ge(std, 1)
            step(dve.reciprocal(rs, sd))
            step(dve.tensor_scalar(rs[:, 0:32], rs[:, 0:32], 64 ** -0.5, None, ALU.mult))
            dve.wait_ge(loaded, 32)
            for n in range(2):
                part = rows[:, 32 * n:32 * n + 32, :]
                step(dve.tensor_tensor(part, part, rs[:, 32 * n:32 * n + 32].unsqueeze(2).broadcast_to([P, 32, 64]),
                                       ALU.mult))
                dve.tensor_tensor(part, part, gains[:, n, :].unsqueeze(1).broadcast_to([P, 32, 64]),
                                  ALU.mult).then_inc(normed, 1)
            copy_heads(dve, dve.tensor_copy, 1)

        @block.sync
        def _(sp):
            sp.dma_start(gains[:, 0, :], bcast(I["q_norm_g"][0], P)).then_inc(loaded, 16)
            sp.dma_start(gains[:, 1, :], bcast(I["k_norm_g"][0], P)).then_inc(loaded, 16)
            flat = bass.AP(K.bias_dram.tensor, P - 1, [[HEADS * BIAS_COLS - 1, P], [BIAS_COLS, HEADS], [1, S]])
            sp.dma_start(K.ht, flat).then_inc(K.bias_in, 16)


def attention(K, tag, dim, out_col, bias=None, keep=None):
    nc = K.nc
    s = K.sem
    maxed, expd, turned = s(f"{tag}_max_ready"), s(f"{tag}_probs_ready"), s(f"{tag}_turned_copied")
    scored, normed = s(f"{tag}_logits_read"), s(f"{tag}_out_normed")
    z = K.scr[:, 4096:5632].rearrange("p (b s) -> p b s", b=3)
    probs = K.scr[:, 5632:7168].rearrange("p (b s) -> p b s", b=3)
    turn = K.scr[:, 7168:8192].rearrange("p (b s) -> p b s", b=2)
    mx, neg, rsum, rinv = (K.small[:, 576 + 32 * n:608 + 32 * n] for n in range(4))
    units = [(h, t) for h in range(HEADS) for t in range(T)]
    N = len(units)
    at_s, at_t, at_o = [], [], []
    with nc.Block(no_gpsimd_drain=True) as block:
        @block.tensor
        def _(pe):
            for i in range(N + 3):
                if i < N:
                    h, t = units[i]
                    n = P * (t + 1)
                    if i >= 3:
                        pe.wait_ge(scored, i - 2)
                    at_s.append(product(K, pe.matmul(K.bank[i % 3][:, 0:n], K.qt[0:dim, h, P * t:P * t + P],
                                                     K.kt[0:dim, h, 0:n], start=True, stop=True)))
                if 2 <= i < N + 2:
                    u = i - 2
                    h, t = units[u]
                    pe.wait_ge(expd, u + 1)
                    if u >= 2:
                        pe.wait_ge(turned, u - 1)
                    for k in range(t + 1):
                        mm = pe.transpose(K.bank[3 + u % 2][:, P * k:P * k + P], probs[:, u % 3, P * k:P * k + P],
                                          K.ident[:, :])
                    at_t.append(product(K, mm))
                if i >= 3:
                    u = i - 3
                    h, t = units[u]
                    pe.wait_ge(turned, u + 1)
                    if u >= 2:
                        pe.wait_ge(normed, u - 1)
                    for k in range(t + 1):
                        mm = pe.matmul(K.bank[5 + u % 2][:, 0:64], turn[:, u % 2, P * k:P * k + P],
                                       K.v[:, k, 64 * h:64 * h + 64], start=k == 0, stop=k == t)
                    at_o.append(product(K, mm))

        @block.scalar
        def _(act):
            for i in range(N + 2):
                if i < N:
                    n = P * (units[i][1] + 1)
                    act.wait_ge(maxed, i + 1)
                    if i >= 3:
                        act.wait_ge(K.products, at_t[i - 3])
                    act.activation(probs[:, i % 3, 0:n], z[:, i % 3, 0:n], ACT.Exp, bias=neg[:, i:i + 1],
                                   accum_out=rsum[:, i:i + 1]).then_inc(expd, 1)
                if i >= 2:
                    u = i - 2
                    n = P * (units[u][1] + 1)
                    act.wait_ge(K.products, at_t[u])
                    if u >= 2:
                        act.wait_ge(K.products, at_o[u - 2])
                    act.activation(turn[:, u % 2, 0:n], K.bank[3 + u % 2][:, 0:n], ACT.Copy).then_inc(turned, 1)

        @block.vector
        def _(dve):
            step = K.dve.on(dve)
            if bias is not None:
                dve.wait_ge(K.bias_in, 16)
            for i in range(N + 3):
                if i < N:
                    h, t = units[i]
                    n = P * (t + 1)
                    dve.wait_ge(K.products, at_s[i])
                    if i >= 3:
                        dve.wait_ge(expd, i - 2)
                    zi, logits = z[:, i % 3, 0:n], K.bank[i % 3][:, 0:n]
                    if bias is not None:
                        step(dve.tensor_tensor(zi, logits, bias[:, h, S - n:S], ALU.add))
                        logits = zi
                    mask = K.causal[:, S - n:S] if keep is None else keep[:, t, 0:n]
                    dve.tensor_tensor_reduce(zi, logits, mask, 1.0, float(MASKED) * 2, ALU.add, ALU.max,
                                             mx[:, i:i + 1]).then_inc(scored, 1)
                    dve.wait_ge(scored, i + 1)
                    dve.tensor_scalar(neg[:, i:i + 1], mx[:, i:i + 1], -1.0, None, ALU.mult).then_inc(maxed, 1)
                if i >= 3:
                    u = i - 3
                    h, t = units[u]
                    dve.wait_ge(expd, u + 1)
                    step(dve.reciprocal(rinv[:, u:u + 1], rsum[:, u:u + 1]))
                    dve.wait_ge(K.products, at_o[u])
                    dve.tensor_scalar(K.hr[:, t, out_col + 64 * h:out_col + 64 * h + 64], K.bank[5 + u % 2][:, 0:64],
                                      rinv[:, u:u + 1], None, ALU.mult).then_inc(normed, 1)


def first_attention(K):
    attention(K, "attn1", 64, 0, bias=K.ht, keep=K.keep)


def turn_rows(K, tag):
    nc = K.nc
    taken = (K.sem(f"{tag}_act_copied"), K.sem(f"{tag}_dve_copied"))
    at = []
    with nc.Block(no_gpsimd_drain=True) as block:
        @block.tensor
        def _(pe):
            for u in range(2 * T):
                t, half = divmod(u, 2)
                for k in range(4):
                    mm = pe.transpose(K.bank[u][:, P * k:P * k + P], K.hr[:, t, 4 * half + k::KC], K.ident[:, :])
                at.append(product(K, mm))

        def copy(eng, ins, which):
            for u in range(which, 2 * T, 2):
                t, half = divmod(u, 2)
                eng.wait_ge(K.products, at[u])
                ins(K.ht[:, 4 * half:4 * half + 4, P * t:P * t + P],
                    K.bank[u][:, :].rearrange("p (k s) -> p k s", k=4)).then_inc(taken[which], 1)
            eng.wait_ge(taken[which], T)

        @block.scalar
        def _(act):
            copy(act, lambda o, i: act.activation(o, i, ACT.Copy), 0)

        @block.vector
        def _(dve):
            copy(dve, dve.tensor_copy, 1)


def add_rows_product(K, tag, jobs_ahead, gate=None, gate_ready=None, vectors=()):
    nc = K.nc
    added = K.sem(f"{tag}_added")
    at = []
    with nc.Block(no_gpsimd_drain=True) as block:
        @block.tensor
        def _(pe):
            for j in range(2):
                w = chunked(take_job(K, pe), KC, 512)
                for t in range(T):
                    u = T * j + t
                    for c in range(KC):
                        mm = pe.matmul(K.bank[u][:, :], K.ht[:, c, P * t:P * t + P], w[:, c, :], start=c == 0,
                                       stop=c == KC - 1)
                    at.append(product(K, mm))
                end_job(K)

        @block.vector
        def _(dve):
            step = K.dve.on(dve)
            if gate is not None:
                dve.wait_ge(*gate_ready)
            for u in range(2 * T):
                j, t = divmod(u, T)
                x = K.x[:, t, 512 * j:512 * j + 512]
                dve.wait_ge(K.products, at[u])
                src = K.bank[u][:, :]
                if gate is not None:
                    step(dve.tensor_tensor(src, src, gate[:, 512 * j:512 * j + 512], ALU.mult))
                dve.tensor_tensor(x, x, src, ALU.add).then_inc(added, 1)
            dve.wait_ge(added, 2 * T)

        @block.sync
        def _(sp):
            load_jobs(K, sp, jobs_ahead)
            for place, src, arrived in vectors:
                sp.dma_start(place, src).then_inc(arrived, 16)


def first_output(K):
    turn_rows(K, "turn1")
    K.gain2_in = K.sem("norm2_gain_arrived")
    add_rows_product(K, "out1", 2, vectors=[(K.gain[:, :], bcast(K.I["norm2_g"][0], P), K.gain2_in)])
    norm_columns(K, "norm2", store=True, gain_ready=(K.gain2_in, 16))



def moe_buffers(K, experts):
    flat = K.keep.rearrange("p t s -> p (t s)")
    m = State()
    m.E = experts
    m.table = flat[:, 0:8 * experts].rearrange("p (t e w) -> p t e w", t=T, w=2)
    m.rank, m.gate, m.chosen, m.work, m.work2 = (
        flat[:, 512 + 256 * n:512 + 256 * n + 4 * experts].rearrange("p (t e) -> p t e", t=T) for n in range(5))
    m.padded = K.small[:, 0:288].rearrange("p (t e) -> p t e", t=T)
    m.top8 = K.small[:, 288:320].rearrange("p (t e) -> p t e", t=T)
    m.tiny = K.small[:, 320:640]
    m.bias = K.small[:, 640:704]
    m.most = K.small[:, 704:705].bitcast(I32)
    return m


def pick_top(step, dve, m, padded, n, top):
    for t in range(T):
        step(dve.max(m.top8[:, t, :], padded[:, t, 0:8 - top + n]))
        step(dve.match_replace(padded[:, t, 0:8 - top + n], m.top8[:, t, :], padded[:, t, 0:8 - top + n], TAKEN))


def hier_router(K, m):
    I, s = K.I, K.sem
    bias_in, exp_in, exp_out = s("router1_bias_arrived"), s("router1_exp_args"), s("router1_exps")
    logits, g_exp = m.tiny[:, 0:144].rearrange("p (t n) -> p t n", t=T), m.tiny[:, 144:160].rearrange("p (t n) -> p t n", t=T)
    picked_g, gsum = m.tiny[:, 160:176].rearrange("p (t n) -> p t n", t=T), m.tiny[:, 176:180]
    e_sel, e_exp = (m.tiny[:, a:a + 32].rearrange("p (t n) -> p t n", t=T) for a in (180, 212))
    picked_e, den = m.tiny[:, 244:276].rearrange("p (t n) -> p t n", t=T), m.tiny[:, 276:280]
    G, EG = 4, 8

    def sync(sp):
        sp.dma_start(m.bias[:, 0:4], bcast(I["b_router_group"][0], P)).then_inc(bias_in, 16)
        sp.dma_start(m.bias[:, 4:36], bcast(I["b_router_expert"][0], P)).then_inc(bias_in, 16)

    def scalar(act):
        act.wait_ge(exp_in, 1)
        act.activation(g_exp, g_exp, ACT.Exp).then_inc(exp_out, 1)
        act.wait_ge(exp_in, 2)
        act.activation(m.tiny[:, 212:244], m.tiny[:, 212:244], ACT.Exp).then_inc(exp_out, 1)

    def vector(dve, step, raw):
        dve.wait_ge(bias_in, 32)
        step(dve.tensor_tensor(logits, raw, m.bias[:, 0:36].unsqueeze(1).broadcast_to([P, T, 36]), ALU.add))
        step(dve.memset(m.padded[:, :, 0:7], SENTINEL))
        step(dve.tensor_copy(m.padded[:, :, 7:11], logits[:, :, 0:4]))
        pick_top(step, dve, m, m.padded, G, 1)
        step(dve.tensor_scalar(picked_g, m.padded[:, :, 7:11], TAKEN, None, ALU.is_equal))
        dve.tensor_tensor(g_exp, logits[:, :, 0:4], m.top8[:, :, 7:8].broadcast_to([P, T, G]),
                          ALU.subtract).then_inc(exp_in, 1)
        step(dve.tensor_tensor(m.work.rearrange("p t (e g) -> p (t e) g", g=G).rearrange("p (t e) g -> p t e g", t=T),
                               logits[:, :, 4:36].rearrange("p t (g e) -> p t e g", g=G),
                               picked_g.unsqueeze(2).broadcast_to([P, T, EG, G]), ALU.mult))
        step(dve.tensor_reduce(m.tiny[:, 180:212], m.work.rearrange("p t (e g) -> p t e g", g=G), AX.X, ALU.add))
        step(dve.memset(m.padded[:, :, 0:6], SENTINEL))
        step(dve.tensor_copy(m.padded[:, :, 6:14], e_sel))
        pick_top(step, dve, m, m.padded, EG, 2)
        step(dve.tensor_scalar(picked_e, m.padded[:, :, 6:14], TAKEN, None, ALU.is_equal))
        dve.tensor_tensor(e_exp, e_sel, m.top8[:, :, 6:7].broadcast_to([P, T, EG]), ALU.subtract).then_inc(exp_in, 1)
        dve.wait_ge(exp_out, 2)
        step(dve.tensor_tensor(e_exp, e_exp, picked_e, ALU.mult))
        step(dve.tensor_reduce(den, e_exp, AX.X, ALU.add))
        step(dve.tensor_reduce(gsum, g_exp, AX.X, ALU.add))
        step(dve.tensor_tensor(den, den, gsum, ALU.mult))
        step(dve.reciprocal(den, den))
        step(dve.tensor_tensor(e_exp, e_exp, den.unsqueeze(2).broadcast_to([P, T, EG]), ALU.mult))
        for dest, per_expert in ((m.gate, e_exp), (m.chosen, picked_e)):
            step(dve.tensor_tensor(dest.rearrange("p t (g e) -> p t g e", g=G),
                                   picked_g.unsqueeze(3).broadcast_to([P, T, G, EG]),
                                   per_expert.unsqueeze(2).broadcast_to([P, T, G, EG]), ALU.mult))

    return sync, scalar, vector


def rank_tokens(K, tag, m, width, router, jobs_ahead=0):
    nc, E = K.nc, m.E
    s = K.sem
    chosen, tables, stored = s(f"{tag}_chosen"), s(f"{tag}_tables"), s(f"{tag}_acc_stored")
    sync, scalar, vector = router
    at = []
    with nc.Block(no_gpsimd_drain=True) as block:
        @block.tensor
        def _(pe):
            w = chunked(take_job(K, pe), KC, width)
            for t in range(T):
                for c in range(KC):
                    mm = pe.matmul(K.bank[0][:, width * t:width * t + width], K.ht[:, c, P * t:P * t + P], w[:, c, :],
                                   start=c == 0, stop=c == KC - 1)
            at.append(product(K, mm))
            end_job(K)
            pe.wait_ge(chosen, 1)
            for t in range(T):
                for before in range(t + 1):
                    mm = pe.matmul(K.bank[1][:, E * t:E * t + E], (K.tri if before == t else K.ones)[:, :],
                                   m.chosen[:, before, :], start=before == 0, stop=before == t)
            for t in range(T):
                mm = pe.matmul(K.bank[2][:, 0:E], K.ones[:, :], m.chosen[:, t, :], start=t == 0, stop=t == T - 1)
            at.append(product(K, mm))

        @block.scalar
        def _(act):
            scalar(act)

        @block.vector
        def _(dve):
            step = K.dve.on(dve)
            dve.wait_ge(K.products, at[0])
            vector(dve, step, K.bank[0][:, 0:T * width].rearrange("p (t n) -> p t n", t=T))
            step(dve.tensor_copy(m.table[:, :, :, 1], m.gate))
            dve.tensor_copy(m.table[:, :, :, 0], K.token_id[:, :].unsqueeze(2).broadcast_to([P, T, E])).then_inc(chosen, 1)
            dve.wait_ge(K.products, at[1])
            step(dve.scalar_tensor_tensor(out=m.rank, in0=K.bank[1][:, 0:T * E].rearrange("p (t e) -> p t e", t=T),
                                          scalar=1.0, in1=m.chosen, op0=ALU.add, op1=ALU.mult))
            dve.tensor_scalar(m.rank, m.rank, -1.0, None, ALU.add).then_inc(tables, 1)
            dve.tensor_reduce(m.tiny[:, 0:1], K.bank[2][:, 0:E], AX.X, ALU.max).then_inc(tables, 1)
            dve.wait_ge(tables, 2)
            step(dve.tensor_copy(m.most, m.tiny[:, 0:1]))

        @block.sync
        def _(sp):
            sync(sp)
            load_jobs(K, sp, jobs_ahead)



def experts_stage(K, tag, m, w_gate, w_up, w_down, init):
    nc, E = K.nc, m.E
    s = K.sem
    w_gate, w_up, w_down = w_gate[0], w_up[0], w_down[0]
    f = K.heads
    ring2 = lambda a, n: a.rearrange("p (b n) -> p b n", b=2)
    xg, xt, ys = (ring2(f[:, 2048 * n:2048 * n + 2048], 2) for n in range(3))
    silu, hid, hidt = (ring2(f[:, 6144 + 512 * n:6656 + 512 * n], 2) for n in range(3))
    onehot = f[:, 7680:8704].rearrange("p (b t s) -> p b t s", b=2, t=T)
    idx = K.small[:, 1024:1028].bitcast(I32)
    gate = K.small[:, 1028:1032]
    gu = [K.big[:, 4096 * b:4096 * b + 4096].rearrange("p (g c f) -> p g c f", g=2, c=KC) for b in range(2)]
    dn = [K.big[:, 8192 + 2048 * b:8192 + 2048 * b + 2048].rearrange("p (j d) -> p j d", j=FH) for b in range(2)]
    b_list, b_xt, b_au, b_ht, b_y = K.bank[0], K.bank[1:3], K.bank[3:5], K.bank[5], K.bank[6:8]

    listed, list_mm, idx_ready = s(f"{tag}_onehot_ready"), s(f"{tag}_list_product"), s(f"{tag}_list_copied")
    *gathered, scattered = K.row_sems[tag]
    xt_mm, xt_copied = s(f"{tag}_rows_turned"), s(f"{tag}_rows_turned_copied")
    au_mm, silu_ready, hid_ready = s(f"{tag}_gate_up_product"), s(f"{tag}_silu_ready"), s(f"{tag}_hidden_ready")
    ht_mm, ht_copied = s(f"{tag}_hidden_turned"), s(f"{tag}_hidden_turned_copied")
    y_mm, y_dve, y_act = s(f"{tag}_down_product"), s(f"{tag}_y_dve_copied"), s(f"{tag}_y_act_copied")
    gu_in = [s(f"{tag}_gate_up_even"), s(f"{tag}_gate_up_odd")]
    d_in = [s(f"{tag}_down_even"), s(f"{tag}_down_odd")]
    cleared = s(f"{tag}_rows_cleared")
    row_dmas = s(f"{tag}_row_dmas")

    def all_steps(eng, step):
        def static(i):
            step(i, i % 4, lambda d: 0 <= i + d < E)
        for i in range(-3, 4):
            static(i)
        with eng.Fori(4, E - 7, 4) as i:
            for r in range(4):
                step(i + r, r, lambda d: True)
        for i in range(E - 4, E + 1):
            static(i)

    def expert1(e):
        return slice(e, e + 1) if isinstance(e, int) else bass.ds(e, 1)

    late = lambda i, n: not isinstance(i, int) or i >= n

    with nc.Block(no_gpsimd_drain=True) as block:
        @block.tensor
        def _(pe):
            def step(i, r, has):
                if has(-1):
                    b = (r - 1) % 2
                    pe.wait_ge(hid_ready, i)
                    if late(i, 2):
                        pe.wait_ge(ht_copied, i - 1)
                    for j in range(FH):
                        mm = pe.transpose(b_ht[:, P * j:P * j + P], hid[:, b, j::FH], K.ident[:, :])
                    mm.then_inc(ht_mm, 1)
                if has(0):
                    b = r % 2
                    pe.wait_ge(xt_copied, 2 * i + 2)
                    pe.wait_ge(gu_in[b], 16 * (i - b) + 32)
                    if late(i, 2):
                        pe.wait_ge(hid_ready, i - 1)
                    for c in range(KC):
                        mm = pe.matmul(b_au[b][:, :], xt[:, b, P * c:P * c + P], gu[b][:, :, c, :], start=c == 0,
                                       stop=c == KC - 1)
                    mm.then_inc(au_mm, 1)
                if has(-1):
                    b = (r - 1) % 2
                    pe.wait_ge(ht_copied, i)
                    pe.wait_ge(d_in[b], 8 * (i - 1 - b) + 16)
                    if late(i, 2):
                        pe.wait_ge(y_dve, i - 1)
                        pe.wait_ge(y_act, i - 1)
                    for half in range(2):
                        for j in range(FH):
                            mm = pe.matmul(b_y[half][:, :], hidt[:, b, P * j:P * j + P],
                                           dn[b][:, j, 512 * half:512 * half + 512], start=j == 0, stop=j == FH - 1)
                    mm.then_inc(y_mm, 1)
                if has(1):
                    b = (r + 1) % 2
                    pe.wait_ge(gathered[b], 8 * (i + 1 - b) + 16)
                    if late(i, 0):
                        pe.wait_ge(xt_copied, 2 * i + 2)
                    for half in range(2):
                        for k in range(4):
                            mm = pe.transpose(b_xt[half][:, P * k:P * k + P], xg[:, b, 4 * half + k::KC], K.ident[:, :])
                        mm.then_inc(xt_mm, 1)
                if has(2):
                    b = r % 2
                    pe.wait_ge(listed, i + 3)
                    if late(i, -1):
                        pe.wait_ge(idx_ready, 2 * i + 4)
                    for t in range(T):
                        mm = pe.matmul(b_list[:, 0:2], onehot[:, b, t, :], m.table[:, t, expert1(i + 2), :],
                                       start=t == 0, stop=t == T - 1)
                    mm.then_inc(list_mm, 1)
            all_steps(pe, step)

        @block.vector
        def _(dve):
            def step(i, r, has):
                if has(0):
                    b = r % 2
                    dve.wait_ge(silu_ready, i + 1)
                    if late(i, 2):
                        dve.wait_ge(ht_mm, i - 1)
                    dve.wait_ge(idx_ready, 2 * i + 2)
                    dve.scalar_tensor_tensor(out=hid[:, b, :], in0=silu[:, b, :], scalar=gate[:, r:r + 1],
                                             in1=b_au[b][:, FE:2 * FE], op0=ALU.mult, op1=ALU.mult).then_inc(hid_ready, 1)
                if has(-1):
                    b = (r - 1) % 2
                    dve.wait_ge(y_mm, i)
                    if late(i, 3):
                        dve.wait_ge(scattered, 16 * (i - 2))
                    dve.tensor_copy(ys[:, b, 0:512], b_y[0][:, :]).then_inc(y_dve, 1)
                if has(2):
                    if late(i, 2):
                        dve.wait_ge(scattered, 16 * (i - 1))
                    q = (r + 2) % 4
                    dve.wait_ge(list_mm, i + 3)
                    dve.tensor_scalar(idx[:, q:q + 1], b_list[:, 0:1], float(NO_TOKEN), None, ALU.add).then_inc(idx_ready, 1)
                    dve.tensor_copy(gate[:, q:q + 1], b_list[:, 1:2]).then_inc(idx_ready, 1)
                if has(3):
                    b = (r + 3) % 2
                    if late(i, -1):
                        dve.wait_ge(list_mm, i + 2)
                    dve.tensor_tensor(onehot[:, b, :, :], K.iota[:, :].unsqueeze(1).broadcast_to([P, T, P]),
                                      m.rank[:, :, expert1(i + 3)].broadcast_to([P, T, P]),
                                      ALU.is_equal).then_inc(listed, 1)
            all_steps(dve, step)

        @block.scalar
        def _(act):
            def step(i, r, has):
                if has(-1):
                    b = (r - 1) % 2
                    act.wait_ge(ht_mm, i)
                    if late(i, 3):
                        act.wait_ge(y_mm, i - 2)
                    act.activation(hidt[:, b, :], b_ht[:, 0:FE], ACT.Copy).then_inc(ht_copied, 1)
                if has(0):
                    b = r % 2
                    act.wait_ge(au_mm, i + 1)
                    if late(i, 2):
                        act.wait_ge(hid_ready, i - 1)
                    act.activation(silu[:, b, :], b_au[b][:, 0:FE], ACT.Silu).then_inc(silu_ready, 1)
                if has(-1):
                    b = (r - 1) % 2
                    act.wait_ge(y_mm, i)
                    if late(i, 3):
                        act.wait_ge(scattered, 16 * (i - 2))
                    act.activation(ys[:, b, 512:1024], b_y[1][:, :], ACT.Copy).then_inc(y_act, 1)
                if has(1):
                    b = (r + 1) % 2
                    if late(i, 1):
                        act.wait_ge(au_mm, i)
                    for half in range(2):
                        act.wait_ge(xt_mm, 2 * i + 3 + half)
                        act.activation(xt[:, b, 512 * half:512 * half + 512], b_xt[half][:, :],
                                       ACT.Copy).then_inc(xt_copied, 1)
            all_steps(act, step)

        @block.gpsimd
        def _(pool):
            pool.memset(f[:, 0:2048], 0.0).then_inc(cleared, 1)
            pool.wait_ge(cleared, 1)
            for ready, n in init:
                pool.wait_ge(ready, n)

            def step(i, r, has):
                if has(2):
                    b, q = r % 2, (r + 2) % 4
                    pool.wait_ge(idx_ready, 2 * i + 6)
                    if late(i, 0):
                        pool.wait_ge(xt_mm, 2 * i + 2)
                    pool.sem_inc(row_dmas, 1)
                    pool.indirect_dma_start(out=xg[:, b, :], out_offset=None, in_=K.h_dram,
                                            in_offset=bass.IndirectOffsetOnAxis(idx[:, q:q + 1], 0),
                                            bounds_check=S - 1, oob_is_err=False).then_inc(gathered[b], 16)
                if has(-1):
                    b, q = (r - 1) % 2, (r - 1) % 4
                    pool.wait_ge(y_dve, i)
                    pool.wait_ge(y_act, i)
                    if late(i, 2):
                        pool.wait_ge(scattered, 16 * (i - 1))
                    pool.sem_inc(row_dmas, 1)
                    scatter_add(K, pool, ys[:, b, :], idx[:, q:q + 1]).then_inc(scattered, 16)
            all_steps(pool, step)
            pool.wait_ge(scattered, 16 * E)

        @block.sync
        def _(sp):
            def load(e, b):
                at = expert1(e)
                for g, w in enumerate((w_gate, w_up)):
                    sp.dma_start(gu[b][:, g, :, :], w[at].rearrange("e (p c) f -> (e p) c f", p=P)).then_inc(gu_in[b], 16)

            def load_down(e, b):
                sp.dma_start(dn[b], w_down[expert1(e)].rearrange("e (p j) d -> (e p) j d", p=P)).then_inc(d_in[b], 16)

            load(0, 0), load_down(0, 0), load(1, 1), load_down(1, 1)
            with sp.Fori(2, E - 1, 2) as e:
                for b in range(2):
                    sp.wait_ge(au_mm, e + b - 1)
                    load(e + b, b)
                    sp.wait_ge(y_mm, e + b - 1)
                    load_down(e + b, b)


def overflow_stage(K, tag, m, w_gate, w_up, w_down):
    nc, E = K.nc, m.E
    s = lambda n: K.sem(f"{tag}_over_{n}")
    w_gate, w_up, w_down = w_gate[0], w_up[0], w_down[0]
    f = K.heads
    xg, xt, ys = f[:, 0:1024], f[:, 2048:3072], f[:, 4096:5120]
    silu, hid, hidt = f[:, 6144:6400], f[:, 6656:6912], f[:, 7168:7424]
    onehot = f[:, 7680:8192].rearrange("p (t s) -> p t s", t=T)
    idx, gate = K.small[:, 1024:1025].bitcast(I32), K.small[:, 1028:1029]
    gu = K.big[:, 0:4096].rearrange("p (g c f) -> p g c f", g=2, c=KC)
    dn = K.big[:, 8192:10240].rearrange("p (j d) -> p j d", j=FH)
    LISTS = range(1, T)
    NL = len(LISTS)
    listed, list_mm, idx_ready, xt_mm, xt_copied = s("onehot"), s("list_product"), s("list"), s("turned"), s("turned_copied")
    au_mm, silu_ready, hid_ready, ht_mm, ht_copied = s("gate_up"), s("silu"), s("hidden"), s("hid_turned"), s("hid_copied")
    y_mm, y_taken, gu_in, d_in = s("down"), s("y_taken"), s("gate_up_arrived"), s("down_arrived")
    gathered, scattered = K.over_sems[tag]
    row_dmas = s("row_dmas")
    experts_done = s("experts_done")
    one = lambda e: bass.ds(e, 1)

    def each(eng, body):
        most = eng.value_load(m.most[0:1, :], min_val=0, max_val=S)
        with eng.If(most > P):
            with eng.Fori(0, E, 1) as e:
                for k, b in enumerate(LISTS):
                    body(e, b, e * NL + k)

    with nc.Block() as block:
        @block.tensor
        def _(pe):
            def body(e, b, n):
                pe.wait_ge(listed, n + 1)
                for t in range(T):
                    mm = pe.matmul(K.bank[0][:, 0:2], onehot[:, t, :], m.table[:, t, one(e), :], start=t == 0,
                                   stop=t == T - 1)
                mm.then_inc(list_mm, 1)
                pe.wait_ge(gathered, 16 * n + 16)
                for half in range(2):
                    for k in range(4):
                        mm = pe.transpose(K.bank[1 + half][:, P * k:P * k + P], xg[:, 4 * half + k::KC], K.ident[:, :])
                    mm.then_inc(xt_mm, 1)
                pe.wait_ge(xt_copied, 2 * n + 2)
                pe.wait_ge(gu_in, 32 * e + 32)
                for c in range(KC):
                    mm = pe.matmul(K.bank[3][:, :], xt[:, P * c:P * c + P], gu[:, :, c, :], start=c == 0, stop=c == KC - 1)
                mm.then_inc(au_mm, 1)
                pe.wait_ge(hid_ready, n + 1)
                for j in range(FH):
                    mm = pe.transpose(K.bank[5][:, P * j:P * j + P], hid[:, j::FH], K.ident[:, :])
                mm.then_inc(ht_mm, 1)
                pe.wait_ge(ht_copied, n + 1)
                pe.wait_ge(d_in, 16 * e + 16)
                for half in range(2):
                    for j in range(FH):
                        mm = pe.matmul(K.bank[6 + half][:, :], hidt[:, P * j:P * j + P],
                                       dn[:, j, 512 * half:512 * half + 512], start=j == 0, stop=j == FH - 1)
                mm.then_inc(y_mm, 1)
            each(pe, body)

        @block.scalar
        def _(act):
            def body(e, b, n):
                for half in range(2):
                    act.wait_ge(xt_mm, 2 * n + 1 + half)
                    act.activation(xt[:, 512 * half:512 * half + 512], K.bank[1 + half][:, :], ACT.Copy)\
                       .then_inc(xt_copied, 1)
                act.wait_ge(au_mm, n + 1)
                act.activation(silu, K.bank[3][:, 0:FE], ACT.Silu).then_inc(silu_ready, 1)
                act.wait_ge(ht_mm, n + 1)
                act.activation(hidt, K.bank[5][:, 0:FE], ACT.Copy).then_inc(ht_copied, 1)
                act.wait_ge(y_mm, n + 1)
                for half in range(2):
                    act.activation(ys[:, 512 * half:512 * half + 512], K.bank[6 + half][:, :], ACT.Copy)\
                       .then_inc(y_taken, 1)
            each(act, body)

        @block.vector
        def _(dve):
            def body(e, b, n):
                dve.scalar_tensor_tensor(out=onehot, in0=K.iota[:, :].unsqueeze(1).broadcast_to([P, T, P]),
                                         scalar=float(P * b), in1=m.rank[:, :, one(e)].broadcast_to([P, T, P]),
                                         op0=ALU.add, op1=ALU.is_equal).then_inc(listed, 1)
                dve.wait_ge(list_mm, n + 1)
                dve.tensor_scalar(idx, K.bank[0][:, 0:1], float(NO_TOKEN), None, ALU.add).then_inc(idx_ready, 1)
                dve.tensor_copy(gate, K.bank[0][:, 1:2]).then_inc(idx_ready, 1)
                dve.wait_ge(idx_ready, 2 * n + 2)
                dve.wait_ge(silu_ready, n + 1)
                dve.scalar_tensor_tensor(out=hid, in0=silu, scalar=gate, in1=K.bank[3][:, FE:2 * FE], op0=ALU.mult,
                                         op1=ALU.mult).then_inc(hid_ready, 1)
                dve.wait_ge(hid_ready, n + 1)
                dve.wait_ge(scattered, 16 * n + 16)
            each(dve, body)

        @block.gpsimd
        def _(pool):
            def body(e, b, n):
                pool.wait_ge(idx_ready, 2 * n + 2)
                pool.sem_inc(row_dmas, 1)
                pool.indirect_dma_start(out=xg, out_offset=None, in_=K.h_dram,
                                        in_offset=bass.IndirectOffsetOnAxis(idx, 0), bounds_check=S - 1,
                                        oob_is_err=False).then_inc(gathered, 16)
                pool.wait_ge(y_taken, 2 * n + 2)
                pool.sem_inc(row_dmas, 1)
                scatter_add(K, pool, ys, idx).then_inc(scattered, 16)
                pool.wait_ge(scattered, 16 * n + 16)
            each(pool, body)

        @block.sync
        def _(sp):
            most = sp.value_load(m.most[0:1, :], min_val=0, max_val=S)
            with sp.If(most > P):
                with sp.Fori(0, E, 1) as e:
                    for g, w in enumerate((w_gate, w_up)):
                        sp.dma_start(gu[:, g, :, :], w[one(e)].rearrange("e (p c) f -> (e p) c f", p=P)).then_inc(gu_in, 16)
                    sp.dma_start(dn, w_down[one(e)].rearrange("e (p j) d -> (e p) j d", p=P)).then_inc(d_in, 16)
                    sp.wait_ge(y_mm, NL * e + NL)
                    sp.sem_inc(experts_done, 1)


def scatter_add(K, pool, rows, at):
    return pool.indirect_dma_start(out=K.acc_dram, out_offset=bass.IndirectOffsetOnAxis(at, 0), in_=rows, in_offset=None,
                                   bounds_check=S - 1, oob_is_err=False, compute_op=ALU.add)


def first_experts(K):
    m = moe_buffers(K, 32)
    K.m1 = m
    rank_tokens(K, "rank1", m, 36, hier_router(K, m))
    I = K.I
    acc_set, acc_back = K.sem("acc1_set"), K.sem("acc1_back")
    with K.nc.Block(no_gpsimd_drain=True) as block:
        @block.sync
        def _(sp):
            sp.dma_start(K.acc_dram.rearrange("(t p) d -> p t d", p=P), K.x).then_inc(acc_set, 16)
            sp.wait_ge(acc_set, 16)
    experts_stage(K, "moe1", m, I["w_exp_gate"], I["w_exp_up"], I["w_exp_down"], [(acc_set, 16)])
    overflow_stage(K, "moe1", m, I["w_exp_gate"], I["w_exp_up"], I["w_exp_down"])
    with K.nc.Block(no_gpsimd_drain=True) as block:
        @block.sync
        def _(sp):
            sp.dma_start(K.x, K.acc_dram.rearrange("(t p) d -> p t d", p=P)).then_inc(acc_back, 16)
            sp.wait_ge(acc_back, 16)



def modulated_norm(K, tag, gain, shift_at, scale_at, store):
    nc = K.nc
    arrived, ready = K.sem(f"{tag}_vectors_arrived"), K.sem(f"{tag}_gain_ready")
    scale = K.scr[:, 2048:2048 + D]
    with nc.Block(no_gpsimd_drain=True) as block:
        @block.sync
        def _(sp):
            sp.dma_start(K.gain[:, :], bcast(gain, P)).then_inc(arrived, 16)
            sp.dma_start(scale, bcast(K.mod_dram[scale_at:scale_at + D], P)).then_inc(arrived, 16)
            sp.dma_start(K.shift[:, :], bcast(K.mod_dram[shift_at:shift_at + D], P)).then_inc(arrived, 16)

        @block.vector
        def _(dve):
            dve.wait_ge(arrived, 48)
            dve.scalar_tensor_tensor(out=K.gain[:, :], in0=scale, scalar=1.0, in1=K.gain[:, :], op0=ALU.add,
                                     op1=ALU.mult).then_inc(ready, 1)
            dve.wait_ge(ready, 1)
    norm_columns(K, tag, shift=True, store=store)


def latents(K):
    nc, I = K.nc, K.I
    s = K.sem
    vec_in, taken, squares, sums, std, normed = (s(f"lat_{n}") for n in
                                                 ("vectors_arrived", "taken", "squares", "sums", "std", "normed"))
    gate_in, gate_mid, logf_ready, sin_in, sin_out, turned = (s(f"lat_{n}") for n in (
        "abs_ready", "log_ready", "logf_ready", "angles_ready", "sines_ready", "turned_copied"))
    small = K.small
    K.lat = K.scr[:, 0:1696].rearrange("p (t n) -> p t n", t=T)
    sq = K.scr[:, 1696:3232].rearrange("p (t n) -> p t n", t=T)
    K.qlT = K.heads[:, 0:1024].rearrange("p (c s) -> p c s", c=2)
    K.kvT = K.heads[:, 1024:1536]
    gq, gkv = small[:, 0:256], small[:, 256:384]
    b_forget = small[:, 384:392]
    ss, sd, rs = (small[:, a:a + 8].rearrange("p (n t) -> p n t", n=2) for a in (392, 400, 408))
    fl, ftmp = (small[:, a:a + 32].rearrange("p (t h) -> p t h", t=T) for a in (416, 448))
    K.forget = small[:, 480:512].rearrange("p (t h) -> p t h", t=T)
    pos_i, pos = small[:, 512:516].bitcast(I32), small[:, 516:520]
    freq = small[:, 520:536]
    ang, turns, r = (small[:, a:a + 64] for a in (704, 768, 832))
    by_t = lambda a: a.rearrange("p (t j) -> p t j", t=T)
    K.sin, K.cos = by_t(small[:, 896:960]), by_t(small[:, 960:1024])
    K.k_pe = small[:, 1024:1152].rearrange("p (t n) -> p t n", t=T)
    rot = [by_t(small[:, 1152 + 64 * n:1216 + 64 * n]) for n in range(2)]
    at = []
    with nc.Block(no_gpsimd_drain=True) as block:
        @block.tensor
        def _(pe):
            w = chunked(take_job(K, pe), KC, 424)
            for t in range(T):
                for c in range(KC):
                    mm = pe.matmul(K.bank[t][:, 0:424], K.ht[:, c, P * t:P * t + P], w[:, c, :], start=c == 0,
                                   stop=c == KC - 1)
                at.append(product(K, mm))
            end_job(K)
            pe.wait_ge(logf_ready, 1)
            for t in range(T):
                for before in range(t + 1):
                    mm = pe.matmul(K.bank[4][:, 8 * t:8 * t + 8], (K.tri_incl if before == t else K.ones)[:, :],
                                   fl[:, before, :], start=before == 0, stop=before == t)
            at.append(product(K, mm))
            pe.wait_ge(normed, 1)
            for n in range(3):
                for t in range(T):
                    src = K.lat[:, t, n:256:2] if n < 2 else K.lat[:, t, 256:384]
                    mm = pe.transpose(K.bank[5 + n][:, P * t:P * t + P], src, K.ident[:, :])
                at.append(product(K, mm))

        @block.scalar
        def _(act):
            step = K.act.on(act)
            for t in range(T):
                act.wait_ge(K.products, at[t])
                act.activation(K.lat[:, t, :], K.bank[t][:, 0:424], ACT.Copy).then_inc(taken, 1)
            act.wait_ge(taken, T)
            act.activation(sq, K.lat[:, :, 0:384], ACT.Square).then_inc(squares, 1)
            act.wait_ge(gate_in, 1)
            step(act.activation(ftmp, fl, ACT.Abs))
            step(act.activation(ftmp, ftmp, ACT.Exp, scale=-1.0))
            act.activation(ftmp, ftmp, ACT.Ln, bias=K.ones[:, 0:1]).then_inc(gate_mid, 1)
            act.wait_ge(sums, 2)
            act.activation(sd[:, 0, :], ss[:, 0, :], ACT.Sqrt, scale=1.0 / 256, bias=K.eps[:, 0:1]).then_inc(std, 1)
            act.activation(sd[:, 1, :], ss[:, 1, :], ACT.Sqrt, scale=1.0 / 128, bias=K.eps[:, 0:1]).then_inc(std, 1)
            act.wait_ge(sin_in, 1)
            act.activation(K.sin, by_t(r), ACT.Sin).then_inc(sin_out, 1)
            step(act.activation(turns, r, ACT.Abs))
            act.activation(K.cos, by_t(turns), ACT.Sin, scale=-1.0, bias=K.half_pi[:, 0:1]).then_inc(sin_out, 1)
            for n in range(3):
                act.wait_ge(K.products, at[5 + n])
                act.activation(K.qlT[:, n, :] if n < 2 else K.kvT, K.bank[5 + n][:, :], ACT.Copy).then_inc(turned, 1)
            act.wait_ge(turned, 3)

        @block.vector
        def _(dve):
            step = K.dve.on(dve)
            step(dve.memset(K.half_pi[:, :], TWO_PI / 4))
            dve.wait_ge(vec_in, 16 * 5)
            step(dve.tensor_copy(pos, pos_i))
            step(dve.tensor_tensor(by_t(ang), pos.unsqueeze(2).broadcast_to([P, T, 16]),
                                   freq.unsqueeze(1).broadcast_to([P, T, 16]), ALU.mult))
            step(dve.tensor_scalar(turns, ang, 1.0 / TWO_PI, None, ALU.mult))
            step(dve.tensor_scalar(turns, turns, ROUNDER, None, ALU.add))
            step(dve.tensor_scalar(turns, turns, -ROUNDER, None, ALU.add))
            step(dve.scalar_tensor_tensor(out=r, in0=turns, scalar=-PI_PARTS[0], in1=ang, op0=ALU.mult, op1=ALU.add))
            step(dve.scalar_tensor_tensor(out=r, in0=turns, scalar=-PI_PARTS[1], in1=r, op0=ALU.mult, op1=ALU.add))
            step(dve.scalar_tensor_tensor(out=r, in0=turns, scalar=-PI_PARTS[2], in1=r, op0=ALU.mult, op1=ALU.add))
            dve.tensor_scalar(r, r, -3.1415925, 3.1415925, ALU.max, ALU.min).then_inc(sin_in, 1)
            dve.wait_ge(taken, T)
            dve.tensor_tensor(fl, K.lat[:, :, 416:424], b_forget.unsqueeze(1).broadcast_to([P, T, 8]),
                              ALU.add).then_inc(gate_in, 1)
            dve.wait_ge(squares, 1)
            dve.tensor_reduce(ss[:, 0, :], sq[:, :, 0:256], AX.X, ALU.add).then_inc(sums, 1)
            dve.tensor_reduce(ss[:, 1, :], sq[:, :, 256:384], AX.X, ALU.add).then_inc(sums, 1)
            dve.wait_ge(gate_mid, 1)
            dve.scalar_tensor_tensor(out=fl, in0=fl, scalar=0.0, in1=ftmp, op0=ALU.min,
                                     op1=ALU.subtract).then_inc(logf_ready, 1)
            dve.wait_ge(std, 2)
            step(dve.reciprocal(small[:, 408:416], small[:, 400:408]))
            for t in range(T):
                step(dve.scalar_tensor_tensor(out=K.lat[:, t, 0:256], in0=K.lat[:, t, 0:256], scalar=rs[:, 0, t:t + 1],
                                              in1=gq, op0=ALU.mult, op1=ALU.mult))
                ins = dve.scalar_tensor_tensor(out=K.lat[:, t, 256:384], in0=K.lat[:, t, 256:384],
                                               scalar=rs[:, 1, t:t + 1], in1=gkv, op0=ALU.mult, op1=ALU.mult)
                if t < T - 1:
                    step(ins)
            ins.then_inc(normed, 1)
            dve.wait_ge(K.products, at[4])
            step(dve.tensor_copy(K.forget, K.bank[4][:, 0:32].rearrange("p (t h) -> p t h", t=T)))
            dve.wait_ge(sin_out, 2)
            rotate(step, dve, K.lat[:, :, 384:400], K.lat[:, :, 400:416], K.cos, K.sin,
                   K.k_pe[:, :, 0:16], K.k_pe[:, :, 16:32], rot)

        @block.sync
        def _(sp):
            load_jobs(K, sp, 1)
            sp.dma_start(gq, bcast(I["g_q_lat_2"][0], P)).then_inc(vec_in, 16)
            sp.dma_start(gkv, bcast(I["g_kv_lat_2"][0], P)).then_inc(vec_in, 16)
            sp.dma_start(b_forget, bcast(I["b_forget_2"][0], P)).then_inc(vec_in, 16)
            sp.dma_start(freq, bcast(I["inv_freq"], P)).then_inc(vec_in, 16)
            sp.dma_start(pos_i, I["positions_2"][0].rearrange("(t p) -> p t", p=P),
                         allow_slow_non_contiguous=True).then_inc(vec_in, 16)
            load_jobs(K, sp, 1)


PI_PARTS = (6.28125, 0.0019352436065673828, 6.357301884918343e-08)


def rotate(step, dve, x1, x2, cos, sin, out1, out2, tmp):
    step(dve.tensor_tensor(tmp[0], x2, sin, ALU.mult))
    step(dve.tensor_tensor(tmp[1], x1, sin, ALU.mult))
    step(dve.tensor_tensor(out1, x1, cos, ALU.mult))
    step(dve.tensor_tensor(out1, out1, tmp[0], ALU.subtract))
    step(dve.tensor_tensor(out2, x2, cos, ALU.mult))
    step(dve.tensor_tensor(out2, out2, tmp[1], ALU.add))


def latent_heads(K):
    nc = K.nc
    taken, rotated = K.sem("up_taken"), K.sem("up_rotated")
    DIM = 96
    q_rows = K.scr[:, 1696:4768].rearrange("p (t h d) -> p t h d", t=T, h=HEADS)
    k_rows = K.scr[:, 4768:7840].rearrange("p (t h d) -> p t h d", t=T, h=HEADS)
    K.head_rows = (q_rows, k_rows)
    tmp = [K.scr[:, 7840 + 512 * n:8352 + 512 * n].rearrange("p (t h d) -> p t h d", t=T, h=HEADS) for n in range(4)]
    at = []
    with nc.Block(no_gpsimd_drain=True) as block:
        @block.tensor
        def _(pe):
            w = chunked(take_job(K, pe), 2, 768)
            for u in range(8):
                t, half = divmod(u, 2)
                for c in range(2):
                    mm = pe.matmul(K.bank[u][:, 0:384], K.qlT[:, c, P * t:P * t + P], w[:, c, 384 * half:384 * half + 384],
                                   start=c == 0, stop=c == 1)
                at.append(product(K, mm))
            end_job(K)
            w = take_job(K, pe)
            for u in range(8):
                t, half = divmod(u, 2)
                pe.wait_ge(taken, u + 1)
                mm = pe.matmul(K.bank[u][:, :], K.kvT[:, P * t:P * t + P], w[:, 512 * half:512 * half + 512], start=True,
                               stop=True)
                at.append(product(K, mm))
            end_job(K)

        @block.scalar
        def _(act):
            for u in range(8):
                t, half = divmod(u, 2)
                act.wait_ge(K.products, at[u])
                act.activation(q_rows[:, t, 4 * half:4 * half + 4, :],
                               K.bank[u][:, 0:384].rearrange("p (h d) -> p h d", h=4), ACT.Copy,
                               scale=DIM ** -0.5).then_inc(taken, 1)
            for u in range(8):
                t, half = divmod(u, 2)
                act.wait_ge(K.products, at[8 + u])
                kv = K.bank[u][:, :].rearrange("p (h d) -> p h d", h=4)
                act.activation(k_rows[:, t, 4 * half:4 * half + 4, 0:64], kv[:, :, 0:64], ACT.Copy).then_inc(taken, 1)
                act.activation(K.v[:, t, 256 * half:256 * half + 256].rearrange("p (h d) -> p h d", h=4),
                               kv[:, :, 64:128], ACT.Copy).then_inc(taken, 1)
            act.wait_ge(taken, 24)

        @block.vector
        def _(dve):
            step = K.dve.on(dve)
            step(dve.tensor_copy(k_rows[:, :, :, 64:96], K.k_pe.unsqueeze(2).broadcast_to([P, T, HEADS, 32])))
            dve.wait_ge(taken, 8)
            cos, sin = (a.unsqueeze(2).broadcast_to([P, T, HEADS, 16]) for a in (K.cos, K.sin))
            rotate(step, dve, q_rows[:, :, :, 64:80], q_rows[:, :, :, 80:96], cos, sin, tmp[2], tmp[3], tmp)
            step(dve.tensor_copy(q_rows[:, :, :, 64:80], tmp[2]))
            step(dve.tensor_copy(q_rows[:, :, :, 80:96], tmp[3]))

        @block.sync
        def _(sp):
            load_jobs(K, sp, 2)


def heads_to_columns(K, tag, dim):
    nc = K.nc
    taken = (K.sem(f"{tag}_act_copied"), K.sem(f"{tag}_dve_copied"))
    at = []
    with nc.Block(no_gpsimd_drain=True) as block:
        @block.tensor
        def _(pe):
            for u in range(2 * HEADS):
                n, h = divmod(u, HEADS)
                if u >= 8:
                    pe.wait_ge(taken[u % 2], (u - 8) // 2 + 1)
                for t in range(T):
                    mm = pe.transpose(K.bank[u % 8][0:dim, P * t:P * t + P], K.head_rows[n][:, t, h, :], K.ident[:, :])
                at.append(product(K, mm))

        def copy_heads(eng, copy, which):
            for u in range(which, 2 * HEADS, 2):
                n, h = divmod(u, HEADS)
                eng.wait_ge(K.products, at[u])
                copy((K.qt, K.kt)[n][0:dim, h, :], K.bank[u % 8][0:dim, :]).then_inc(taken[which], 1)
            eng.wait_ge(taken[which], HEADS)

        @block.scalar
        def _(act):
            copy_heads(act, lambda o, i: act.activation(o, i, ACT.Copy), 0)

        @block.vector
        def _(dve):
            copy_heads(dve, dve.tensor_copy, 1)


def latent_attention(K):
    latent_heads(K)
    heads_to_columns(K, "mla_turn", 96)
    attention(K, "mla", 96, 0)


def fox_heads(K):
    nc = K.nc
    taken = K.sem("fox_taken")
    q_rows, k_rows = (K.scr[:, a:a + 2112].rearrange("p (t h d) -> p t h d", t=T, h=HEADS) for a in (0, 2112))
    K.head_rows = (q_rows, k_rows)
    at = []
    with nc.Block(no_gpsimd_drain=True) as block:
        @block.tensor
        def _(pe):
            for n in range(3):
                w = chunked(take_job(K, pe), KC, 512)
                for t in range(T):
                    u = T * n + t
                    if u >= 8:
                        pe.wait_ge(taken, u - 7)
                    for c in range(KC):
                        mm = pe.matmul(K.bank[u % 8][:, :], K.ht[:, c, P * t:P * t + P], w[:, c, :], start=c == 0,
                                       stop=c == KC - 1)
                    at.append(product(K, mm))
                end_job(K)

        @block.scalar
        def _(act):
            for u in range(3 * T):
                n, t = divmod(u, T)
                act.wait_ge(K.products, at[u])
                dest = K.v[:, t, :].rearrange("p (h d) -> p h d", h=HEADS) if n == 2 else K.head_rows[n][:, t, :, 0:64]
                act.activation(dest, K.bank[u % 8][:, :].rearrange("p (h d) -> p h d", h=HEADS), ACT.Copy,
                               scale=64 ** -0.5 if n == 0 else 1.0).then_inc(taken, 1)
            act.wait_ge(taken, 3 * T)

        @block.vector
        def _(dve):
            step = K.dve.on(dve)
            step(dve.tensor_copy(q_rows[:, :, :, 64], K.forget))
            step(dve.memset(q_rows[:, :, :, 65:66], 1.0))
            step(dve.memset(k_rows[:, :, :, 64:65], 1.0))
            step(dve.tensor_scalar(k_rows[:, :, :, 65], K.forget, -1.0, None, ALU.mult))

        @block.sync
        def _(sp):
            load_jobs(K, sp, 3)


def fox_attention(K):
    fox_heads(K)
    heads_to_columns(K, "fox_turn", 66)
    attention(K, "fox", 66, 512)


def merge(K):
    nc = K.nc
    s = K.sem
    turned = (s("mrg_act_copied"), s("mrg_dve_copied"))
    cols = K.heads[:, 0:4096].rearrange("p (n c s) -> p n c s", n=2, c=4)
    at = []
    with nc.Block(no_gpsimd_drain=True) as block:
        @block.tensor
        def _(pe):
            for u in range(8):
                n, c = divmod(u, 4)
                for t in range(T):
                    mm = pe.transpose(K.bank[u][:, P * t:P * t + P], K.hr[:, t, 512 * n + c:512 * n + 512:4], K.ident[:, :])
                at.append(product(K, mm))

        def copy(eng, ins, which):
            for u in range(which, 8, 2):
                n, c = divmod(u, 4)
                eng.wait_ge(K.products, at[u])
                ins(cols[:, n, c, :], K.bank[u][:, :]).then_inc(turned[which], 1)
            eng.wait_ge(turned[which], 4)

        @block.scalar
        def _(act):
            copy(act, lambda o, i: act.activation(o, i, ACT.Copy), 0)

        @block.vector
        def _(dve):
            copy(dve, dve.tensor_copy, 1)

        @block.sync
        def _(sp):
            load_jobs(K, sp, 1)

    sig, merged = s("mrg_sigmoids"), s("mrg_merged")
    gates = K.scr[:, 0:4096].rearrange("p (n t d) -> p n t d", n=2, t=T)
    base = K.n_products
    units = [(half, n, what, t) for half in range(2) for n in range(2) for what in range(2) for t in range(T)]
    with nc.Block(no_gpsimd_drain=True) as block:
        @block.tensor
        def _(pe):
            w_o = None
            for u, (half, n, what, t) in enumerate(units):
                if what == 0:
                    if t == 0:
                        w = chunked(take_job(K, pe), KC, 512)
                    if u >= 8:
                        pe.wait_ge(sig, (u - 8) // 8 * 4 + t + 1)
                    lhs, rhs, count = K.ht, w, KC
                else:
                    if t == 0 and n == 0:
                        w_o = chunked(take_job(K, pe), 4, 1024)
                    if u >= 8:
                        pe.wait_ge(merged, (u - 8) // 8 * 4 + t + 1)
                    lhs, rhs, count = cols[:, n, :, :], w_o[:, :, 512 * n:512 * n + 512], 4
                for c in range(count):
                    mm = pe.matmul(K.bank[u % 8][:, :], lhs[:, c, P * t:P * t + P], rhs[:, c, :], start=c == 0,
                                   stop=c == count - 1)
                product(K, mm)
                if t == T - 1 and (n, what) == (0, 0):
                    end_job(K)
                if t == T - 1 and (n, what) == (1, 1):
                    end_job(K)
                    end_job(K)

        @block.scalar
        def _(act):
            for u, (half, n, what, t) in enumerate(units):
                if what == 0:
                    act.wait_ge(K.products, base + u + 1)
                    if half == 1:
                        act.wait_ge(merged, 4 * n + t + 1)
                    act.activation(gates[:, n, t, :], K.bank[u % 8][:, :], ACT.Sigmoid).then_inc(sig, 1)

        @block.vector
        def _(dve):
            step = K.dve.on(dve)
            for u, (half, n, what, t) in enumerate(units):
                if what == 1:
                    dve.wait_ge(K.products, base + u + 1)
                    dve.wait_ge(sig, 8 * half + 4 * n + t + 1)
                    out = K.hr[:, t, 512 * half:512 * half + 512]
                    if n == 0:
                        dve.tensor_tensor(out, K.bank[u % 8][:, :], gates[:, n, t, :], ALU.mult).then_inc(merged, 1)
                    else:
                        step(dve.tensor_tensor(gates[:, n, t, :], K.bank[u % 8][:, :], gates[:, n, t, :], ALU.mult))
                        dve.wait_ge(merged, 8 * half + t + 1)
                        dve.tensor_tensor(out, out, gates[:, n, t, :], ALU.add).then_inc(merged, 1)
            dve.wait_ge(merged, 16)

        @block.sync
        def _(sp):
            load_jobs(K, sp, 6)
    turn_rows(K, "turn2")
    K.gate_in = K.sem("gate_m_arrived")
    add_rows_product(K, "out2", 2, gate=K.gain, gate_ready=(K.gate_in, 16),
                     vectors=[(K.gain[:, :], bcast(K.mod_dram[2 * D:3 * D], P), K.gate_in)])


def grouped_router(K, m):
    I, s = K.I, K.sem
    bias_in, scored = s("router2_bias_arrived"), s("router2_scores")
    G, EG = 8, 8
    W = T * G * EG
    by_group = lambda a: a.rearrange("p t (g e) -> p (t g) e", g=G)
    flat = K.keep.rearrange("p t s -> p (t s)")
    score = flat[:, 768:1024].rearrange("p (t e) -> p t e", t=T)
    choice, w1 = m.work, m.work2
    m1, m2, keep_g = (m.tiny[:, a:a + 32] for a in (0, 32, 64))
    den = m.tiny[:, 96:100]

    def sync(sp):
        sp.dma_start(m.bias, bcast(I["b_router_2"][0], P)).then_inc(bias_in, 16)

    def scalar(act):
        act.wait_ge(K.products, K.router_at)
        act.activation(score, K.bank[0][:, 0:256].rearrange("p (t e) -> p t e", t=T), ACT.Sigmoid).then_inc(scored, 1)

    def vector(dve, step, raw):
        dve.wait_ge(bias_in, 16)
        dve.wait_ge(scored, 1)
        over_e = lambda a: a.unsqueeze(2).broadcast_to([P, T * G, EG])
        step(dve.tensor_tensor(choice, score, m.bias.unsqueeze(1).broadcast_to([P, T, 64]), ALU.add))
        step(dve.tensor_reduce(m1, by_group(choice), AX.X, ALU.max))
        step(dve.tensor_tensor(by_group(w1), by_group(choice), over_e(m1), ALU.is_equal))
        step(dve.tensor_tensor(by_group(w1), by_group(w1), K.desc[:, :].unsqueeze(1).broadcast_to([P, T * G, EG]), ALU.mult))
        step(dve.tensor_reduce(m2, by_group(w1), AX.X, ALU.max))
        step(dve.tensor_tensor(by_group(w1), by_group(w1), over_e(m2), ALU.is_equal))
        step(dve.scalar_tensor_tensor(out=w1, in0=w1, scalar=MASKED, in1=choice, op0=ALU.mult, op1=ALU.add))
        step(dve.tensor_reduce(m2, by_group(w1), AX.X, ALU.max))
        step(dve.tensor_tensor(m1, m1, m2, ALU.add))
        step(dve.memset(m.padded[:, :, 0:4], SENTINEL))
        step(dve.tensor_copy(m.padded[:, :, 4:12], m1.rearrange("p (t g) -> p t g", t=T)))
        pick_top(step, dve, m, m.padded, G, 4)
        step(dve.tensor_scalar(keep_g.rearrange("p (t g) -> p t g", t=T), m.padded[:, :, 4:12], TAKEN, None, ALU.is_equal))
        step(dve.tensor_scalar(m2, keep_g, -MASKED, MASKED, ALU.mult, ALU.add))
        step(dve.tensor_tensor(by_group(choice), by_group(choice), over_e(keep_g), ALU.mult))
        step(dve.tensor_tensor(by_group(choice), by_group(choice), over_e(m2), ALU.add))
        step(dve.memset(m.padded[:, :, 0:2], SENTINEL))
        step(dve.tensor_copy(m.padded[:, :, 2:66], choice))
        pick_top(step, dve, m, m.padded, 64, 6)
        step(dve.tensor_scalar(m.chosen, m.padded[:, :, 2:66], TAKEN, None, ALU.is_equal))
        step(dve.tensor_tensor(m.gate, score, m.chosen, ALU.mult))
        step(dve.tensor_reduce(den, m.gate, AX.X, ALU.add))
        step(dve.reciprocal(den, den))
        step(dve.tensor_scalar(den, den, ROUTED_SCALE, None, ALU.mult))
        step(dve.tensor_tensor(m.gate, m.gate, den.unsqueeze(2).broadcast_to([P, T, 64]), ALU.mult))

    return sync, scalar, vector


def shared_expert(K):
    nc = K.nc
    s = K.sem
    silu_ready, hid_ready, turned, y_taken, stored = (s(f"shared_{n}") for n in ("silu", "hidden", "turned", "y", "stored"))
    K.acc_stored = stored
    silu = K.heads[:, 0:1024].rearrange("p (t f) -> p t f", t=T)
    hid = K.heads[:, 1024:2048].rearrange("p (t f) -> p t f", t=T)
    hidt = K.heads[:, 2048:3072].rearrange("p (j s) -> p j s", j=FH)
    base = K.n_products
    with nc.Block(no_gpsimd_drain=True) as block:
        @block.tensor
        def _(pe):
            w = chunked(take_job(K, pe), KC, 512)
            for t in range(T):
                for c in range(KC):
                    mm = pe.matmul(K.bank[t][:, :], K.ht[:, c, P * t:P * t + P], w[:, c, :], start=c == 0, stop=c == KC - 1)
                product(K, mm)
            end_job(K)
            pe.wait_ge(hid_ready, T)
            for j in range(FH):
                for t in range(T):
                    mm = pe.transpose(K.bank[4 + j][:, P * t:P * t + P], hid[:, t, j::FH], K.ident[:, :])
                product(K, mm)
            w = chunked(take_job(K, pe), FH, D)
            pe.wait_ge(turned, FH)
            for u in range(2 * T):
                t, half = divmod(u, 2)
                if u >= 4:
                    pe.wait_ge(y_taken, u - 3)
                for j in range(FH):
                    mm = pe.matmul(K.bank[u % 4][:, :], hidt[:, j, P * t:P * t + P], w[:, j, 512 * half:512 * half + 512],
                                   start=j == 0, stop=j == FH - 1)
                product(K, mm)
            end_job(K)

        @block.scalar
        def _(act):
            for t in range(T):
                act.wait_ge(K.products, base + t + 1)
                act.activation(silu[:, t, :], K.bank[t][:, 0:FE], ACT.Silu).then_inc(silu_ready, 1)
            for j in range(FH):
                act.wait_ge(K.products, base + T + j + 1)
                act.activation(hidt[:, j, :], K.bank[4 + j][:, :], ACT.Copy).then_inc(turned, 1)
            for u in range(2 * T):
                t, half = divmod(u, 2)
                act.wait_ge(K.products, base + T + FH + u + 1)
                act.activation(K.hr[:, t, 512 * half:512 * half + 512], K.bank[u % 4][:, :], ACT.Copy).then_inc(y_taken, 1)

        @block.vector
        def _(dve):
            for t in range(T):
                dve.wait_ge(silu_ready, t + 1)
                dve.tensor_tensor(hid[:, t, :], silu[:, t, :], K.bank[t][:, FE:2 * FE], ALU.mult).then_inc(hid_ready, 1)

        @block.sync
        def _(sp):
            sp.wait_ge(y_taken, 2 * T)
            sp.dma_start(K.acc_dram.rearrange("(t p) d -> p t d", p=P), K.hr).then_inc(stored, 16)
            sp.wait_ge(stored, 16)


def second_norm(K):
    modulated_norm(K, "norm3", K.I["g_mix_norm_2"][0], 0, D, store=False)


def second_experts(K):
    modulated_norm(K, "norm4", K.I["g_ffn_norm_2"][0], 3 * D, 4 * D, store=True)
    m = moe_buffers(K, 64)
    K.router_at = K.n_products + 1
    rank_tokens(K, "rank2", m, 64, grouped_router(K, m), jobs_ahead=1)
    shared_expert(K)
    I = K.I
    experts_stage(K, "moe2", m, I["w_exp_gate_2"], I["w_exp_up_2"], I["w_exp_down_2"], [(K.acc_stored, 16)])
    overflow_stage(K, "moe2", m, I["w_exp_gate_2"], I["w_exp_up_2"], I["w_exp_down_2"])


def final(K):
    nc = K.nc
    s = K.sem
    arrived, added, squares, std, ready, stored = (s(f"final_{n}") for n in (
        "arrived", "added", "squares", "std", "rows_ready", "stored"))
    ss, sd, rs = K.small[:, 0:4], K.small[:, 4:8], K.small[:, 8:12]
    with nc.Block(no_gpsimd_drain=True) as block:
        @block.scalar
        def _(act):
            for t in range(T):
                act.wait_ge(added, t + 1)
                act.activation(K.scr[:, 1024 * t:1024 * t + 1024], K.x[:, t, :], ACT.Square,
                               accum_out=ss[:, t:t + 1]).then_inc(squares, 1)
                act.wait_ge(squares, t + 1)
                act.activation(sd[:, t:t + 1], ss[:, t:t + 1], ACT.Sqrt, scale=1.0 / D, bias=K.eps[:, 0:1]).then_inc(std, 1)

        @block.vector
        def _(dve):
            step = K.dve.on(dve)
            dve.wait_ge(arrived, 48)
            for t in range(T):
                step(dve.tensor_tensor(K.hr[:, t, :], K.hr[:, t, :], K.gain[:, :], ALU.mult))
                dve.tensor_tensor(K.x[:, t, :], K.x[:, t, :], K.hr[:, t, :], ALU.add).then_inc(added, 1)
            for t in range(T):
                dve.wait_ge(std, t + 1)
                step(dve.reciprocal(rs[:, t:t + 1], sd[:, t:t + 1]))
                dve.scalar_tensor_tensor(out=K.hr[:, t, :], in0=K.x[:, t, :], scalar=rs[:, t:t + 1], in1=K.shift[:, :],
                                         op0=ALU.mult, op1=ALU.mult).then_inc(ready, 1)

        @block.sync
        def _(sp):
            sp.dma_start(K.gain[:, :], bcast(K.mod_dram[5 * D:6 * D], P)).then_inc(arrived, 16)
            sp.dma_start(K.shift[:, :], bcast(K.I["g_final_2"], P)).then_inc(arrived, 16)
            sp.dma_start(K.hr, K.acc_dram.rearrange("(t p) d -> p t d", p=P)).then_inc(arrived, 16)
            for t in range(T):
                sp.wait_ge(ready, t + 1)
                sp.dma_start(K.out[0, P * t:P * t + P, :], K.hr[:, t, :]).then_inc(stored, 16)
            sp.wait_ge(stored, 16 * T)


FIRST_BLOCK = [("setup", setup_and_modulation), ("norm1", first_norm), ("proj1", first_projection), ("gla", gla), ("qkn", qk_norm),
          ("attn1", first_attention), ("out1", first_output), ("moe1", first_experts)]
SECOND_BLOCK = [("norm3", second_norm), ("lat", latents), ("mla", latent_attention), ("fox", fox_attention), ("merge", merge),
          ("moe2", second_experts), ("final", final)]

_CONSTS = {"bucket_onehot": (N_BUCKETS, BIAS_COLS), "inv_freq": (16,)}
_INS = ["x", "norm1_g", "w_in", "q_norm_g", "k_norm_g", "rel_bias", "gla_gate_w2", "gla_gate_b", "gla_out_norm_g",
        "w_out", "norm2_g", "w_router_group", "b_router_group", "w_router_expert", "b_router_expert", "w_exp_gate",
        "w_exp_up", "w_exp_down", "c_2", "positions_2", "w_mod_2", "b_mod_2", "g_mix_norm_2", "w_in_2", "b_forget_2",
        "g_q_lat_2", "w_q_up_2", "g_kv_lat_2", "w_kv_up_2", "w_o_mla_2", "w_o_fox_2", "w_out_2", "g_ffn_norm_2",
        "w_router_2", "b_router_2", "w_exp_gate_2", "w_exp_up_2", "w_exp_down_2", "w_sh_gate_2", "w_sh_up_2",
        "w_sh_down_2", "g_final_2"]

_OUTS = [((1, S, D), "float32")]


def kernel(**inputs):
    import concourse.bacc as _bacc
    from concourse.bass_utils import run_bass_kernel_spmd as _run

    nc = _bacc.Bacc("TRN2", target_bir_lowering=False, num_devices=1)
    arrays, args = {}, []
    constants = shape_constants()
    for name in _INS + list(_CONSTS):
        a = np.ascontiguousarray(inputs[name] if name in inputs else constants[name])
        arrays[f"in_{name}_dram"] = a
        args.append(nc.dram_tensor(f"in_{name}_dram", a.shape, mybir.dt.from_np(a.dtype), kind="ExternalInput").ap())
    for i, (shape, dtype) in enumerate(_OUTS):
        args.append(nc.dram_tensor(f"out_{i}_dram", shape, mybir.dt.from_np(np.dtype(dtype)), kind="ExternalOutput").ap())
    build_program(nc, *args)
    r = _run(nc, [arrays], core_ids=[0])
    return r.results[0]["out_0_dram"]
```

```python
from contextlib import ExitStack

import numpy as np

import concourse.bass as bass
from concourse import mybir

F32 = mybir.dt.float32
I32 = mybir.dt.int32
BF16 = mybir.dt.bfloat16
F32R = mybir.dt.float32r
ALU = mybir.AluOpType
ACT = mybir.ActivationFunctionType
AX = mybir.AxisListType

P = 128
S = 512
T = S // P
D = 1024
KC = D // P
EPS = 1e-6
MASKED = -float(2 ** 100)
TAKEN = -float(2 ** 120)
SENTINEL = float(2 ** 100)
NO_TOKEN = 4096
WARM_UP = 4
HEADS = 8
FE = 256
FH = 2
ROUTED_SCALE = 2.5
N_BUCKETS = 32
BIAS_COLS = 640
TWO_PI = 6.283185307179586
ROUNDER = 1.5 * 2.0 ** 23


def shape_constants():
    dist = np.maximum(511 - np.arange(BIAS_COLS), 0)
    big = 16 + (np.log(np.maximum(dist, 1).astype(np.float32) / np.float32(16)) / np.float32(np.log(8.0)) * np.float32(16)).astype(np.int32)
    bucket = np.where(dist < 16, dist, np.minimum(big, N_BUCKETS - 1))
    onehot = (bucket[None, :] == np.arange(N_BUCKETS)[:, None]).astype(np.float32)
    inv_freq = np.power(np.float32(10000.0), -np.arange(16, dtype=np.float32) / np.float32(16)).astype(np.float32)
    return {"bucket_onehot": onehot, "inv_freq": inv_freq}


class Chain:

    def __init__(self, sem):
        self.sem, self.n, self.eng = sem, 0, None

    def on(self, eng):
        self.eng = eng
        return self

    def __call__(self, ins):
        self.n += 1
        ins.then_inc(self.sem, 1)
        self.eng.wait_ge(self.sem, self.n)
        return ins


class State:
    pass


def bcast(ap, n):
    return ap.partition_broadcast(n)


def build_program(nc, *args, stop_after=None):
    names = _INS + list(_CONSTS)
    I = dict(zip(names, args[:len(names)]))
    out = args[len(names)]
    with ExitStack() as ctx:
        K = State()
        K.nc, K.I, K.out = nc, I, out

        def sb(name, cols, dt=F32, parts=P):
            return ctx.enter_context(nc.sbuf_tensor(name, [parts, cols], dt))

        def sb_and_parts(name, cols):
            whole = sb(name, cols)
            at = nc.sbuf_base - 4 * cols
            return whole, nc.alloc_sbuf_tensor_at(f"{name}_parts", [P, cols], F32R, offset=at)

        def sem(name):
            return ctx.enter_context(nc.semaphore(name))

        def dram(name, shape):
            return nc.dram_tensor(name, shape, F32, kind="Internal").ap()

        K.sb, K.dram = sb, dram
        K.big, K.big_parts = sb_and_parts("big", 18432)
        K.x = sb("x_res", T * D)[:, :].rearrange("p (t d) -> p t d", t=T)
        K.hr = sb("h_rows", T * D)[:, :].rearrange("p (t d) -> p t d", t=T)
        ht, K.ht_parts = sb_and_parts("h_cols", T * D)
        K.ht = ht[:, :].rearrange("p (c s) -> p c s", c=KC)
        K.ht2 = K.ht.rearrange("p c s -> p (c s)")
        K.heads, K.heads_parts = sb_and_parts("heads", 10240)
        K.qt = K.heads[:, 0:4096].rearrange("p (h s) -> p h s", h=HEADS)
        K.kt = K.heads[:, 4096:8192].rearrange("p (h s) -> p h s", h=HEADS)
        K.v = K.heads[:, 8192:10240].rearrange("p (t d) -> p t d", t=T)
        K.keep = sb("keep_mask", T * S)[:, :].rearrange("p (t s) -> p t s", t=T)
        K.small = sb("small", 2048)
        K.gain = sb("gain", D)
        K.shift = sb("shift", D)
        K.ident = sb("ident", P)
        K.tri = sb("tri_strict", P)
        K.tri_incl = sb("tri_incl", P)
        K.ones = sb("ones", P)
        K.iota = sb("iota", P)
        K.causal = sb("causal", S)
        K.token_id = sb("token_id", T)
        K.desc = sb("desc", 8)
        K.eps = sb("eps", 1)
        K.half_pi = sb("half_pi", 1)
        K.bank = [ctx.enter_context(nc.psum_tensor(f"bank{i}", [P, 512], F32)) for i in range(8)]
        K.dve, K.act, K.pool = (Chain(sem(f"{n}_step")) for n in ("vector", "scalar", "pool"))
        K.slot = [K.big[:, 0:4096], K.big[:, 4096:8192]]
        K.scr = K.big[:, 8192:18432]
        K.w_in_slot = [sem("weights_in_slot0"), sem("weights_in_slot1")]
        K.products = sem("products_ready")
        K.row_sems = {tag: [sem(f"{tag}_{n}") for n in ("gathered_even", "gathered_odd", "scattered")]
                      for tag in ("moe1", "moe2")}
        K.over_sems = {tag: [sem(f"{tag}_over_{n}") for n in ("gathered", "scattered")] for tag in ("moe1", "moe2")}
        K.n_products = 0
        K.job_end = []
        K.jobs = []
        K.next_load = 0
        K.next_job = 0
        K.h_dram = dram("h_scratch", [S, D])
        K.acc_dram = dram("acc_scratch", [S, D])
        K.mod_dram = dram("mod_scratch", [6 * D])
        K.bias_dram = dram("bias_scratch", [P, HEADS, BIAS_COLS])
        list_jobs(K)
        K.fill_of = [16 * sum(len(job) for job in K.jobs[g % 2:g + 1:2]) for g in range(len(K.jobs))]

        for stages in (FIRST_BLOCK, SECOND_BLOCK):
            with ExitStack() as stage_ctx:
                used = []

                def stage_sem(name, ctx=stage_ctx, used=used):
                    handle = ctx.enter_context(nc.semaphore(name))
                    used.append(handle.num)
                    return handle

                K.sem = stage_sem
                for name, stage in stages:
                    stage(K)
                    if name == stop_after:
                        return
                if stages is FIRST_BLOCK:
                    assert sorted(used) == list(range(min(used), max(used) + 1)), sorted(used)
                    nc.all_engine_barrier(sems_to_clear=range(min(used), max(used) + 1))



def list_jobs(K):
    I = K.I

    def cols(name, c0, n, at, width):
        src = I[name][0].rearrange("(p c) n -> p c n", p=P)[:, :, c0:c0 + n]
        chunks = src.shape[1]
        return (lambda slot: slot[:, 0:chunks * width].rearrange("p (c n) -> p c n", c=chunks)[:, :, at:at + n], src)

    def job(*parts):
        K.jobs.append(parts)

    job(cols("w_in", 1536, 256, 0, 408), *[cols("w_in", 1792, 32, 256 + 32 * r, 408) for r in range(4)],
        cols("w_in", 2856, 16, 384, 408), cols("w_in", 1824, 8, 400, 408))
    for c0 in (0, 512, 1024, 1832, 2344, 2872):
        job(cols("w_in", c0, 512, 0, 512))
    for j in range(2):
        job(cols("w_out", 512 * j, 512, 0, 512))
    job(cols("w_router_group", 0, 4, 0, 36), cols("w_router_expert", 0, 32, 4, 36))
    job(cols("w_in_2", 0, 416, 0, 424), cols("w_in_2", 1952, 8, 416, 424))
    job(cols("w_q_up_2", 0, 768, 0, 768))
    job(cols("w_kv_up_2", 0, 1024, 0, 1024))
    for c0 in (416, 928, 1440):
        job(cols("w_in_2", c0, 512, 0, 512))
    for half in range(2):
        job(cols("w_in_2", 1960 + 512 * half, 512, 0, 512))
        job(cols("w_in_2", 2984 + 512 * half, 512, 0, 512))
        job(cols("w_o_mla_2", 512 * half, 512, 0, 1024), cols("w_o_fox_2", 512 * half, 512, 512, 1024))
    for j in range(2):
        job(cols("w_out_2", 512 * j, 512, 0, 512))
    job(cols("w_router_2", 0, 64, 0, 64))
    job(cols("w_sh_gate_2", 0, 256, 0, 512), cols("w_sh_up_2", 0, 256, 256, 512))
    job(cols("w_sh_down_2", 0, 1024, 0, 1024))


def load_jobs(K, sp, n):
    for _ in range(n):
        g = K.next_load
        if g >= 2:
            sp.wait_ge(K.products, K.job_end[g - 2])
        for place, src in K.jobs[g]:
            sp.dma_start(place(K.slot[g % 2]), src).then_inc(K.w_in_slot[g % 2], 16)
        K.next_load += 1


def take_job(K, pe):
    g = K.next_job
    K.next_job += 1
    pe.wait_ge(K.w_in_slot[g % 2], K.fill_of[g])
    return K.slot[g % 2]


def product(K, mm):
    mm.then_inc(K.products, 1)
    K.n_products += 1
    return K.n_products


def end_job(K):
    K.job_end.append(K.n_products)


def chunked(slot, chunks, width):
    return slot[:, 0:chunks * width].rearrange("p (c n) -> p c n", c=chunks)



def setup(K):
    nc, I = K.nc, K.I
    s = K.sem
    consts, c_in, gain_in = s("consts_ready"), s("c_arrived"), s("norm1_gain_arrived")
    x_in = [s(f"x_tile{t}_arrived") for t in range(T)]
    cond_ready = s("cond_ready")
    K.cond = K.small[:, 16:16 + KC]
    craw = K.small[:, 24:24 + KC]
    K.rel = K.scr[0:N_BUCKETS, 7168:7168 + HEADS]
    K.hot = K.scr[0:N_BUCKETS, 7200:7200 + BIAS_COLS]
    bias_rows = K.scr[0:HEADS, 7840:7840 + BIAS_COLS]
    bias_in, bias_sb, bias_out = s("bias_arrived"), s("bias_rows_ready"), s("bias_stored")
    K.x_in, K.gain1_in, K.bias_out = x_in, gain_in, bias_out
    with nc.Block(no_gpsimd_drain=True) as block:
        @block.tensor
        def _(pe):
            pe.wait_ge(bias_in, 32)
            pe.matmul(K.bank[2][0:HEADS, :], K.rel, K.hot[:, 0:512], start=True, stop=True)
            mm = pe.matmul(K.bank[3][0:HEADS, 0:128], K.rel, K.hot[:, 512:640], start=True, stop=True)
            product(K, mm)

        @block.sync
        def _(sp):
            sp.dma_start(craw, I["c_2"][0].rearrange("(p c) -> p c", p=P)).then_inc(c_in, 16)
            sp.dma_start(K.rel, I["rel_bias"]).then_inc(bias_in, 16)
            sp.dma_start(K.hot, I["bucket_onehot"]).then_inc(bias_in, 16)
            for t in range(T):
                sp.dma_start(K.x[:, t, :], I["x"][0, P * t:P * t + P, :]).then_inc(x_in[t], 16)
            sp.dma_start(K.gain[:, :], bcast(I["norm1_g"][0], P)).then_inc(gain_in, 16)
            load_jobs(K, sp, 2)

        @block.gpsimd
        def _(pool):
            for buf, value in ((K.ident, 0.0), (K.tri, 1.0), (K.tri_incl, 1.0), (K.ones, 1.0), (K.eps, EPS)):
                pool.memset(buf[:, :], value).then_inc(consts, 1)
            pool.memset(K.causal[:, :], 0.0).then_inc(consts, 1)
            pool.wait_ge(consts, 6)
            for buf, compare, fill, base, pattern, mult in (
                    (K.ident, ALU.not_equal, 1.0, 0, [[-1, P]], 1), (K.tri, ALU.is_gt, 0.0, 0, [[1, P]], -1),
                    (K.tri_incl, ALU.is_ge, 0.0, 0, [[1, P]], -1), (K.causal, ALU.is_ge, MASKED, S - P, [[-1, S]], 1)):
                pool.affine_select(out=buf[:, :], in_=buf[:, :], compare_op=compare, fill=fill, base=base,
                                   pattern=pattern, channel_multiplier=mult).then_inc(consts, 1)
            for buf, pattern, base, mult in ((K.iota, [[1, P]], 0, 0), (K.token_id, [[P, T]], -NO_TOKEN, 1),
                                             (K.desc, [[-1, 8]], 8, 0)):
                pool.iota(buf[:, :], pattern=pattern, base=base, channel_multiplier=mult,
                          allow_small_or_imprecise_dtypes=True).then_inc(consts, 1)
            pool.wait_ge(consts, 13)

        @block.scalar
        def _(act):
            act.wait_ge(c_in, 16)
            act.activation(K.cond, craw, ACT.Silu).then_inc(cond_ready, 1)
            act.wait_ge(bias_sb, 2)
            act.dma_start(K.bias_dram.rearrange("p h k -> h p k"),
                          bias_rows.unsqueeze(1).broadcast_to([HEADS, P, BIAS_COLS])).then_inc(bias_out, 16)
            act.wait_ge(cond_ready, 1)

        @block.vector
        def _(dve):
            dve.wait_ge(K.products, 1)
            dve.tensor_copy(bias_rows[:, 0:512], K.bank[2][0:HEADS, :]).then_inc(bias_sb, 1)
            dve.tensor_copy(bias_rows[:, 512:640], K.bank[3][0:HEADS, 0:128]).then_inc(bias_sb, 1)



def norm_columns(K, tag, modulation=None, store=False, gain_ready=None, x_ready=None,
                 x_from=None):
    nc = K.nc
    squares, std, normed = K.sem(f"{tag}_squares"), K.sem(f"{tag}_std"), K.sem(f"{tag}_rows_ready")
    taken, stored = K.sem(f"{tag}_columns_copied"), K.sem(f"{tag}_stored")
    if x_from is not None:
        x_ready = [K.sem(f"{tag}_x_tile{t}_arrived") for t in range(T)]
    ss, sd, rs = K.small[:, 0:4], K.small[:, 4:8], K.small[:, 8:12]
    junk = K.scr[:, 0:2048].rearrange("p (b d) -> p b d", b=2)
    base = K.n_products
    with nc.Block(no_gpsimd_drain=True) as block:
        @block.tensor
        def _(pe):
            for t in range(T):
                pe.wait_ge(normed, t + 1)
                for half in range(2):
                    u = 2 * t + half
                    if u >= 4:
                        pe.wait_ge(taken, u - 3)
                    for k in range(4):
                        mm = pe.transpose(K.bank[u % 4][:, P * k:P * k + P], K.hr[:, t, 4 * half + k::KC], K.ident[:, :])
                    product(K, mm)

        @block.scalar
        def _(act):
            for t in range(T):
                if x_ready:
                    act.wait_ge(x_ready[t], 16)
                if t >= 2:
                    act.wait_ge(squares, t - 1)
                act.activation(junk[:, t % 2, :], K.x[:, t, :], ACT.Square, accum_out=ss[:, t:t + 1]).then_inc(squares, 1)
                act.wait_ge(squares, t + 1)
                act.activation(sd[:, t:t + 1], ss[:, t:t + 1], ACT.Sqrt, scale=1.0 / D,
                               bias=K.eps[:, 0:1]).then_inc(std, 1)
            for u in range(2 * T):
                t, half = divmod(u, 2)
                act.wait_ge(K.products, base + u + 1)
                act.activation(K.ht[:, 4 * half:4 * half + 4, P * t:P * t + P],
                               K.bank[u % 4][:, :].rearrange("p (k s) -> p k s", k=4), ACT.Copy).then_inc(taken, 1)

        @block.vector
        def _(dve):
            step = K.dve.on(dve)
            if modulation:
                gain, scale, arrived = modulation
                if arrived:
                    dve.wait_ge(*arrived)
                step(dve.scalar_tensor_tensor(out=K.gain[:, :], in0=scale, scalar=1.0, in1=gain, op0=ALU.add,
                                              op1=ALU.mult))
            if gain_ready:
                dve.wait_ge(*gain_ready)
            for t in range(T):
                dve.wait_ge(std, t + 1)
                step(dve.reciprocal(rs[:, t:t + 1], sd[:, t:t + 1]))
                ins = dve.scalar_tensor_tensor(out=K.hr[:, t, :], in0=K.x[:, t, :], scalar=rs[:, t:t + 1],
                                               in1=K.gain[:, :], op0=ALU.mult, op1=ALU.mult)
                if modulation:
                    step(ins)
                    ins = dve.tensor_tensor(K.hr[:, t, :], K.hr[:, t, :], K.shift[:, :], ALU.add)
                ins.then_inc(normed, 1)

        @block.sync
        def _(sp):
            if x_from is not None:
                for t in range(T):
                    sp.dma_start(K.x[:, t, :], x_from[P * t:P * t + P, :]).then_inc(x_ready[t], 16)
            if store:
                for t in range(T):
                    sp.wait_ge(normed, t + 1)
                    sp.dma_start(K.h_dram[P * t:P * t + P, :], K.hr[:, t, :]).then_inc(stored, 16)
                sp.wait_ge(stored, 16 * T)


def first_norm(K):
    norm_columns(K, "norm1", gain_ready=(K.gain1_in, 16), x_ready=K.x_in)



def first_projection(K):
    nc, I = K.nc, K.I
    taken, scored, picked = K.sem("p1_taken"), K.sem("p1_scored"), K.sem("p1_picked")
    iqT = K.heads[:, 0:1024].rearrange("p (j s) -> p j s", j=2)
    ikT = K.heads[:, 1024:1536]
    relu = K.heads[:, 1536:3072].rearrange("p (b s) -> p b s", b=3)
    iw = K.small[:, 32:64].rearrange("p (t h) -> p t h", t=T)
    top8 = K.small[:, 64:72]
    K.glr = K.small[0:16, 1024:1536]
    K.q_rows = K.scr[:, 0:2048].rearrange("p (t d) -> p t d", t=T)
    K.k_rows = K.scr[:, 2048:4096].rearrange("p (t d) -> p t d", t=T)
    K.vb = K.scr[:, 4096:6144].rearrange("p (t d) -> p t d", t=T)
    K.rg = K.scr[:, 6144:8192].rearrange("p (t d) -> p t d", t=T)
    K.qb = K.scr[:, 8192:9216].rearrange("p (j s) -> p j s", j=2)
    K.kb = K.scr[:, 9216:10240].rearrange("p (j s) -> p j s", j=2)
    copies = []
    mod_in = (K.sem("mod_even_arrived"), K.sem("mod_odd_arrived"))
    mod_out = (K.sem("mod_even_stored"), K.sem("mod_odd_stored"))
    mod_sums = K.sem("mod_sums_ready")
    mod_w = [chunked(w, KC, MOD) for w in (K.heads[:, 3072:7168], K.hr.rearrange("p t d -> p (t d)"))]
    mod_acc = [K.heads[:, 7168 + MOD * b:7168 + MOD * b + MOD] for b in range(2)]
    mod_bias = [K.gain[0:1, MOD * b:MOD * b + MOD] for b in range(2)]
    mod_row = [K.shift[0:1, MOD * b:MOD * b + MOD] for b in range(2)]
    mod_at = []
    score_units = [(t, h) for t in range(1, T) for h in range(HEADS)]
    base = K.n_products

    with nc.Block(no_gpsimd_drain=True) as block:
        @block.tensor
        def _(pe):
            def unit(lhs_rhs, out_of, dest, func=ACT.Copy, scale=1.0, mod=None):
                u = len(copies)
                if u >= 8:
                    pe.wait_ge(taken, u - 7)
                bank = K.bank[u % 8]
                for c, (lhsT, rhs) in enumerate(lhs_rhs):
                    mm = pe.matmul(out_of(bank), lhsT, rhs, start=c == 0, stop=c == len(lhs_rhs) - 1)
                copies.append((dest, out_of(bank), func, scale, mod))
                return product(K, mm)

            def columns(w, c0, n, dest, func=ACT.Copy, scale=1.0):
                unit([(w[:, c, c0:c0 + n], K.ht[:, c, :]) for c in range(KC)], lambda b: b[0:n, :], dest, func, scale)

            def rows(w, dest, mod=False):
                for t in range(T):
                    unit([(K.ht[:, c, P * t:P * t + P], w[:, c, :]) for c in range(KC)], lambda b: b[:, :], dest[:, t, :])
                    if mod:
                        mod_sum()

            def mod_sum():
                j = len(mod_at)
                pe.wait_ge(mod_sums, j + 1)
                mod_at.append(unit([(K.ones[:, 0:1], mod_acc[j % 2])], lambda b: b[0:1, :], mod_row[j % 2], mod=j))

            w = chunked(take_job(K, pe), KC, 408)
            columns(w, 0, 128, iqT[:, 0, :], scale=32 ** -0.5)
            columns(w, 128, 128, iqT[:, 1, :], scale=32 ** -0.5)
            columns(w, 256, 128, ikT)
            columns(w, 384, 16, K.glr)
            for t in range(T):
                unit([(K.ht[:, c, P * t:P * t + P], w[:, c, 400:408]) for c in range(KC)], lambda b: b[:, 0:8],
                     iw[:, t, :], scale=8 ** -0.5)
            end_job(K)
            pe.wait_ge(taken, 3)
            for i, (t, h) in enumerate(score_units):
                g, n = 32 * (h % 4), P * (t + 1)
                unit([(iqT[g:g + 32, h // 4, P * t:P * t + P], ikT[g:g + 32, 0:n])], lambda b, n=n: b[:, 0:n],
                     relu[:, i % 3, 0:n], func=ACT.Relu)
            for dest in (K.q_rows, K.k_rows, K.v):
                rows(chunked(take_job(K, pe), KC, 512), dest, mod=dest is K.v)
                end_job(K)
            w = chunked(take_job(K, pe), KC, 512)
            for j in range(2):
                columns(w, 128 * j, 128, K.qb[:, j, :])
                mod_sum()
                columns(w, 256 + 128 * j, 128, K.kb[:, j, :])
                mod_sum()
            end_job(K)
            for dest in (K.vb, K.rg):
                rows(chunked(take_job(K, pe), KC, 512), dest, mod=dest is K.vb)
                end_job(K)

        first_score = 8

        @block.scalar
        def _(act):
            act.wait_ge(K.bias_out, 16)
            for u, (dest, src, func, scale, mod) in enumerate(copies):
                act.wait_ge(K.products, base + u + 1)
                i = u - first_score
                if 3 <= i < len(score_units):
                    act.wait_ge(scored, i - 2)
                if mod is not None and mod >= 2:
                    act.wait_ge(mod_out[mod % 2], 16 * (mod // 2))
                act.activation(dest, src, func, scale=scale).then_inc(taken, 1)
                if mod is not None:
                    act.wait_ge(taken, u + 1)
                    act.dma_start(K.mod_dram[MOD * mod:MOD * mod + MOD].unsqueeze(0), dest).then_inc(mod_out[mod % 2], 16)
            for b in range(2):
                act.wait_ge(mod_out[b], 16 * (MODS // 2))

        @block.vector
        def _(dve):
            step = K.dve.on(dve)
            step(dve.tensor_copy(K.keep[:, 0, 0:P], K.causal[:, S - P:S]))
            for i, (t, h) in enumerate(score_units):
                n = P * (t + 1)
                dve.wait_ge(taken, first_score + i + 1)
                if h == 0:
                    ins = dve.tensor_scalar(K.keep[:, t, 0:n], relu[:, i % 3, 0:n], iw[:, t, h:h + 1], None, ALU.mult)
                else:
                    dve.wait_ge(scored, i)
                    ins = dve.scalar_tensor_tensor(out=K.keep[:, t, 0:n], in0=relu[:, i % 3, 0:n],
                                                   scalar=iw[:, t, h:h + 1], in1=K.keep[:, t, 0:n], op0=ALU.mult,
                                                   op1=ALU.add)
                ins.then_inc(scored, 1)
            dve.wait_ge(scored, len(score_units))
            for t in range(1, T):
                n = P * (t + 1)
                score = K.keep[:, t, 0:n]
                step(dve.tensor_tensor(score[:, n - P:n], score[:, n - P:n], K.causal[:, S - P:S], ALU.add))
                for _ in range(TOPK // 8):
                    step(dve.max(top8, score))
                    step(dve.match_replace(score, top8, score, TAKEN))
                step(dve.tensor_scalar(score, score, TAKEN, MASKED, ALU.not_equal, ALU.mult))
            for j in range(MODS):
                w, acc = mod_w[j % 2], mod_acc[j % 2]
                dve.wait_ge(mod_in[j % 2], 32 * (j // 2 + 1))
                if j >= 2:
                    dve.wait_ge(K.products, mod_at[j - 2])
                step(dve.tensor_scalar(acc, w[:, 0, :], K.cond[:, 0:1], None, ALU.mult))
                for c in range(1, KC):
                    step(dve.scalar_tensor_tensor(out=acc, in0=w[:, c, :], scalar=K.cond[:, c:c + 1], in1=acc,
                                                  op0=ALU.mult, op1=ALU.add))
                dve.tensor_tensor(acc[0:1, :], acc[0:1, :], mod_bias[j % 2], ALU.add).then_inc(mod_sums, 1)

        @block.sync
        def _(sp):
            def load_mod(first, end):
                for j in range(first, end):
                    if j >= 2:
                        sp.wait_ge(mod_sums, j - 1)
                    sp.dma_start(mod_w[j % 2], I["w_mod_2"][0][:, MOD * j:MOD * j + MOD].rearrange(
                        "(p c) n -> p c n", p=P)).then_inc(mod_in[j % 2], 16)
                    sp.dma_start(mod_bias[j % 2], I["b_mod_2"][:, MOD * j:MOD * j + MOD]).then_inc(mod_in[j % 2], 16)
            load_jobs(K, sp, 1)
            load_mod(0, 2)
            load_jobs(K, sp, 2)
            load_mod(2, 6)
            load_jobs(K, sp, 1)
            load_mod(6, 9)
            load_jobs(K, sp, 1)
            load_mod(9, MODS)
            load_jobs(K, sp, 1)


TOPK = 128
MOD = 512
MODS = 6 * D // MOD



def gla(K):
    nc, I = K.nc, K.I
    C, NCH = 64, S // 64
    s = K.sem
    loaded = s("gla_weights_arrived")
    w2 = K.small[0:16, 1536:1792]
    gate_b = K.small[:, 72:74]
    gla_g = K.small[:, 80:208]
    el = K.small[:, 208:224].rearrange("p (j c) -> p j c", j=2)
    per_head = lambda a: a.rearrange("p (h s) -> p h s", h=4)
    qe, ke = per_head(K.ht2[0:C, 0:2048]), per_head(K.ht2[0:C, 2048:4096])
    qi, v_odd = per_head(K.slot[0][0:C, 0:2048]), per_head(K.slot[0][0:C, 2048:4096])
    el_head = K.small[0:C, 1792:1824].rearrange("p (c h) -> p c h", h=4)
    z, tmp, cum, e_up, e_down = (K.heads[:, 1024 * n:1024 * n + 1024].rearrange("p (j s) -> p j s", j=2)
                                 for n in range(5))
    kdr = K.heads[:, 5120:6144].rearrange("p (t d) -> p t d", t=T)
    kdr_odd = K.heads[0:C, 6144:7168].rearrange("p (t d) -> p t d", t=T)
    e_in, kd = z, tmp
    reset = K.gain[:, 0:512]
    masked = K.gain[0:C, 512:1024].rearrange("p (b h s) -> p b h s", b=2, h=4)
    state = K.shift[0:C, 0:1024].rearrange("p (b h v) -> p b h v", b=2, h=4)

    def of_chunk(even, odd, c):
        return (odd if c % 2 else even)[0:C, c // 2]

    both = lambda a: a.rearrange("p j (c s) -> p (j c) s", s=C)
    z_in, gate_in, decays, kd_ready = s("gla_z_ready"), s("gla_abs_ready"), s("gla_exponents"), s("gla_exps")
    ops_ready, kd_rows = s("gla_operands"), s("gla_kd_rows")
    masked_ready, outs_taken, state_ready = s("gla_masked"), s("gla_outs_taken"), s("gla_state")
    silu_ready, squares, std = s("gla_silu"), s("gla_squares"), s("gla_std")
    base = K.n_products

    with nc.Block(no_gpsimd_drain=True) as block:
        @block.tensor
        def _(pe):
            pe.wait_ge(loaded, 48)
            for j in range(2):
                product(K, pe.matmul(K.bank[j][:, :], w2[:, P * j:P * j + P], K.glr, start=True, stop=True))
            pe.wait_ge(ops_ready, 1)
            for j in range(2):
                for t in range(T):
                    mm = pe.transpose(K.bank[2 + j][:, P * t:P * t + P], kd[:, j, P * t:P * t + P], K.ident[:, :])
                product(K, mm)
            pe.wait_ge(kd_rows, 4)

            def scores(c):
                if c >= 2:
                    pe.wait_ge(masked_ready, c - 1)
                for h in range(4):
                    mm = pe.matmul(K.bank[c % 2][0:C, C * h:C * h + C], ke[:, h, C * c:C * c + C],
                                   qe[:, h, C * c:C * c + C], start=True, stop=True)
                product(K, mm)

            scores(0)
            for c in range(NCH):
                pb = C * (c % 2)
                keys, values = of_chunk(kdr, kdr_odd, c), of_chunk(K.vb, v_odd, c)
                if c + 1 < NCH:
                    scores(c + 1)
                if c >= 2:
                    pe.wait_ge(state_ready, c - 1)
                for h in range(4):
                    mm = pe.matmul(K.bank[4 + c % 2][0:C, P * h:P * h + P], keys[:, C * h:C * h + C],
                                   values[:, P * h:P * h + P], start=True, stop=True)
                product(K, mm)
                pe.wait_ge(masked_ready, c + 1)
                if c >= 1:
                    pe.wait_ge(state_ready, c)
                if c >= 2:
                    pe.wait_ge(outs_taken, c - 1)
                for h in range(4):
                    o = K.bank[6 + c % 2][pb:pb + C, P * h:P * h + P]
                    mm = pe.matmul(o, masked[:, c % 2, h, :], values[:, P * h:P * h + P], start=True, stop=c == 0)
                    if c > 0:
                        mm = pe.matmul(o, qi[:, h, C * c:C * c + C], state[:, (c - 1) % 2, h, :], start=False, stop=True)
                product(K, mm)

        def at_scores(c):
            return base + 5 + (3 * (c - 1) + 1 if c else 0)

        def at_state(c):
            return base + 5 + 3 * c + (2 if c + 1 < NCH else 1)

        @block.scalar
        def _(act):
            step = K.act.on(act)
            act.wait_ge(z_in, 2)
            step(act.activation(tmp, z, ACT.Abs))
            step(act.activation(tmp, tmp, ACT.Exp, scale=-1.0))
            act.activation(tmp, tmp, ACT.Ln, bias=K.ones[:, 0:1]).then_inc(gate_in, 1)
            act.wait_ge(decays, 1)
            act.activation(e_down, e_up, ACT.Exp, scale=-1.0).then_inc(kd_rows, 1)
            act.wait_ge(kd_rows, 1)
            act.activation(e_up, e_up, ACT.Exp)
            act.activation(e_in, cum, ACT.Exp)
            act.activation(kd, kd, ACT.Exp)
            act.activation(el, cum.rearrange("p j (c s) -> p j c s", s=C)[:, :, :, C - 1], ACT.Exp).then_inc(kd_ready, 1)
            act.activation(v_odd, K.vb[C:P, :, :], ACT.Copy).then_inc(kd_rows, 1)
            for j in range(2):
                act.wait_ge(K.products, base + 3 + j)
                both_chunks = K.bank[2 + j][:, :].rearrange("p (t d) -> p t d", t=T)
                act.activation(kdr[:, :, P * j:P * j + P], both_chunks, ACT.Copy)
                act.activation(kdr_odd[:, :, P * j:P * j + P], both_chunks[C:P], ACT.Copy).then_inc(kd_rows, 1)
            act.activation(K.rg, K.rg, ACT.Silu).then_inc(silu_ready, 1)
            for c in range(NCH):
                pb, t = C * (c % 2), c // 2
                act.wait_ge(K.products, at_state(c) + 1)
                act.activation(K.hr[pb:pb + C, t, 512:1024], K.bank[6 + c % 2][pb:pb + C, :], ACT.Copy).then_inc(outs_taken, 1)
            act.wait_ge(outs_taken, NCH)
            act.activation(K.heads[:, 0:2048].rearrange("p (t d) -> p t d", t=T), K.hr[:, :, 512:1024],
                           ACT.Square).then_inc(squares, 1)
            act.wait_ge(std, 1)
            act.activation(K.small[:, 240:256], K.small[:, 224:240], ACT.Sqrt, scale=1.0 / P,
                           bias=K.eps[:, 0:1]).then_inc(silu_ready, 1)

        @block.vector
        def _(dve):
            step = K.dve.on(dve)
            dve.wait_ge(loaded, 48)
            step(dve.memset(reset, 1.0))
            step(dve.memset(reset.rearrange("p (c s) -> p c s", s=C)[:, :, 0:1], 0.0))
            for j in range(2):
                dve.wait_ge(K.products, base + 1 + j)
                dve.tensor_scalar(z[:, j, :], K.bank[j][:, :], gate_b[:, j:j + 1], None, ALU.add).then_inc(z_in, 1)
            dve.wait_ge(gate_in, 1)
            step(dve.scalar_tensor_tensor(out=z, in0=z, scalar=0.0, in1=tmp, op0=ALU.min, op1=ALU.subtract))
            step(dve.tensor_scalar(z, z, 1.0 / 16.0, None, ALU.mult))
            for j in range(2):
                step(dve.tensor_tensor_scan(cum[:, j, :], reset, z[:, j, :], 0.0, ALU.mult, ALU.add))
            cb = both(cum)
            mid = cb[:, :, C // 2 - 1:C // 2].broadcast_to([P, 2 * NCH, C])
            end = cb[:, :, C - 1:C].broadcast_to([P, 2 * NCH, C])
            step(dve.tensor_tensor(both(e_up), cb, mid, ALU.subtract))
            step(dve.tensor_tensor(both(kd), end, cb, ALU.subtract))
            dve.tensor_scalar(e_up, e_up, -EXP_LIMIT, EXP_LIMIT, ALU.max, ALU.min).then_inc(decays, 1)
            dve.wait_ge(kd_ready, 1)
            for odd in range(2):
                half = slice(C * odd, C * odd + C)
                dve.scalar_tensor_tensor(out=qe[:, odd::2, :], in0=K.qb[half], scalar=C ** -0.5, in1=e_up[half],
                                         op0=ALU.mult, op1=ALU.mult)
                dve.scalar_tensor_tensor(out=qi[:, odd::2, :], in0=K.qb[half], scalar=C ** -0.5, in1=e_in[half],
                                         op0=ALU.mult, op1=ALU.mult)
                dve.tensor_tensor(ke[:, odd::2, :], K.kb[half], e_down[half], ALU.mult)
                dve.tensor_copy(el_head[:, :, odd::2], el[half].rearrange("p j c -> p c j"))
            dve.tensor_tensor(kd, K.kb, kd, ALU.mult).then_inc(ops_ready, 1)
            dve.wait_ge(ops_ready, 1)
            for c in range(NCH):
                dve.wait_ge(K.products, at_scores(c))
                if c >= 2:
                    dve.wait_ge(K.products, at_state(c - 2) + 1)
                dve.tensor_tensor(masked[:, c % 2, :, :],
                                  K.bank[c % 2][0:C, 0:256].rearrange("p (h s) -> p h s", h=4),
                                  K.tri_incl[0:C, 0:C].unsqueeze(1).broadcast_to([C, 4, C]),
                                  ALU.mult).then_inc(masked_ready, 1)
                dve.wait_ge(K.products, at_state(c))
                added = K.bank[4 + c % 2][0:C, :].rearrange("p (h v) -> p h v", h=4)
                if c == 0:
                    dve.tensor_copy(state[:, 0, :, :], added).then_inc(state_ready, 1)
                else:
                    if c >= 2:
                        dve.wait_ge(K.products, at_state(c - 1) + 1)
                    dve.wait_ge(state_ready, c)
                    step(dve.tensor_tensor(state[:, c % 2, :, :], state[:, (c - 1) % 2, :, :],
                                           el_head[:, c, :].unsqueeze(2).broadcast_to([C, 4, P]), ALU.mult))
                    dve.tensor_tensor(state[:, c % 2, :, :], state[:, c % 2, :, :], added,
                                      ALU.add).then_inc(state_ready, 1)
            dve.wait_ge(squares, 1)
            dve.tensor_reduce(K.small[:, 224:240], K.heads[:, 0:2048].rearrange("p (g v) -> p g v", v=P), AX.X,
                              ALU.add).then_inc(std, 1)
            dve.wait_ge(silu_ready, 2)
            step(dve.reciprocal(K.small[:, 224:240], K.small[:, 240:256]))
            for t in range(T):
                o = K.hr[:, t, 512:1024].rearrange("p (h v) -> p h v", h=4)
                r = K.small[:, 224 + 4 * t:228 + 4 * t].unsqueeze(2).broadcast_to([P, 4, P])
                step(dve.tensor_tensor(o, o, r, ALU.mult))
                step(dve.tensor_tensor(o, o, gla_g.unsqueeze(1).broadcast_to([P, 4, P]), ALU.mult))
                step(dve.tensor_tensor(o, o, K.rg[:, t, :].rearrange("p (h v) -> p h v", h=4), ALU.mult))

        @block.sync
        def _(sp):
            sp.dma_start(w2, I["gla_gate_w2"][0]).then_inc(loaded, 16)
            sp.dma_start(gate_b, I["gla_gate_b"][0].rearrange("(j p) -> p j", p=P),
                         allow_slow_non_contiguous=True).then_inc(loaded, 16)
            sp.dma_start(gla_g, bcast(I["gla_out_norm_g"][0], P)).then_inc(loaded, 16)


EXP_LIMIT = 80.0



def qk_norm(K):
    nc, I = K.nc, K.I
    s = K.sem
    loaded, squares, sums, std, normed = (s("qkn_gains"), s("qkn_squares"), s("qkn_sums"), s("qkn_std"), s("qkn_rows"))
    taken = (s("qkn_act_copied"), s("qkn_dve_copied"))
    K.bias_in = s("bias_matrix_arrived")
    gains = K.small[:, 256:384].rearrange("p (n d) -> p n d", n=2)
    ss, sd, rs = K.small[:, 384:448], K.small[:, 448:512], K.small[:, 512:576]
    sq = K.slot[0]
    rows = K.scr[:, 0:4096].rearrange("p (g d) -> p g d", d=64)
    at = []
    with nc.Block(no_gpsimd_drain=True) as block:
        @block.tensor
        def _(pe):
            for u in range(2 * HEADS):
                n, h = divmod(u, HEADS)
                pe.wait_ge(normed, n + 1)
                if u >= 8:
                    pe.wait_ge(taken[u % 2], (u - 8) // 2 + 1)
                src = (K.q_rows, K.k_rows)[n]
                for t in range(T):
                    mm = pe.transpose(K.bank[u % 8][0:64, P * t:P * t + P], src[:, t, 64 * h:64 * h + 64], K.ident[:, :])
                at.append(product(K, mm))

        def copy_heads(eng, copy, which):
            for u in range(which, 2 * HEADS, 2):
                n, h = divmod(u, HEADS)
                eng.wait_ge(K.products, at[u])
                copy((K.qt, K.kt)[n][0:64, h, :], K.bank[u % 8][0:64, :]).then_inc(taken[which], 1)

        @block.scalar
        def _(act):
            act.activation(sq, K.scr[:, 0:4096], ACT.Square).then_inc(squares, 1)
            act.wait_ge(sums, 1)
            act.activation(sd, ss, ACT.Sqrt, scale=1.0 / 64, bias=K.eps[:, 0:1]).then_inc(std, 1)
            copy_heads(act, lambda o, i: act.activation(o, i, ACT.Copy), 0)

        @block.vector
        def _(dve):
            step = K.dve.on(dve)
            dve.wait_ge(squares, 1)
            dve.tensor_reduce(ss, sq.rearrange("p (g d) -> p g d", d=64), AX.X, ALU.add).then_inc(sums, 1)
            dve.wait_ge(std, 1)
            step(dve.reciprocal(rs, sd))
            step(dve.tensor_scalar(rs[:, 0:32], rs[:, 0:32], 64 ** -0.5, None, ALU.mult))
            dve.wait_ge(loaded, 32)
            for n in range(2):
                part = rows[:, 32 * n:32 * n + 32, :]
                step(dve.tensor_tensor(part, part, rs[:, 32 * n:32 * n + 32].unsqueeze(2).broadcast_to([P, 32, 64]),
                                       ALU.mult))
                dve.tensor_tensor(part, part, gains[:, n, :].unsqueeze(1).broadcast_to([P, 32, 64]),
                                  ALU.mult).then_inc(normed, 1)
            copy_heads(dve, dve.tensor_copy, 1)

        @block.sync
        def _(sp):
            sp.dma_start(gains[:, 0, :], bcast(I["q_norm_g"][0], P)).then_inc(loaded, 16)
            sp.dma_start(gains[:, 1, :], bcast(I["k_norm_g"][0], P)).then_inc(loaded, 16)
            flat = bass.AP(K.bias_dram.tensor, P - 1, [[HEADS * BIAS_COLS - 1, P], [BIAS_COLS, HEADS], [1, S]])
            sp.dma_start(K.ht, flat).then_inc(K.bias_in, 16)


def attention(K, tag, dim, out_col, bias=None, keep=None):
    nc = K.nc
    s = K.sem
    maxed, expd, turned = s(f"{tag}_max_ready"), s(f"{tag}_probs_ready"), s(f"{tag}_turned_copied")
    scored, normed = s(f"{tag}_logits_read"), s(f"{tag}_out_normed")
    z = K.scr[:, 4096:5632].rearrange("p (b s) -> p b s", b=3)
    probs = K.scr[:, 5632:7680].rearrange("p (b s) -> p b s", b=4)
    turn = K.scr[:, 7680:9216].rearrange("p (b s) -> p b s", b=3)
    mx, neg, rsum, rinv = (K.small[:, 576 + 32 * n:608 + 32 * n] for n in range(4))
    units = [(h, t) for h in range(HEADS) for t in range(T)]
    N = len(units)
    at_s, at_t, at_o = [], [], []
    with nc.Block(no_gpsimd_drain=True) as block:
        @block.tensor
        def _(pe):
            for _ in range(WARM_UP):
                pe.matmul(K.bank[7][:, :], K.ident[:, :], K.causal[:, :], start=True, stop=True)
            for i in range(N + 5):
                if i < N:
                    h, t = units[i]
                    n = P * (t + 1)
                    if i >= 3:
                        pe.wait_ge(scored, i - 2)
                    at_s.append(product(K, pe.matmul(K.bank[i % 3][:, 0:n], K.qt[0:dim, h, P * t:P * t + P],
                                                     K.kt[0:dim, h, 0:n], start=True, stop=True)))
                if 3 <= i < N + 3:
                    u = i - 3
                    h, t = units[u]
                    pe.wait_ge(expd, u + 1)
                    if u >= 2:
                        pe.wait_ge(turned, u - 1)
                    for k in range(t + 1):
                        mm = pe.transpose(K.bank[3 + u % 2][:, P * k:P * k + P], probs[:, u % 4, P * k:P * k + P],
                                          K.ident[:, :])
                    at_t.append(product(K, mm))
                if i >= 5:
                    u = i - 5
                    h, t = units[u]
                    pe.wait_ge(turned, u + 1)
                    if u >= 2:
                        pe.wait_ge(normed, u - 1)
                    for k in range(t + 1):
                        mm = pe.matmul(K.bank[5 + u % 2][:, 0:64], turn[:, u % 3, P * k:P * k + P],
                                       K.v[:, k, 64 * h:64 * h + 64], start=k == 0, stop=k == t)
                    at_o.append(product(K, mm))

        @block.scalar
        def _(act):
            for i in range(N + 3):
                if i >= 3:
                    u = i - 3
                    n = P * (units[u][1] + 1)
                    act.wait_ge(K.products, at_t[u])
                    if u >= 3:
                        act.wait_ge(K.products, at_o[u - 3])
                    act.activation(turn[:, u % 3, 0:n], K.bank[3 + u % 2][:, 0:n], ACT.Copy).then_inc(turned, 1)
                if i < N:
                    n = P * (units[i][1] + 1)
                    act.wait_ge(maxed, i + 1)
                    if i >= 4:
                        act.wait_ge(K.products, at_t[i - 4])
                    act.activation(probs[:, i % 4, 0:n], z[:, i % 3, 0:n], ACT.Exp, bias=neg[:, i:i + 1],
                                   accum_out=rsum[:, i:i + 1]).then_inc(expd, 1)

        @block.vector
        def _(dve):
            step = K.dve.on(dve)
            if bias is not None:
                dve.wait_ge(K.bias_in, 16)
            for i in range(N + 5):
                if i < N:
                    h, t = units[i]
                    n = P * (t + 1)
                    dve.wait_ge(K.products, at_s[i])
                    if i >= 3:
                        dve.wait_ge(expd, i - 2)
                    zi, logits = z[:, i % 3, 0:n], K.bank[i % 3][:, 0:n]
                    if bias is not None:
                        step(dve.tensor_tensor(zi, logits, bias[:, h, S - n:S], ALU.add))
                        logits = zi
                    mask = K.causal[:, S - n:S] if keep is None else keep[:, t, 0:n]
                    dve.tensor_tensor_reduce(zi, logits, mask, 1.0, float(MASKED) * 2, ALU.add, ALU.max,
                                             mx[:, i:i + 1]).then_inc(scored, 1)
                    dve.wait_ge(scored, i + 1)
                    dve.tensor_scalar(neg[:, i:i + 1], mx[:, i:i + 1], -1.0, None, ALU.mult).then_inc(maxed, 1)
                if i >= 5:
                    u = i - 5
                    h, t = units[u]
                    dve.wait_ge(expd, u + 1)
                    step(dve.reciprocal(rinv[:, u:u + 1], rsum[:, u:u + 1]))
                    dve.wait_ge(K.products, at_o[u])
                    dve.tensor_scalar(K.hr[:, t, out_col + 64 * h:out_col + 64 * h + 64], K.bank[5 + u % 2][:, 0:64],
                                      rinv[:, u:u + 1], None, ALU.mult).then_inc(normed, 1)


def first_attention(K):
    attention(K, "attn1", 64, 0, bias=K.ht, keep=K.keep)



class SplitWeights:

    def __init__(self, K, tag, ring, groups):
        self.K, self.ring = K, ring
        self.high_ready, self.low_ready = K.sem(f"{tag}_weights_high"), K.sem(f"{tag}_weights_low")
        self.loaded, self.used = K.sem(f"{tag}_weights_loaded"), K.sem(f"{tag}_weights_used")
        self.first = [sum(groups[:g]) for g in range(len(groups))]
        self.groups = groups
        self.raw, self.low_part, self.need = {}, {}, {}
        self.n_used, self.released = 0, []

    def block(self, g, job, chunks, width, at=0):
        views = [chunked(a, chunks, width)[:, :, at:at + 512] for a in (
            self.K.slot[job % 2], self.K.big_parts[:, 4096 * (job % 2):4096 * (job % 2) + 4096])]
        self.raw[g], self.low_part[g] = ([v[:, c, :] for c in range(chunks)] for v in views)
        self.need[g] = (self.K.w_in_slot[job % 2], self.K.fill_of[job])

    def high(self, act, g, first=lambda c: None):
        act.wait_ge(*self.need[g])
        for c, raw in enumerate(self.raw[g]):
            k = self.first[g] + c
            first(c)
            if k >= 8:
                act.wait_ge(*self.released[k - 8])
            act.activation(self.ring[k % 8], raw, ACT.Copy).then_inc(self.high_ready, 1)

    def low(self, dve, g, first=lambda c: None):
        dve.wait_ge(*self.need[g])
        for c, raw in enumerate(self.raw[g]):
            k = self.first[g] + c
            first(c)
            dve.wait_ge(self.high_ready, k + 1)
            dve.tensor_tensor(self.low_part[g][c], raw, self.ring[k % 8].bitcast(F32), ALU.subtract).then_inc(self.low_ready, 1)

    def products(self, pe, g, lhs_high, lhs_low, banks, before=None, lhs_ready=None):
        K, n, at = self.K, self.groups[g], []
        for c in range(n):
            k = self.first[g] + c
            pe.wait_ge(self.low_ready, k + 1)
            if lhs_ready:
                pe.wait_ge(lhs_ready, c + 1)
            high, low = self.ring[k % 8], self.low_part[g][c]
            for t in range(T):
                if c == 0 and before:
                    before(t)
                a_high, a_low = (a[:, c, P * t:P * t + P] for a in (lhs_high, lhs_low))
                pe.matmul(banks[t][:, :], a_high, high, start=c == 0, stop=False)
                pe.matmul(banks[t][:, :], a_high, low, start=False, stop=False)
                mm = pe.matmul(banks[t][:, :], a_low, high, start=False, stop=c == n - 1)
                if c == n - 1:
                    at.append(product(K, mm))
            if c < n - 1:
                mm.then_inc(self.used, 1)
                self.n_used += 1
                self.released.append((self.used, self.n_used))
            else:
                self.released.append((K.products, at[-1]))
        return at


def split_columns(act, dve, sem, which, chunks, high, low):
    if act:
        for c in which:
            act.activation(high[:, c, :], chunks[:, c, :], ACT.Copy).then_inc(sem[0], 1)
    if dve:
        for c in which:
            dve.wait_ge(sem[0], c + 1)
            dve.tensor_tensor(low[:, c, :], chunks[:, c, :], high[:, c, :].bitcast(F32), ALU.subtract).then_inc(sem[1], 1)


def turn_rows(K, tag):
    nc = K.nc
    high_ready, low_ready = K.sem(f"{tag}_high"), K.sem(f"{tag}_low")
    at = []
    K.turned_high = K.heads_parts[:, 0:4096].rearrange("p (c s) -> p c s", c=KC)
    K.turned_low = K.ht_parts[:, :].rearrange("p (c s) -> p c s", c=KC)
    with nc.Block(no_gpsimd_drain=True) as block:
        @block.tensor
        def _(pe):
            for u in range(2 * T):
                t, half = divmod(u, 2)
                for k in range(4):
                    mm = pe.transpose(K.bank[u][:, P * k:P * k + P], K.hr[:, t, 4 * half + k::KC], K.ident[:, :])
                at.append(product(K, mm))

        def place(a, u):
            t, half = divmod(u, 2)
            return a[:, 4 * half:4 * half + 4, P * t:P * t + P]

        def source(u):
            return K.bank[u][:, :].rearrange("p (k s) -> p k s", k=4)

        @block.scalar
        def _(act):
            for u in range(2 * T):
                act.wait_ge(K.products, at[u])
                act.activation(place(K.turned_high, u), source(u), ACT.Copy).then_inc(high_ready, 1)

        @block.vector
        def _(dve):
            for u in range(2 * T):
                dve.wait_ge(high_ready, u + 1)
                dve.tensor_tensor(place(K.turned_low, u), source(u), place(K.turned_high, u).bitcast(F32),
                                  ALU.subtract).then_inc(low_ready, 1)
            dve.wait_ge(low_ready, 2 * T)


def add_rows_product(K, tag, jobs_ahead, gate=None, gate_ready=None, vectors=()):
    nc = K.nc
    added = K.sem(f"{tag}_added")
    weights = SplitWeights(K, tag, [K.heads_parts[:, 4096 + 512 * k:4608 + 512 * k] for k in range(8)], [KC, KC])
    for j in range(2):
        weights.block(j, K.next_job + j, KC, 512)
    at = []
    with nc.Block(no_gpsimd_drain=True) as block:
        @block.tensor
        def _(pe):
            for j in range(2):
                at.extend(weights.products(pe, j, K.turned_high, K.turned_low, K.bank[4 * j:4 * j + 4]))
                end_job(K)
            K.next_job += 2

        @block.scalar
        def _(act):
            for j in range(2):
                weights.high(act, j)

        @block.vector
        def _(dve):
            step = K.dve.on(dve)
            weights.low(dve, 0)
            weights.low(dve, 1)
            if gate is not None:
                dve.wait_ge(*gate_ready)
            for u in range(2 * T):
                j, t = divmod(u, T)
                x = K.x[:, t, 512 * j:512 * j + 512]
                dve.wait_ge(K.products, at[u])
                src = K.bank[u][:, :]
                if gate is not None:
                    step(dve.tensor_tensor(src, src, gate[:, 512 * j:512 * j + 512], ALU.mult))
                dve.tensor_tensor(x, x, src, ALU.add).then_inc(added, 1)
            dve.wait_ge(added, 2 * T)

        @block.sync
        def _(sp):
            for place, src, arrived in vectors:
                sp.dma_start(place, src).then_inc(arrived, 16)
            load_jobs(K, sp, jobs_ahead)


def first_output(K):
    turn_rows(K, "turn1")
    K.gain2_in = K.sem("norm2_gain_arrived")
    add_rows_product(K, "out1", 2, vectors=[(K.gain[:, :], bcast(K.I["norm2_g"][0], P), K.gain2_in)])
    norm_columns(K, "norm2", store=True, gain_ready=(K.gain2_in, 16))



def moe_buffers(K, experts):
    flat = K.keep.rearrange("p t s -> p (t s)")
    m = State()
    m.E = experts
    m.table = flat[:, 0:8 * experts].rearrange("p (t e w) -> p t e w", t=T, w=2)
    m.rank, m.gate, m.chosen, m.work, m.work2 = (
        flat[:, 512 + 256 * n:512 + 256 * n + 4 * experts].rearrange("p (t e) -> p t e", t=T) for n in range(5))
    m.parts = flat[:, 1280:1280 + 12 * experts].bitcast(BF16).rearrange("p (t e w) -> p t e w", t=T, w=6)
    m.rest = K.small[:, 1100:1100 + 4 * experts].rearrange("p (t e) -> p t e", t=T)
    m.padded = K.small[:, 0:288].rearrange("p (t e) -> p t e", t=T)
    m.top8 = K.small[:, 288:320].rearrange("p (t e) -> p t e", t=T)
    m.tiny = K.small[:, 320:640]
    m.bias = K.small[:, 640:704]
    m.most = K.small[:, 704:705].bitcast(I32)
    return m


def pick_top(step, dve, m, padded, n, top):
    for t in range(T):
        step(dve.max(m.top8[:, t, :], padded[:, t, 0:8 - top + n]))
        step(dve.match_replace(padded[:, t, 0:8 - top + n], m.top8[:, t, :], padded[:, t, 0:8 - top + n], TAKEN))


def hier_router(K, m):
    I, s = K.I, K.sem
    bias_in, exp_in, exp_out = s("router1_bias_arrived"), s("router1_exp_args"), s("router1_exps")
    logits, g_exp = m.tiny[:, 0:144].rearrange("p (t n) -> p t n", t=T), m.tiny[:, 144:160].rearrange("p (t n) -> p t n", t=T)
    picked_g, gsum = m.tiny[:, 160:176].rearrange("p (t n) -> p t n", t=T), m.tiny[:, 176:180]
    e_sel, e_exp = (m.tiny[:, a:a + 32].rearrange("p (t n) -> p t n", t=T) for a in (180, 212))
    picked_e, den = m.tiny[:, 244:276].rearrange("p (t n) -> p t n", t=T), m.tiny[:, 276:280]
    G, EG = 4, 8

    norm3_in = s("norm3_vectors_arrived")

    def sync(sp):
        sp.dma_start(m.bias[:, 0:4], bcast(I["b_router_group"][0], P)).then_inc(bias_in, 16)
        sp.dma_start(m.bias[:, 4:36], bcast(I["b_router_expert"][0], P)).then_inc(bias_in, 16)
        for place, src in ((K.gain[:, :], I["g_mix_norm_2"][0]), (K.hr[:, 0, :], K.mod_dram[D:2 * D]),
                           (K.shift[:, :], K.mod_dram[0:D])):
            sp.dma_start(place, bcast(src, P)).then_inc(norm3_in, 16)
        sp.wait_ge(norm3_in, 48)

    def scalar(act):
        act.wait_ge(exp_in, 1)
        act.activation(g_exp, g_exp, ACT.Exp).then_inc(exp_out, 1)
        act.wait_ge(exp_in, 2)
        act.activation(m.tiny[:, 212:244], m.tiny[:, 212:244], ACT.Exp).then_inc(exp_out, 1)

    def vector(dve, step, raw):
        dve.wait_ge(bias_in, 32)
        step(dve.tensor_tensor(logits, raw, m.bias[:, 0:36].unsqueeze(1).broadcast_to([P, T, 36]), ALU.add))
        step(dve.memset(m.padded[:, :, 0:7], SENTINEL))
        step(dve.tensor_copy(m.padded[:, :, 7:11], logits[:, :, 0:4]))
        pick_top(step, dve, m, m.padded, G, 1)
        step(dve.tensor_scalar(picked_g, m.padded[:, :, 7:11], TAKEN, None, ALU.is_equal))
        dve.tensor_tensor(g_exp, logits[:, :, 0:4], m.top8[:, :, 7:8].broadcast_to([P, T, G]),
                          ALU.subtract).then_inc(exp_in, 1)
        step(dve.tensor_tensor(m.work.rearrange("p t (e g) -> p (t e) g", g=G).rearrange("p (t e) g -> p t e g", t=T),
                               logits[:, :, 4:36].rearrange("p t (g e) -> p t e g", g=G),
                               picked_g.unsqueeze(2).broadcast_to([P, T, EG, G]), ALU.mult))
        step(dve.tensor_reduce(m.tiny[:, 180:212], m.work.rearrange("p t (e g) -> p t e g", g=G), AX.X, ALU.add))
        step(dve.memset(m.padded[:, :, 0:6], SENTINEL))
        step(dve.tensor_copy(m.padded[:, :, 6:14], e_sel))
        pick_top(step, dve, m, m.padded, EG, 2)
        step(dve.tensor_scalar(picked_e, m.padded[:, :, 6:14], TAKEN, None, ALU.is_equal))
        dve.tensor_tensor(e_exp, e_sel, m.top8[:, :, 6:7].broadcast_to([P, T, EG]), ALU.subtract).then_inc(exp_in, 1)
        dve.wait_ge(exp_out, 2)
        step(dve.tensor_tensor(e_exp, e_exp, picked_e, ALU.mult))
        step(dve.tensor_reduce(den, e_exp, AX.X, ALU.add))
        step(dve.tensor_reduce(gsum, g_exp, AX.X, ALU.add))
        step(dve.tensor_tensor(den, den, gsum, ALU.mult))
        step(dve.reciprocal(den, den))
        step(dve.tensor_tensor(e_exp, e_exp, den.unsqueeze(2).broadcast_to([P, T, EG]), ALU.mult))
        for dest, per_expert in ((m.gate, e_exp), (m.chosen, picked_e)):
            step(dve.tensor_tensor(dest.rearrange("p t (g e) -> p t g e", g=G),
                                   picked_g.unsqueeze(3).broadcast_to([P, T, G, EG]),
                                   per_expert.unsqueeze(2).broadcast_to([P, T, G, EG]), ALU.mult))

    return sync, scalar, vector


def rank_tokens(K, tag, m, width, router, jobs_ahead=0, shared=None):
    nc, E = K.nc, m.E
    s = K.sem
    chosen, tables, stored = s(f"{tag}_chosen"), s(f"{tag}_tables"), s(f"{tag}_acc_stored")
    sync, scalar, vector = router
    at = []
    with nc.Block(no_gpsimd_drain=True) as block:
        @block.tensor
        def _(pe):
            w = chunked(take_job(K, pe), KC, width)
            for t in range(T):
                for c in range(KC):
                    mm = pe.matmul(K.bank[0][:, width * t:width * t + width], K.ht[:, c, P * t:P * t + P], w[:, c, :],
                                   start=c == 0, stop=c == KC - 1)
            at.append(product(K, mm))
            end_job(K)
            if shared:
                shared.gate_up(pe)
            pe.wait_ge(chosen, 1)
            for t in range(T):
                for before in range(t + 1):
                    mm = pe.matmul(K.bank[1][:, E * t:E * t + E], (K.tri if before == t else K.ones)[:, :],
                                   m.chosen[:, before, :], start=before == 0, stop=before == t)
            for t in range(T):
                mm = pe.matmul(K.bank[2][:, 0:E], K.ones[:, :], m.chosen[:, t, :], start=t == 0, stop=t == T - 1)
            at.append(product(K, mm))
            if shared:
                shared.down(pe)

        @block.scalar
        def _(act):
            scalar(act)
            if shared:
                shared.scalar(act)

        @block.vector
        def _(dve):
            step = K.dve.on(dve)
            dve.wait_ge(K.products, at[0])
            vector(dve, step, K.bank[0][:, 0:T * width].rearrange("p (t n) -> p t n", t=T))
            step(dve.tensor_copy(m.table[:, :, :, 1], m.gate))
            dve.tensor_copy(m.table[:, :, :, 0], K.token_id[:, :].unsqueeze(2).broadcast_to([P, T, E])).then_inc(chosen, 1)
            for t in range(T):
                step(dve.memset(m.parts[:, t, :, 0], float(P * t - NO_TOKEN)))
            step(dve.tensor_scalar(m.parts[:, :, :, 1], K.token_id[:, 0:1].unsqueeze(2).broadcast_to([P, T, E]),
                                   float(NO_TOKEN), None, ALU.add))
            step(dve.tensor_copy(m.parts[:, :, :, 2], m.gate))
            step(dve.tensor_tensor(m.rest, m.gate, m.parts[:, :, :, 2], ALU.subtract))
            step(dve.tensor_copy(m.parts[:, :, :, 3], m.rest))
            step(dve.tensor_tensor(m.rest, m.rest, m.parts[:, :, :, 3], ALU.subtract))
            step(dve.tensor_copy(m.parts[:, :, :, 4], m.rest))
            dve.wait_ge(K.products, at[1])
            step(dve.scalar_tensor_tensor(out=m.rank, in0=K.bank[1][:, 0:T * E].rearrange("p (t e) -> p t e", t=T),
                                          scalar=1.0, in1=m.chosen, op0=ALU.add, op1=ALU.mult))
            dve.tensor_scalar(m.rank, m.rank, -1.0, None, ALU.add).then_inc(tables, 1)
            dve.tensor_reduce(m.tiny[:, 0:1], K.bank[2][:, 0:E], AX.X, ALU.max).then_inc(tables, 1)
            dve.wait_ge(tables, 2)
            step(dve.tensor_copy(m.most, m.tiny[:, 0:1]))
            if shared:
                shared.vector(dve)

        @block.sync
        def _(sp):
            sync(sp)
            load_jobs(K, sp, jobs_ahead)
            if shared:
                shared.sync(sp)



def experts_stage(K, tag, m, w_gate, w_up, w_down, init):
    nc, E = K.nc, m.E
    s = K.sem
    w_gate, w_up, w_down = w_gate[0], w_up[0], w_down[0]
    f = K.heads
    ring2 = lambda a, n: a.rearrange("p (b n) -> p b n", b=2)
    xg, xt, ys = (ring2(f[:, 2048 * n:2048 * n + 2048], 2) for n in range(3))
    silu, hid, hidt = (ring2(f[:, 6144 + 512 * n:6656 + 512 * n], 2) for n in range(3))
    onehot = f[:, 7680:8192].bitcast(BF16).rearrange("p (b t s) -> p b t s", b=2, t=T)
    idx = K.small[:, 1024:1032].bitcast(I32)
    gate = K.small[:, 1032:1040]
    gu = [K.big[:, 4096 * b:4096 * b + 4096].rearrange("p (g c f) -> p g c f", g=2, c=KC) for b in range(2)]
    dn = [K.big[:, 8192 + 2048 * q:8192 + 2048 * q + 2048].rearrange("p (j d) -> p j d", j=FH) for q in range(4)]
    b_list, b_xt, b_au, b_ht, b_y = K.bank[0], K.bank[1:3], K.bank[3:5], K.bank[5], K.bank[6:8]

    listed, list_mm, idx_ready = s(f"{tag}_onehot_ready"), s(f"{tag}_list_product"), s(f"{tag}_list_copied")
    *gathered, scattered = K.row_sems[tag]
    xt_mm, xt_copied = s(f"{tag}_rows_turned"), s(f"{tag}_rows_turned_copied")
    au_mm, silu_ready, hid_ready = s(f"{tag}_gate_up_product"), s(f"{tag}_silu_ready"), s(f"{tag}_hidden_ready")
    ht_mm, ht_copied = s(f"{tag}_hidden_turned"), s(f"{tag}_hidden_turned_copied")
    y_mm, y_dve, y_act = s(f"{tag}_down_product"), s(f"{tag}_y_dve_copied"), s(f"{tag}_y_act_copied")
    gu_in = [s(f"{tag}_gate_up_even"), s(f"{tag}_gate_up_odd")]
    d_in = [s(f"{tag}_down{q}_arrived") for q in range(4)]
    cleared = s(f"{tag}_rows_cleared")
    row_dmas = s(f"{tag}_row_dmas")

    def all_steps(eng, step):
        def static(i):
            step(i, i % 8, lambda d: 0 <= i + d < E)
        for i in range(-4, 4):
            static(i)
        with eng.Fori(4, E - 11, 8) as i:
            for k in range(8):
                step(i + k, (4 + k) % 8, lambda d: True)
        for i in range(E - 4, E + 1):
            static(i)

    def expert1(e):
        return slice(e, e + 1) if isinstance(e, int) else bass.ds(e, 1)

    late = lambda i, n: not isinstance(i, int) or i >= n

    with nc.Block(no_gpsimd_drain=True) as block:
        @block.tensor
        def _(pe):
            def step(i, r, has):
                if has(-1):
                    b = (r - 1) % 2
                    pe.wait_ge(hid_ready, i)
                    if late(i, 2):
                        pe.wait_ge(ht_copied, i - 1)
                    for j in range(FH):
                        mm = pe.transpose(b_ht[:, P * j:P * j + P], hid[:, b, j::FH], K.ident[:, :])
                    mm.then_inc(ht_mm, 1)
                if has(0):
                    b = r % 2
                    pe.wait_ge(xt_copied, 2 * i + 2)
                    pe.wait_ge(gu_in[b], 16 * (i - b) + 32)
                    if late(i, 2):
                        pe.wait_ge(hid_ready, i - 1)
                    for c in range(KC):
                        mm = pe.matmul(b_au[b][:, :], xt[:, b, P * c:P * c + P], gu[b][:, :, c, :], start=c == 0,
                                       stop=c == KC - 1)
                    mm.then_inc(au_mm, 1)
                if has(1):
                    b = (r + 1) % 2
                    pe.wait_ge(gathered[b], 8 * (i + 1 - b) + 16)
                    if late(i, 0):
                        pe.wait_ge(xt_copied, 2 * i + 2)
                    for half in range(2):
                        for k in range(4):
                            mm = pe.transpose(b_xt[half][:, P * k:P * k + P], xg[:, b, 4 * half + k::KC], K.ident[:, :])
                        mm.then_inc(xt_mm, 1)
                if has(3):
                    b = (r + 3) % 2
                    pe.wait_ge(listed, i + 4)
                    if late(i, -2):
                        pe.wait_ge(idx_ready, 2 * i + 6)
                    for t in range(T):
                        mm = pe.matmul(b_list[:, 0:5], onehot[:, b, t, :], m.parts[:, t, expert1(i + 3), 0:5],
                                       start=t == 0, stop=t == T - 1)
                    mm.then_inc(list_mm, 1)
                if has(-1):
                    b, q = (r - 1) % 2, (r - 1) % 4
                    pe.wait_ge(ht_copied, i)
                    pe.wait_ge(d_in[q], 4 * (i - 1 - q) + 16)
                    if late(i, 2):
                        pe.wait_ge(y_dve, i - 1)
                        pe.wait_ge(y_act, i - 1)
                    for half in range(2):
                        for j in range(FH):
                            mm = pe.matmul(b_y[half][:, :], hidt[:, b, P * j:P * j + P],
                                           dn[q][:, j, 512 * half:512 * half + 512], start=j == 0, stop=j == FH - 1)
                    mm.then_inc(y_mm, 1)
            all_steps(pe, step)

        @block.vector
        def _(dve):
            def step(i, r, has):
                if has(0):
                    b = r % 2
                    dve.wait_ge(silu_ready, i + 1)
                    if late(i, 2):
                        dve.wait_ge(ht_mm, i - 1)
                    dve.wait_ge(idx_ready, 2 * i + 2)
                    dve.scalar_tensor_tensor(out=hid[:, b, :], in0=silu[:, b, :], scalar=gate[:, r:r + 1],
                                             in1=b_au[b][:, FE:2 * FE], op0=ALU.mult, op1=ALU.mult).then_inc(hid_ready, 1)
                if has(3):
                    if late(i, 4):
                        dve.wait_ge(scattered, 16 * (i - 3))
                    q = (r + 3) % 8
                    dve.wait_ge(list_mm, i + 4)
                    dve.tensor_scalar(idx[:, q:q + 1], b_list[:, 0:1], b_list[:, 1:2], float(NO_TOKEN), ALU.add,
                                      ALU.add).then_inc(idx_ready, 1)
                    dve.tensor_reduce(gate[:, q:q + 1], b_list[:, 2:5], AX.X, ALU.add).then_inc(idx_ready, 1)
                if has(4):
                    b = r % 2
                    if late(i, -2):
                        dve.wait_ge(list_mm, i + 3)
                    dve.tensor_tensor(onehot[:, b, :, :], K.iota[:, :].unsqueeze(1).broadcast_to([P, T, P]),
                                      m.rank[:, :, expert1(i + 4)].broadcast_to([P, T, P]),
                                      ALU.is_equal).then_inc(listed, 1)
                if has(-1):
                    b = (r - 1) % 2
                    dve.wait_ge(y_mm, i)
                    if late(i, 3):
                        dve.wait_ge(scattered, 16 * (i - 2))
                    dve.tensor_copy(ys[:, b, 0:512], b_y[0][:, :]).then_inc(y_dve, 1)
            all_steps(dve, step)

        @block.scalar
        def _(act):
            def step(i, r, has):
                if has(-1):
                    b = (r - 1) % 2
                    act.wait_ge(ht_mm, i)
                    if late(i, 3):
                        act.wait_ge(y_mm, i - 2)
                    act.activation(hidt[:, b, :], b_ht[:, 0:FE], ACT.Copy).then_inc(ht_copied, 1)
                if has(0):
                    b = r % 2
                    act.wait_ge(au_mm, i + 1)
                    if late(i, 2):
                        act.wait_ge(hid_ready, i - 1)
                    act.activation(silu[:, b, :], b_au[b][:, 0:FE], ACT.Silu).then_inc(silu_ready, 1)
                if has(1):
                    b = (r + 1) % 2
                    if late(i, 1):
                        act.wait_ge(au_mm, i)
                    for half in range(2):
                        act.wait_ge(xt_mm, 2 * i + 3 + half)
                        act.activation(xt[:, b, 512 * half:512 * half + 512], b_xt[half][:, :],
                                       ACT.Copy).then_inc(xt_copied, 1)
                if has(-1):
                    b = (r - 1) % 2
                    act.wait_ge(y_mm, i)
                    if late(i, 3):
                        act.wait_ge(scattered, 16 * (i - 2))
                    act.activation(ys[:, b, 512:1024], b_y[1][:, :], ACT.Copy).then_inc(y_act, 1)
            all_steps(act, step)

        @block.gpsimd
        def _(pool):
            pool.memset(f[:, 0:2048], 0.0).then_inc(cleared, 1)
            pool.wait_ge(cleared, 1)
            for ready, n in init:
                pool.wait_ge(ready, n)

            def step(i, r, has):
                if has(3):
                    b, q = (r + 3) % 2, (r + 3) % 8
                    pool.wait_ge(idx_ready, 2 * i + 8)
                    if late(i, -1):
                        pool.wait_ge(xt_mm, 2 * i + 4)
                    pool.sem_inc(row_dmas, 1)
                    pool.indirect_dma_start(out=xg[:, b, :], out_offset=None, in_=K.h_dram,
                                            in_offset=bass.IndirectOffsetOnAxis(idx[:, q:q + 1], 0),
                                            bounds_check=S - 1, oob_is_err=False).then_inc(gathered[b], 16)
                if has(-1):
                    b, q = (r - 1) % 2, (r - 1) % 8
                    pool.wait_ge(y_dve, i)
                    pool.wait_ge(y_act, i)
                    if late(i, 2):
                        pool.wait_ge(scattered, 16 * (i - 1))
                    pool.sem_inc(row_dmas, 1)
                    scatter_add(K, pool, ys[:, b, :], idx[:, q:q + 1]).then_inc(scattered, 16)
            all_steps(pool, step)
            pool.wait_ge(scattered, 16 * E)

        @block.sync
        def _(sp):
            def load(e, b):
                at = expert1(e)
                for g, w in enumerate((w_gate, w_up)):
                    sp.dma_start(gu[b][:, g, :, :], w[at].rearrange("e (p c) f -> (e p) c f", p=P)).then_inc(gu_in[b], 16)

            def load_down(e, q):
                sp.dma_start(dn[q], w_down[expert1(e)].rearrange("e (p j) d -> (e p) j d", p=P)).then_inc(d_in[q], 16)

            for e in range(4):
                if e >= 2:
                    sp.wait_ge(au_mm, e - 1)
                load(e, e % 2), load_down(e, e)
            with sp.Fori(4, E - 3, 4) as e:
                for q in range(4):
                    sp.wait_ge(au_mm, e + q - 1)
                    load(e + q, q % 2)
                    sp.wait_ge(y_mm, e + q - 3)
                    load_down(e + q, q)


def overflow_stage(K, tag, m, w_gate, w_up, w_down):
    nc, E = K.nc, m.E
    s = lambda n: K.sem(f"{tag}_over_{n}")
    w_gate, w_up, w_down = w_gate[0], w_up[0], w_down[0]
    f = K.heads
    xg, xt, ys = f[:, 0:1024], f[:, 2048:3072], f[:, 4096:5120]
    silu, hid, hidt = f[:, 6144:6400], f[:, 6656:6912], f[:, 7168:7424]
    onehot = f[:, 7680:8192].rearrange("p (t s) -> p t s", t=T)
    idx, gate = K.small[:, 1024:1025].bitcast(I32), K.small[:, 1028:1029]
    gu = K.big[:, 0:4096].rearrange("p (g c f) -> p g c f", g=2, c=KC)
    dn = K.big[:, 8192:10240].rearrange("p (j d) -> p j d", j=FH)
    LISTS = range(1, T)
    NL = len(LISTS)
    listed, list_mm, idx_ready, xt_mm, xt_copied = s("onehot"), s("list_product"), s("list"), s("turned"), s("turned_copied")
    au_mm, silu_ready, hid_ready, ht_mm, ht_copied = s("gate_up"), s("silu"), s("hidden"), s("hid_turned"), s("hid_copied")
    y_mm, y_taken, gu_in, d_in = s("down"), s("y_taken"), s("gate_up_arrived"), s("down_arrived")
    gathered, scattered = K.over_sems[tag]
    row_dmas = s("row_dmas")
    experts_done = s("experts_done")
    one = lambda e: bass.ds(e, 1)

    def each(eng, body):
        most = eng.value_load(m.most[0:1, :], min_val=0, max_val=S)
        with eng.If(most > P):
            with eng.Fori(0, E, 1) as e:
                for k, b in enumerate(LISTS):
                    body(e, b, e * NL + k)

    with nc.Block() as block:
        @block.tensor
        def _(pe):
            def body(e, b, n):
                pe.wait_ge(listed, n + 1)
                for t in range(T):
                    mm = pe.matmul(K.bank[0][:, 0:2], onehot[:, t, :], m.table[:, t, one(e), :], start=t == 0,
                                   stop=t == T - 1)
                mm.then_inc(list_mm, 1)
                pe.wait_ge(gathered, 16 * n + 16)
                for half in range(2):
                    for k in range(4):
                        mm = pe.transpose(K.bank[1 + half][:, P * k:P * k + P], xg[:, 4 * half + k::KC], K.ident[:, :])
                    mm.then_inc(xt_mm, 1)
                pe.wait_ge(xt_copied, 2 * n + 2)
                pe.wait_ge(gu_in, 32 * e + 32)
                for c in range(KC):
                    mm = pe.matmul(K.bank[3][:, :], xt[:, P * c:P * c + P], gu[:, :, c, :], start=c == 0, stop=c == KC - 1)
                mm.then_inc(au_mm, 1)
                pe.wait_ge(hid_ready, n + 1)
                for j in range(FH):
                    mm = pe.transpose(K.bank[5][:, P * j:P * j + P], hid[:, j::FH], K.ident[:, :])
                mm.then_inc(ht_mm, 1)
                pe.wait_ge(ht_copied, n + 1)
                pe.wait_ge(d_in, 16 * e + 16)
                for half in range(2):
                    for j in range(FH):
                        mm = pe.matmul(K.bank[6 + half][:, :], hidt[:, P * j:P * j + P],
                                       dn[:, j, 512 * half:512 * half + 512], start=j == 0, stop=j == FH - 1)
                mm.then_inc(y_mm, 1)
            each(pe, body)

        @block.scalar
        def _(act):
            def body(e, b, n):
                for half in range(2):
                    act.wait_ge(xt_mm, 2 * n + 1 + half)
                    act.activation(xt[:, 512 * half:512 * half + 512], K.bank[1 + half][:, :], ACT.Copy)\
                       .then_inc(xt_copied, 1)
                act.wait_ge(au_mm, n + 1)
                act.activation(silu, K.bank[3][:, 0:FE], ACT.Silu).then_inc(silu_ready, 1)
                act.wait_ge(ht_mm, n + 1)
                act.activation(hidt, K.bank[5][:, 0:FE], ACT.Copy).then_inc(ht_copied, 1)
                act.wait_ge(y_mm, n + 1)
                for half in range(2):
                    act.activation(ys[:, 512 * half:512 * half + 512], K.bank[6 + half][:, :], ACT.Copy)\
                       .then_inc(y_taken, 1)
            each(act, body)

        @block.vector
        def _(dve):
            def body(e, b, n):
                dve.scalar_tensor_tensor(out=onehot, in0=K.iota[:, :].unsqueeze(1).broadcast_to([P, T, P]),
                                         scalar=float(P * b), in1=m.rank[:, :, one(e)].broadcast_to([P, T, P]),
                                         op0=ALU.add, op1=ALU.is_equal).then_inc(listed, 1)
                dve.wait_ge(list_mm, n + 1)
                dve.tensor_scalar(idx, K.bank[0][:, 0:1], float(NO_TOKEN), None, ALU.add).then_inc(idx_ready, 1)
                dve.tensor_copy(gate, K.bank[0][:, 1:2]).then_inc(idx_ready, 1)
                dve.wait_ge(idx_ready, 2 * n + 2)
                dve.wait_ge(silu_ready, n + 1)
                dve.scalar_tensor_tensor(out=hid, in0=silu, scalar=gate, in1=K.bank[3][:, FE:2 * FE], op0=ALU.mult,
                                         op1=ALU.mult).then_inc(hid_ready, 1)
                dve.wait_ge(hid_ready, n + 1)
                dve.wait_ge(scattered, 16 * n + 16)
            each(dve, body)

        @block.gpsimd
        def _(pool):
            def body(e, b, n):
                pool.wait_ge(idx_ready, 2 * n + 2)
                pool.sem_inc(row_dmas, 1)
                pool.indirect_dma_start(out=xg, out_offset=None, in_=K.h_dram,
                                        in_offset=bass.IndirectOffsetOnAxis(idx, 0), bounds_check=S - 1,
                                        oob_is_err=False).then_inc(gathered, 16)
                pool.wait_ge(y_taken, 2 * n + 2)
                pool.sem_inc(row_dmas, 1)
                scatter_add(K, pool, ys, idx).then_inc(scattered, 16)
                pool.wait_ge(scattered, 16 * n + 16)
            each(pool, body)

        @block.sync
        def _(sp):
            most = sp.value_load(m.most[0:1, :], min_val=0, max_val=S)
            with sp.If(most > P):
                with sp.Fori(0, E, 1) as e:
                    for g, w in enumerate((w_gate, w_up)):
                        sp.dma_start(gu[:, g, :, :], w[one(e)].rearrange("e (p c) f -> (e p) c f", p=P)).then_inc(gu_in, 16)
                    sp.dma_start(dn, w_down[one(e)].rearrange("e (p j) d -> (e p) j d", p=P)).then_inc(d_in, 16)
                    sp.wait_ge(y_mm, NL * e + NL)
                    sp.sem_inc(experts_done, 1)


def scatter_add(K, pool, rows, at):
    return pool.indirect_dma_start(out=K.acc_dram, out_offset=bass.IndirectOffsetOnAxis(at, 0), in_=rows, in_offset=None,
                                   bounds_check=S - 1, oob_is_err=False, compute_op=ALU.add)


def first_experts(K):
    m = moe_buffers(K, 32)
    K.m1 = m
    rank_tokens(K, "rank1", m, 36, hier_router(K, m))
    I = K.I
    acc_set = K.sem("acc1_set")
    with K.nc.Block(no_gpsimd_drain=True) as block:
        @block.sync
        def _(sp):
            sp.dma_start(K.acc_dram.rearrange("(t p) d -> p t d", p=P), K.x).then_inc(acc_set, 16)
            sp.wait_ge(acc_set, 16)
    experts_stage(K, "moe1", m, I["w_exp_gate"], I["w_exp_up"], I["w_exp_down"], [(acc_set, 16)])
    overflow_stage(K, "moe1", m, I["w_exp_gate"], I["w_exp_up"], I["w_exp_down"])



def latents(K):
    nc, I = K.nc, K.I
    s = K.sem
    vec_in, taken, squares, sums, std, normed = (s(f"lat_{n}") for n in
                                                 ("vectors_arrived", "taken", "squares", "sums", "std", "normed"))
    gate_in, gate_mid, logf_ready, sin_in, sin_out, turned = (s(f"lat_{n}") for n in (
        "abs_ready", "log_ready", "logf_ready", "angles_ready", "sines_ready", "turned_copied"))
    small = K.small
    K.lat = K.scr[:, 0:1696].rearrange("p (t n) -> p t n", t=T)
    sq = K.scr[:, 1696:3232].rearrange("p (t n) -> p t n", t=T)
    K.qlT = K.heads[:, 0:1024].rearrange("p (c s) -> p c s", c=2)
    K.kvT = K.heads[:, 1024:1536]
    gq, gkv = small[:, 0:256], small[:, 256:384]
    b_forget = small[:, 384:392]
    ss, sd, rs = (small[:, a:a + 8].rearrange("p (n t) -> p n t", n=2) for a in (392, 400, 408))
    fl, ftmp = (small[:, a:a + 32].rearrange("p (t h) -> p t h", t=T) for a in (416, 448))
    K.forget = small[:, 480:512].rearrange("p (t h) -> p t h", t=T)
    pos_i, pos = small[:, 512:516].bitcast(I32), small[:, 516:520]
    freq = small[:, 520:536]
    ang, turns, r = (small[:, a:a + 64] for a in (704, 768, 832))
    by_t = lambda a: a.rearrange("p (t j) -> p t j", t=T)
    K.sin, K.cos = by_t(small[:, 896:960]), by_t(small[:, 960:1024])
    K.k_pe = small[:, 1024:1152].rearrange("p (t n) -> p t n", t=T)
    rot = [by_t(small[:, 1152 + 64 * n:1216 + 64 * n]) for n in range(2)]
    at = []
    with nc.Block(no_gpsimd_drain=True) as block:
        @block.tensor
        def _(pe):
            w = chunked(take_job(K, pe), KC, 424)
            for t in range(T):
                for c in range(KC):
                    mm = pe.matmul(K.bank[t][:, 0:424], K.ht[:, c, P * t:P * t + P], w[:, c, :], start=c == 0,
                                   stop=c == KC - 1)
                at.append(product(K, mm))
            end_job(K)
            pe.wait_ge(logf_ready, 1)
            for t in range(T):
                for before in range(t + 1):
                    mm = pe.matmul(K.bank[4][:, 8 * t:8 * t + 8], (K.tri_incl if before == t else K.ones)[:, :],
                                   fl[:, before, :], start=before == 0, stop=before == t)
            at.append(product(K, mm))
            pe.wait_ge(normed, 1)
            for n in range(3):
                for t in range(T):
                    src = K.lat[:, t, n:256:2] if n < 2 else K.lat[:, t, 256:384]
                    mm = pe.transpose(K.bank[5 + n][:, P * t:P * t + P], src, K.ident[:, :])
                at.append(product(K, mm))

        @block.scalar
        def _(act):
            step = K.act.on(act)
            for t in range(T):
                act.wait_ge(K.products, at[t])
                act.activation(K.lat[:, t, :], K.bank[t][:, 0:424], ACT.Copy).then_inc(taken, 1)
            act.wait_ge(taken, T)
            act.activation(sq, K.lat[:, :, 0:384], ACT.Square).then_inc(squares, 1)
            act.wait_ge(gate_in, 1)
            step(act.activation(ftmp, fl, ACT.Abs))
            step(act.activation(ftmp, ftmp, ACT.Exp, scale=-1.0))
            act.activation(ftmp, ftmp, ACT.Ln, bias=K.ones[:, 0:1]).then_inc(gate_mid, 1)
            act.wait_ge(sums, 2)
            act.activation(sd[:, 0, :], ss[:, 0, :], ACT.Sqrt, scale=1.0 / 256, bias=K.eps[:, 0:1]).then_inc(std, 1)
            act.activation(sd[:, 1, :], ss[:, 1, :], ACT.Sqrt, scale=1.0 / 128, bias=K.eps[:, 0:1]).then_inc(std, 1)
            act.wait_ge(sin_in, 1)
            act.activation(K.sin, by_t(r), ACT.Sin).then_inc(sin_out, 1)
            step(act.activation(turns, r, ACT.Abs))
            act.activation(K.cos, by_t(turns), ACT.Sin, scale=-1.0, bias=K.half_pi[:, 0:1]).then_inc(sin_out, 1)
            for n in range(3):
                act.wait_ge(K.products, at[5 + n])
                act.activation(K.qlT[:, n, :] if n < 2 else K.kvT, K.bank[5 + n][:, :], ACT.Copy).then_inc(turned, 1)
            act.wait_ge(turned, 3)

        @block.vector
        def _(dve):
            step = K.dve.on(dve)
            step(dve.memset(K.half_pi[:, :], TWO_PI / 4))
            dve.wait_ge(vec_in, 16 * 5)
            step(dve.tensor_copy(pos, pos_i))
            step(dve.tensor_tensor(by_t(ang), pos.unsqueeze(2).broadcast_to([P, T, 16]),
                                   freq.unsqueeze(1).broadcast_to([P, T, 16]), ALU.mult))
            step(dve.tensor_scalar(turns, ang, 1.0 / TWO_PI, None, ALU.mult))
            step(dve.tensor_scalar(turns, turns, ROUNDER, None, ALU.add))
            step(dve.tensor_scalar(turns, turns, -ROUNDER, None, ALU.add))
            step(dve.scalar_tensor_tensor(out=r, in0=turns, scalar=-PI_PARTS[0], in1=ang, op0=ALU.mult, op1=ALU.add))
            step(dve.scalar_tensor_tensor(out=r, in0=turns, scalar=-PI_PARTS[1], in1=r, op0=ALU.mult, op1=ALU.add))
            step(dve.scalar_tensor_tensor(out=r, in0=turns, scalar=-PI_PARTS[2], in1=r, op0=ALU.mult, op1=ALU.add))
            dve.tensor_scalar(r, r, -3.1415925, 3.1415925, ALU.max, ALU.min).then_inc(sin_in, 1)
            dve.wait_ge(taken, T)
            dve.tensor_tensor(fl, K.lat[:, :, 416:424], b_forget.unsqueeze(1).broadcast_to([P, T, 8]),
                              ALU.add).then_inc(gate_in, 1)
            dve.wait_ge(squares, 1)
            dve.tensor_reduce(ss[:, 0, :], sq[:, :, 0:256], AX.X, ALU.add).then_inc(sums, 1)
            dve.tensor_reduce(ss[:, 1, :], sq[:, :, 256:384], AX.X, ALU.add).then_inc(sums, 1)
            dve.wait_ge(gate_mid, 1)
            dve.scalar_tensor_tensor(out=fl, in0=fl, scalar=0.0, in1=ftmp, op0=ALU.min,
                                     op1=ALU.subtract).then_inc(logf_ready, 1)
            dve.wait_ge(std, 2)
            step(dve.reciprocal(small[:, 408:416], small[:, 400:408]))
            for t in range(T):
                step(dve.scalar_tensor_tensor(out=K.lat[:, t, 0:256], in0=K.lat[:, t, 0:256], scalar=rs[:, 0, t:t + 1],
                                              in1=gq, op0=ALU.mult, op1=ALU.mult))
                ins = dve.scalar_tensor_tensor(out=K.lat[:, t, 256:384], in0=K.lat[:, t, 256:384],
                                               scalar=rs[:, 1, t:t + 1], in1=gkv, op0=ALU.mult, op1=ALU.mult)
                if t < T - 1:
                    step(ins)
            ins.then_inc(normed, 1)
            dve.wait_ge(K.products, at[4])
            step(dve.tensor_copy(K.forget, K.bank[4][:, 0:32].rearrange("p (t h) -> p t h", t=T)))
            dve.wait_ge(sin_out, 2)
            rotate(step, dve, K.lat[:, :, 384:400], K.lat[:, :, 400:416], K.cos, K.sin,
                   K.k_pe[:, :, 0:16], K.k_pe[:, :, 16:32], rot)

        @block.sync
        def _(sp):
            load_jobs(K, sp, 1)
            sp.dma_start(gq, bcast(I["g_q_lat_2"][0], P)).then_inc(vec_in, 16)
            sp.dma_start(gkv, bcast(I["g_kv_lat_2"][0], P)).then_inc(vec_in, 16)
            sp.dma_start(b_forget, bcast(I["b_forget_2"][0], P)).then_inc(vec_in, 16)
            sp.dma_start(freq, bcast(I["inv_freq"], P)).then_inc(vec_in, 16)
            sp.dma_start(pos_i, I["positions_2"][0].rearrange("(t p) -> p t", p=P),
                         allow_slow_non_contiguous=True).then_inc(vec_in, 16)
            load_jobs(K, sp, 1)


PI_PARTS = (6.28125, 0.0019352436065673828, 6.357301884918343e-08)


def rotate(step, dve, x1, x2, cos, sin, out1, out2, tmp):
    step(dve.tensor_tensor(tmp[0], x2, sin, ALU.mult))
    step(dve.tensor_tensor(tmp[1], x1, sin, ALU.mult))
    step(dve.tensor_tensor(out1, x1, cos, ALU.mult))
    step(dve.tensor_tensor(out1, out1, tmp[0], ALU.subtract))
    step(dve.tensor_tensor(out2, x2, cos, ALU.mult))
    step(dve.tensor_tensor(out2, out2, tmp[1], ALU.add))


def latent_heads(K):
    nc = K.nc
    taken, rotated = K.sem("up_taken"), K.sem("up_rotated")
    DIM = 96
    q_rows = K.scr[:, 1696:4768].rearrange("p (t h d) -> p t h d", t=T, h=HEADS)
    k_rows = K.scr[:, 4768:7840].rearrange("p (t h d) -> p t h d", t=T, h=HEADS)
    K.head_rows = (q_rows, k_rows)
    tmp = [K.scr[:, 7840 + 512 * n:8352 + 512 * n].rearrange("p (t h d) -> p t h d", t=T, h=HEADS) for n in range(4)]
    at = []
    with nc.Block(no_gpsimd_drain=True) as block:
        @block.tensor
        def _(pe):
            w = chunked(take_job(K, pe), 2, 768)
            for u in range(8):
                t, half = divmod(u, 2)
                for c in range(2):
                    mm = pe.matmul(K.bank[u][:, 0:384], K.qlT[:, c, P * t:P * t + P], w[:, c, 384 * half:384 * half + 384],
                                   start=c == 0, stop=c == 1)
                at.append(product(K, mm))
            end_job(K)
            w = take_job(K, pe)
            for u in range(8):
                t, half = divmod(u, 2)
                pe.wait_ge(taken, u + 1)
                mm = pe.matmul(K.bank[u][:, :], K.kvT[:, P * t:P * t + P], w[:, 512 * half:512 * half + 512], start=True,
                               stop=True)
                at.append(product(K, mm))
            end_job(K)

        @block.scalar
        def _(act):
            for u in range(8):
                t, half = divmod(u, 2)
                act.wait_ge(K.products, at[u])
                act.activation(q_rows[:, t, 4 * half:4 * half + 4, :],
                               K.bank[u][:, 0:384].rearrange("p (h d) -> p h d", h=4), ACT.Copy,
                               scale=DIM ** -0.5).then_inc(taken, 1)
            for u in range(8):
                t, half = divmod(u, 2)
                act.wait_ge(K.products, at[8 + u])
                kv = K.bank[u][:, :].rearrange("p (h d) -> p h d", h=4)
                act.activation(k_rows[:, t, 4 * half:4 * half + 4, 0:64], kv[:, :, 0:64], ACT.Copy).then_inc(taken, 1)
                act.activation(K.v[:, t, 256 * half:256 * half + 256].rearrange("p (h d) -> p h d", h=4),
                               kv[:, :, 64:128], ACT.Copy).then_inc(taken, 1)
            act.wait_ge(taken, 24)

        @block.vector
        def _(dve):
            step = K.dve.on(dve)
            step(dve.tensor_copy(k_rows[:, :, :, 64:96], K.k_pe.unsqueeze(2).broadcast_to([P, T, HEADS, 32])))
            dve.wait_ge(taken, 8)
            cos, sin = (a.unsqueeze(2).broadcast_to([P, T, HEADS, 16]) for a in (K.cos, K.sin))
            rotate(step, dve, q_rows[:, :, :, 64:80], q_rows[:, :, :, 80:96], cos, sin, tmp[2], tmp[3], tmp)
            step(dve.tensor_copy(q_rows[:, :, :, 64:80], tmp[2]))
            step(dve.tensor_copy(q_rows[:, :, :, 80:96], tmp[3]))

        @block.sync
        def _(sp):
            load_jobs(K, sp, 2)


def heads_to_columns(K, tag, dim):
    nc = K.nc
    taken = (K.sem(f"{tag}_act_copied"), K.sem(f"{tag}_dve_copied"))
    at = []
    with nc.Block(no_gpsimd_drain=True) as block:
        @block.tensor
        def _(pe):
            for u in range(2 * HEADS):
                n, h = divmod(u, HEADS)
                if u >= 8:
                    pe.wait_ge(taken[u % 2], (u - 8) // 2 + 1)
                for t in range(T):
                    mm = pe.transpose(K.bank[u % 8][0:dim, P * t:P * t + P], K.head_rows[n][:, t, h, :], K.ident[:, :])
                at.append(product(K, mm))

        def copy_heads(eng, copy, which):
            for u in range(which, 2 * HEADS, 2):
                n, h = divmod(u, HEADS)
                eng.wait_ge(K.products, at[u])
                copy((K.qt, K.kt)[n][0:dim, h, :], K.bank[u % 8][0:dim, :]).then_inc(taken[which], 1)
            eng.wait_ge(taken[which], HEADS)

        @block.scalar
        def _(act):
            copy_heads(act, lambda o, i: act.activation(o, i, ACT.Copy), 0)

        @block.vector
        def _(dve):
            copy_heads(dve, dve.tensor_copy, 1)


def latent_attention(K):
    latent_heads(K)
    heads_to_columns(K, "mla_turn", 96)
    attention(K, "mla", 96, 0)


def fox_heads(K):
    nc = K.nc
    taken = K.sem("fox_taken")
    q_rows, k_rows = (K.scr[:, a:a + 2112].rearrange("p (t h d) -> p t h d", t=T, h=HEADS) for a in (0, 2112))
    K.head_rows = (q_rows, k_rows)
    at = []
    columns = lambda a: a.rearrange("p (c s) -> p c s", c=KC)
    h_high, h_low = columns(K.heads_parts[:, 0:4096]), columns(K.heads_parts[:, 4096:8192])
    h_split = (K.sem("fox_h_high"), K.sem("fox_h_low"))
    weights = SplitWeights(K, "fox", [K.big_parts[:, 12800 + 512 * k:13312 + 512 * k] for k in range(8)], [KC] * 3)
    for n in range(3):
        weights.block(n, K.next_job + n, KC, 512)
    with nc.Block(no_gpsimd_drain=True) as block:
        @block.tensor
        def _(pe):
            for n in range(3):

                def before(t):
                    if n == 2:
                        pe.wait_ge(taken, t + 1)

                at.extend(weights.products(pe, n, h_high, h_low, K.bank[4 * (n % 2):4 * (n % 2) + 4], before,
                                           lhs_ready=None if n else h_split[1]))
                end_job(K)
            K.next_job += 3

        @block.scalar
        def _(act):
            weights.high(act, 0, lambda c: split_columns(act, None, h_split, [c], K.ht, h_high, h_low))
            for u in range(3 * T):
                n, t = divmod(u, T)
                if t == 0 and n < 2:
                    weights.high(act, n + 1)
                act.wait_ge(K.products, at[u])
                dest = K.v[:, t, :].rearrange("p (h d) -> p h d", h=HEADS) if n == 2 else K.head_rows[n][:, t, :, 0:64]
                act.activation(dest, K.bank[u % 8][:, :].rearrange("p (h d) -> p h d", h=HEADS), ACT.Copy,
                               scale=64 ** -0.5 if n == 0 else 1.0).then_inc(taken, 1)
            act.wait_ge(taken, 3 * T)

        @block.vector
        def _(dve):
            step = K.dve.on(dve)
            step(dve.tensor_copy(q_rows[:, :, :, 64], K.forget))
            step(dve.memset(q_rows[:, :, :, 65:66], 1.0))
            step(dve.memset(k_rows[:, :, :, 64:65], 1.0))
            step(dve.tensor_scalar(k_rows[:, :, :, 65], K.forget, -1.0, None, ALU.mult))
            weights.low(dve, 0, lambda c: split_columns(None, dve, h_split, [c], K.ht, h_high, h_low))
            weights.low(dve, 1)
            weights.low(dve, 2)

        @block.sync
        def _(sp):
            load_jobs(K, sp, 3)


def fox_attention(K):
    fox_heads(K)
    heads_to_columns(K, "fox_turn", 66)
    attention(K, "fox", 66, 512)


def merge(K):
    nc = K.nc
    s = K.sem
    chunks8 = lambda a: a.rearrange("p (c s) -> p c s", c=KC)
    h_high, h_low = chunks8(K.heads_parts[:, 4096:8192]), chunks8(K.ht_parts[:, :])
    o_high, o_low = chunks8(K.big_parts[:, 8192 + 4096:8192 + 8192]), chunks8(K.heads_parts[:, 0:4096])
    h_split, o_split = [(s(f"mrg_{x}_high"), s(f"mrg_{x}_low")) for x in ("h", "o")]
    at = []
    with nc.Block(no_gpsimd_drain=True) as block:
        @block.tensor
        def _(pe):
            for u in range(8):
                n, c = divmod(u, 4)
                for t in range(T):
                    mm = pe.transpose(K.bank[u][:, P * t:P * t + P], K.hr[:, t, 512 * n + c:512 * n + 512:4], K.ident[:, :])
                at.append(product(K, mm))

        @block.scalar
        def _(act):
            for u in range(8):
                act.wait_ge(K.products, at[u])
                act.activation(o_high[:, u, :], K.bank[u][:, :], ACT.Copy).then_inc(o_split[0], 1)
            split_columns(act, None, h_split, range(KC), K.ht, h_high, h_low)

        @block.vector
        def _(dve):
            for u in range(8):
                dve.wait_ge(o_split[0], u + 1)
                dve.tensor_tensor(o_low[:, u, :], K.bank[u][:, :], o_high[:, u, :].bitcast(F32),
                                  ALU.subtract).then_inc(o_split[1], 1)
            split_columns(None, dve, h_split, range(KC), K.ht, h_high, h_low)
            dve.wait_ge(o_split[1], KC)
            dve.wait_ge(h_split[1], KC)

        @block.sync
        def _(sp):
            load_jobs(K, sp, 1)

    sig, merged = s("mrg_sigmoids"), s("mrg_merged")
    gates = K.scr[:, 0:4096].rearrange("p (n t d) -> p n t d", n=2, t=T)
    base = K.n_products
    units = [(half, n, what, t) for half in range(2) for what in range(2) for n in range(2) for t in range(T)]
    groups = [(half, n, what) for half in range(2) for what in range(2) for n in range(2)]
    ring = [part[:, 8192 + 512 * k:8704 + 512 * k] for part in (K.heads_parts, K.big_parts[:, 8192:]) for k in range(4)]
    weights = SplitWeights(K, "mrg", ring, [4 if what else KC for _, _, what in groups])
    first_job = K.next_job
    for g, (half, n, what) in enumerate(groups):
        job = first_job + 3 * half + (2 if what else n)
        if what:
            weights.block(g, job, 4, 1024, 512 * n)
        else:
            weights.block(g, job, KC, 512)
    with nc.Block(no_gpsimd_drain=True) as block:
        @block.tensor
        def _(pe):
            for g, (half, n, what) in enumerate(groups):
                def before(t):
                    if g >= 2:
                        last_half, last_n, last_what = groups[g - 2]
                        pe.wait_ge(merged if last_what else sig, 8 * last_half + 4 * last_n + t + 1)

                high, low = (h_high, h_low) if what == 0 else (o_high[:, 4 * n:4 * n + 4], o_low[:, 4 * n:4 * n + 4])
                weights.products(pe, g, high, low, K.bank[4 * (g % 2):4 * (g % 2) + 4], before)
                if (n, what) != (0, 1):
                    end_job(K)
            K.next_job += 6

        @block.scalar
        def _(act):
            weights.high(act, 0)
            for u, (half, n, what, t) in enumerate(units):
                if t == 0 and u // T + 1 < len(groups):
                    weights.high(act, u // T + 1)
                if what == 0:
                    act.wait_ge(K.products, base + u + 1)
                    if half == 1:
                        act.wait_ge(merged, 4 * n + t + 1)
                    act.activation(gates[:, n, t, :], K.bank[u % 8][:, :], ACT.Sigmoid).then_inc(sig, 1)

        @block.vector
        def _(dve):
            step = K.dve.on(dve)
            weights.low(dve, 0)
            for u, (half, n, what, t) in enumerate(units):
                if t == 0 and u // T + 1 < len(groups):
                    weights.low(dve, u // T + 1)
                if what == 1:
                    dve.wait_ge(K.products, base + u + 1)
                    dve.wait_ge(sig, 8 * half + 4 * n + t + 1)
                    out = K.hr[:, t, 512 * half:512 * half + 512]
                    if n == 0:
                        dve.tensor_tensor(out, K.bank[u % 8][:, :], gates[:, n, t, :], ALU.mult).then_inc(merged, 1)
                    else:
                        step(dve.tensor_tensor(gates[:, n, t, :], K.bank[u % 8][:, :], gates[:, n, t, :], ALU.mult))
                        dve.wait_ge(merged, 8 * half + t + 1)
                        dve.tensor_tensor(out, out, gates[:, n, t, :], ALU.add).then_inc(merged, 1)
            dve.wait_ge(merged, 16)

        @block.sync
        def _(sp):
            load_jobs(K, sp, 6)
    turn_rows(K, "turn2")
    K.gate_in = K.sem("gate_m_arrived")
    K.norm4_in = K.sem("norm4_vectors_arrived")
    K.norm4_scale, K.norm4_gain = K.scr[:, 2048:2048 + D], K.scr[:, 3072:3072 + D]
    add_rows_product(K, "out2", 2, gate=K.gain, gate_ready=(K.gate_in, 16),
                     vectors=[(K.gain[:, :], bcast(K.mod_dram[2 * D:3 * D], P), K.gate_in),
                              (K.shift[:, :], bcast(K.mod_dram[3 * D:4 * D], P), K.norm4_in),
                              (K.norm4_scale, bcast(K.mod_dram[4 * D:5 * D], P), K.norm4_in),
                              (K.norm4_gain, bcast(K.I["g_ffn_norm_2"][0], P), K.norm4_in)])


def grouped_router(K, m):
    I, s = K.I, K.sem
    bias_in, scored = s("router2_bias_arrived"), s("router2_scores")
    G, EG = 8, 8
    W = T * G * EG
    by_group = lambda a: a.rearrange("p t (g e) -> p (t g) e", g=G)
    flat = K.keep.rearrange("p t s -> p (t s)")
    score = flat[:, 768:1024].rearrange("p (t e) -> p t e", t=T)
    choice, w1 = m.work, m.work2
    m1, m2, keep_g = (m.tiny[:, a:a + 32] for a in (0, 32, 64))
    den = m.tiny[:, 96:100]

    final_in = s("final_vectors_arrived")

    def sync(sp):
        sp.dma_start(m.bias, bcast(I["b_router_2"][0], P)).then_inc(bias_in, 16)
        sp.dma_start(K.gain[:, :], bcast(K.mod_dram[5 * D:6 * D], P)).then_inc(final_in, 16)
        sp.dma_start(K.shift[:, :], bcast(I["g_final_2"], P)).then_inc(final_in, 16)
        sp.wait_ge(final_in, 32)

    def scalar(act):
        act.wait_ge(K.products, K.router_at)
        act.activation(score, K.bank[0][:, 0:256].rearrange("p (t e) -> p t e", t=T), ACT.Sigmoid).then_inc(scored, 1)

    def vector(dve, step, raw):
        dve.wait_ge(bias_in, 16)
        dve.wait_ge(scored, 1)
        over_e = lambda a: a.unsqueeze(2).broadcast_to([P, T * G, EG])
        step(dve.tensor_tensor(choice, score, m.bias.unsqueeze(1).broadcast_to([P, T, 64]), ALU.add))
        step(dve.tensor_reduce(m1, by_group(choice), AX.X, ALU.max))
        step(dve.tensor_tensor(by_group(w1), by_group(choice), over_e(m1), ALU.is_equal))
        step(dve.tensor_tensor(by_group(w1), by_group(w1), K.desc[:, :].unsqueeze(1).broadcast_to([P, T * G, EG]), ALU.mult))
        step(dve.tensor_reduce(m2, by_group(w1), AX.X, ALU.max))
        step(dve.tensor_tensor(by_group(w1), by_group(w1), over_e(m2), ALU.is_equal))
        step(dve.scalar_tensor_tensor(out=w1, in0=w1, scalar=MASKED, in1=choice, op0=ALU.mult, op1=ALU.add))
        step(dve.tensor_reduce(m2, by_group(w1), AX.X, ALU.max))
        step(dve.tensor_tensor(m1, m1, m2, ALU.add))
        step(dve.memset(m.padded[:, :, 0:4], SENTINEL))
        step(dve.tensor_copy(m.padded[:, :, 4:12], m1.rearrange("p (t g) -> p t g", t=T)))
        pick_top(step, dve, m, m.padded, G, 4)
        step(dve.tensor_scalar(keep_g.rearrange("p (t g) -> p t g", t=T), m.padded[:, :, 4:12], TAKEN, None, ALU.is_equal))
        step(dve.tensor_scalar(m2, keep_g, -MASKED, MASKED, ALU.mult, ALU.add))
        step(dve.tensor_tensor(by_group(choice), by_group(choice), over_e(keep_g), ALU.mult))
        step(dve.tensor_tensor(by_group(choice), by_group(choice), over_e(m2), ALU.add))
        step(dve.memset(m.padded[:, :, 0:2], SENTINEL))
        step(dve.tensor_copy(m.padded[:, :, 2:66], choice))
        pick_top(step, dve, m, m.padded, 64, 6)
        step(dve.tensor_scalar(m.chosen, m.padded[:, :, 2:66], TAKEN, None, ALU.is_equal))
        step(dve.tensor_tensor(m.gate, score, m.chosen, ALU.mult))
        step(dve.tensor_reduce(den, m.gate, AX.X, ALU.add))
        step(dve.reciprocal(den, den))
        step(dve.tensor_scalar(den, den, ROUTED_SCALE, None, ALU.mult))
        step(dve.tensor_tensor(m.gate, m.gate, den.unsqueeze(2).broadcast_to([P, T, 64]), ALU.mult))

    return sync, scalar, vector


def shared_expert(K):
    s = K.sem
    silu_ready, hid_ready, turned, y_taken, stored = (s(f"shared_{n}") for n in ("silu", "hidden", "turned", "y", "stored"))
    K.acc_stored = stored
    silu = K.heads[:, 0:1024].rearrange("p (t f) -> p t f", t=T)
    hid = K.heads[:, 1024:2048].rearrange("p (t f) -> p t f", t=T)
    hidt = K.heads[:, 2048:3072].rearrange("p (j s) -> p j s", j=FH)
    b_au, b_ht, b_y = K.bank[3:7], (K.bank[7], K.bank[0]), K.bank[3:7]
    at_au, at_ht, at_y = [], [], []

    def gate_up(pe):
        w = chunked(take_job(K, pe), KC, 512)
        for t in range(T):
            for c in range(KC):
                mm = pe.matmul(b_au[t][:, :], K.ht[:, c, P * t:P * t + P], w[:, c, :], start=c == 0, stop=c == KC - 1)
            at_au.append(product(K, mm))
        end_job(K)

    def down(pe):
        pe.wait_ge(hid_ready, T)
        for j in range(FH):
            for t in range(T):
                mm = pe.transpose(b_ht[j][:, P * t:P * t + P], hid[:, t, j::FH], K.ident[:, :])
            at_ht.append(product(K, mm))
        w = chunked(take_job(K, pe), FH, D)
        pe.wait_ge(turned, FH)
        for u in range(2 * T):
            t, half = divmod(u, 2)
            if u >= 4:
                pe.wait_ge(y_taken, u - 3)
            for j in range(FH):
                mm = pe.matmul(b_y[u % 4][:, :], hidt[:, j, P * t:P * t + P], w[:, j, 512 * half:512 * half + 512],
                               start=j == 0, stop=j == FH - 1)
            at_y.append(product(K, mm))
        end_job(K)

    def scalar(act):
        for t in range(T):
            act.wait_ge(K.products, at_au[t])
            act.activation(silu[:, t, :], b_au[t][:, 0:FE], ACT.Silu).then_inc(silu_ready, 1)
        for j in range(FH):
            act.wait_ge(K.products, at_ht[j])
            act.activation(hidt[:, j, :], b_ht[j][:, :], ACT.Copy).then_inc(turned, 1)
        for u in range(2 * T):
            t, half = divmod(u, 2)
            act.wait_ge(K.products, at_y[u])
            act.activation(K.hr[:, t, 512 * half:512 * half + 512], b_y[u % 4][:, :], ACT.Copy).then_inc(y_taken, 1)

    def vector(dve):
        for t in range(T):
            dve.wait_ge(silu_ready, t + 1)
            dve.tensor_tensor(hid[:, t, :], silu[:, t, :], b_au[t][:, FE:2 * FE], ALU.mult).then_inc(hid_ready, 1)

    def sync(sp):
        for t in range(T):
            sp.wait_ge(y_taken, 2 * t + 2)
            sp.dma_start(K.acc_dram[P * t:P * t + P, :], K.hr[:, t, :]).then_inc(stored, 16)
        sp.wait_ge(stored, 16 * T)

    parts = State()
    parts.gate_up, parts.down, parts.scalar, parts.vector, parts.sync = gate_up, down, scalar, vector, sync
    return parts


def second_norm(K):
    norm_columns(K, "norm3", modulation=(K.gain[:, :], K.hr[:, 0, :], None), x_from=K.acc_dram)


def second_experts(K):
    norm_columns(K, "norm4", modulation=(K.norm4_gain, K.norm4_scale, (K.norm4_in, 48)), store=True)
    m = moe_buffers(K, 64)
    K.router_at = K.n_products + 1
    rank_tokens(K, "rank2", m, 64, grouped_router(K, m), jobs_ahead=1, shared=shared_expert(K))
    I = K.I
    experts_stage(K, "moe2", m, I["w_exp_gate_2"], I["w_exp_up_2"], I["w_exp_down_2"], [(K.acc_stored, 16 * T)])
    overflow_stage(K, "moe2", m, I["w_exp_gate_2"], I["w_exp_up_2"], I["w_exp_down_2"])


def final(K):
    nc = K.nc
    s = K.sem
    added, squares, std, ready, stored = (s(f"final_{n}") for n in (
        "added", "squares", "std", "rows_ready", "stored"))
    rows_in = [s(f"final_rows{t}_arrived") for t in range(T)]
    ss, sd, rs = K.small[:, 0:4], K.small[:, 4:8], K.small[:, 8:12]
    with nc.Block(no_gpsimd_drain=True) as block:
        @block.scalar
        def _(act):
            for t in range(T):
                act.wait_ge(added, t + 1)
                act.activation(K.scr[:, 1024 * t:1024 * t + 1024], K.x[:, t, :], ACT.Square,
                               accum_out=ss[:, t:t + 1]).then_inc(squares, 1)
                act.wait_ge(squares, t + 1)
                act.activation(sd[:, t:t + 1], ss[:, t:t + 1], ACT.Sqrt, scale=1.0 / D, bias=K.eps[:, 0:1]).then_inc(std, 1)

        @block.vector
        def _(dve):
            step = K.dve.on(dve)
            for t in range(T):
                dve.wait_ge(rows_in[t], 16)
                step(dve.tensor_tensor(K.hr[:, t, :], K.hr[:, t, :], K.gain[:, :], ALU.mult))
                dve.tensor_tensor(K.x[:, t, :], K.x[:, t, :], K.hr[:, t, :], ALU.add).then_inc(added, 1)
            for t in range(T):
                dve.wait_ge(std, t + 1)
                step(dve.reciprocal(rs[:, t:t + 1], sd[:, t:t + 1]))
                dve.scalar_tensor_tensor(out=K.hr[:, t, :], in0=K.x[:, t, :], scalar=rs[:, t:t + 1], in1=K.shift[:, :],
                                         op0=ALU.mult, op1=ALU.mult).then_inc(ready, 1)

        @block.sync
        def _(sp):
            for t in range(T):
                sp.dma_start(K.hr[:, t, :], K.acc_dram[P * t:P * t + P, :]).then_inc(rows_in[t], 16)
            for t in range(T):
                sp.wait_ge(ready, t + 1)
                sp.dma_start(K.out[0, P * t:P * t + P, :], K.hr[:, t, :]).then_inc(stored, 16)
            sp.wait_ge(stored, 16 * T)


FIRST_BLOCK = [("setup", setup), ("norm1", first_norm), ("proj1", first_projection), ("gla", gla), ("qkn", qk_norm),
          ("attn1", first_attention), ("out1", first_output), ("moe1", first_experts)]
SECOND_BLOCK = [("norm3", second_norm), ("lat", latents), ("mla", latent_attention), ("fox", fox_attention), ("merge", merge),
          ("moe2", second_experts), ("final", final)]

_CONSTS = {"bucket_onehot": (N_BUCKETS, BIAS_COLS), "inv_freq": (16,)}
_INS = ["x", "norm1_g", "w_in", "q_norm_g", "k_norm_g", "rel_bias", "gla_gate_w2", "gla_gate_b", "gla_out_norm_g",
        "w_out", "norm2_g", "w_router_group", "b_router_group", "w_router_expert", "b_router_expert", "w_exp_gate",
        "w_exp_up", "w_exp_down", "c_2", "positions_2", "w_mod_2", "b_mod_2", "g_mix_norm_2", "w_in_2", "b_forget_2",
        "g_q_lat_2", "w_q_up_2", "g_kv_lat_2", "w_kv_up_2", "w_o_mla_2", "w_o_fox_2", "w_out_2", "g_ffn_norm_2",
        "w_router_2", "b_router_2", "w_exp_gate_2", "w_exp_up_2", "w_exp_down_2", "w_sh_gate_2", "w_sh_up_2",
        "w_sh_down_2", "g_final_2"]

_OUTS = [((1, S, D), "float32")]


def kernel(**inputs):
    import concourse.bacc as _bacc
    from concourse.bass_utils import run_bass_kernel_spmd as _run

    nc = _bacc.Bacc("TRN2", target_bir_lowering=False, num_devices=1)
    arrays, args = {}, []
    constants = shape_constants()
    for name in _INS + list(_CONSTS):
        a = np.ascontiguousarray(inputs[name] if name in inputs else constants[name])
        arrays[f"in_{name}_dram"] = a
        args.append(nc.dram_tensor(f"in_{name}_dram", a.shape, mybir.dt.from_np(a.dtype), kind="ExternalInput").ap())
    for i, (shape, dtype) in enumerate(_OUTS):
        args.append(nc.dram_tensor(f"out_{i}_dram", shape, mybir.dt.from_np(np.dtype(dtype)), kind="ExternalOutput").ap())
    build_program(nc, *args)
    r = _run(nc, [arrays], core_ids=[0])
    return r.results[0]["out_0_dram"]
```
